# Optimizing a Trainium2 kernel written in Bass

```python
import jax
import jax.numpy as jnp
from jax import lax
import numpy as np

D_MODEL = 1024
BATCH = 1
SEQ = 256
DEPTH = 2
DEC_BATCH = 8
DEC_SEQ = 1
PAST_LEN = 1024
PAGE_SIZE = 128

N_AB = (DEPTH + 1) // 2
N_C = DEPTH // 2
H_A = 8
DH_A = 64
MOBA_BLOCK = 256
MOBA_TOPK = 3
MOBA_Q_BLOCK = 16
H_B = 8
DK_B = 64
DV_B = 64
RET_CHUNK = 128
H_C = 8
DH_C = D_MODEL // H_C
MLSTM_CHUNK = 128
D_FF = 11 * D_MODEL // 4
CONV_W = 3
ROPE_THETA = 10000.0
EPS = 1e-6
W_A = H_A * DH_A
W_B = H_B * DV_B
W_C = H_C * DH_C
IN_AB = 3 * W_A + 2 * H_B * DK_B + 2 * W_B
IN_C = 4 * W_C + 2 * H_C
AB_SPLITS = (W_A, 2 * W_A, 3 * W_A, 3 * W_A + H_B * DK_B, 3 * W_A + 2 * H_B * DK_B, 3 * W_A + 2 * H_B * DK_B + W_B)
C_SPLITS = (W_C, 2 * W_C, 3 * W_C, 4 * W_C, 4 * W_C + H_C)
F32 = jnp.float32

kernel_name = "moba_retnet_mlstm_convffn_step"

def rmsnorm(x, g):
    xf = x.astype(F32)
    y = xf * lax.rsqrt(jnp.mean(xf * xf, axis=-1, keepdims=True) + EPS)
    return (y * g.astype(F32)).astype(x.dtype)

def head_rmsnorm(x, g):
    H, d = x.shape[-2], x.shape[-1]
    y = x * lax.rsqrt(jnp.mean(x * x, axis=-1, keepdims=True) + EPS)
    return y * g.astype(F32).reshape(H, d)

def rope(x, pos):
    half = x.shape[-1] // 2
    inv = ROPE_THETA ** (-jnp.arange(half, dtype=F32) / half)
    ang = pos[:, None] * inv[None, :]
    cos = jnp.cos(ang)[None, :, None, :]
    sin = jnp.sin(ang)[None, :, None, :]
    xf = x.astype(F32)
    x1, x2 = xf[..., :half], xf[..., half:]
    return jnp.concatenate([x1 * cos - x2 * sin, x2 * cos + x1 * sin], axis=-1).astype(x.dtype)

def to_chunks(a, c):
    B, T = a.shape[0], a.shape[1]
    return jnp.moveaxis(a.reshape((B, T // c, c) + a.shape[2:]), 1, 0)

def from_chunks(a):
    n, B, c = a.shape[0], a.shape[1], a.shape[2]
    return jnp.moveaxis(a, 0, 1).reshape((B, n * c) + a.shape[3:])

def moba_attend(q, q_pos, k_all, v_all):
    B, Q, H, dh = q.shape
    L = k_all.shape[1]
    nb = -(-L // MOBA_BLOCK)
    pad = ((0, 0), (0, nb * MOBA_BLOCK - L), (0, 0), (0, 0))
    kb = jnp.pad(k_all, pad).reshape(B, nb, MOBA_BLOCK, H, dh)
    vb = jnp.pad(v_all, pad).reshape(B, nb, MOBA_BLOCK, H, dh)
    kmean = jnp.mean(kb.astype(F32), axis=2)
    topk = min(MOBA_TOPK, nb)
    n_slots = topk + 1
    bi = jnp.arange(B)[:, None, None, None]
    hi = jnp.arange(H)[None, None, :, None]
    is_own = (jnp.arange(n_slots) == topk)[:, None]
    offs = jnp.arange(MOBA_BLOCK)
    scale = dh ** -0.5

    def attend(args):
        qc, pc = args
        own = pc // MOBA_BLOCK
        gate = jnp.einsum('bqhd,bnhd->bqhn', qc.astype(F32), kmean)
        past = jnp.arange(nb)[None, :] < own[:, None]
        gate = jnp.where(past[None, :, None, :], gate, -jnp.inf)
        _, sel = lax.top_k(gate, topk)
        own_idx = jnp.broadcast_to(own[None, :, None, None], sel.shape[:3] + (1,)).astype(sel.dtype)
        idx = jnp.concatenate([sel, own_idx], axis=-1)
        kg = kb[bi, idx, :, hi, :]
        vg = vb[bi, idx, :, hi, :]
        s = jnp.einsum('bqhd,bqhjkd->bqhjk', qc.astype(F32), kg.astype(F32)) * scale
        kpos = idx[..., None] * MOBA_BLOCK + offs
        valid = jnp.where(is_own, kpos <= pc[None, :, None, None, None],
                          (idx < own[None, :, None, None])[..., None])
        s = jnp.where(valid, s, -jnp.inf)
        p = jax.nn.softmax(s.reshape(s.shape[:3] + (-1,)), axis=-1).reshape(s.shape)
        return jnp.einsum('bqhjk,bqhjkd->bqhd', p, vg.astype(F32)).astype(q.dtype)

    qblk = MOBA_Q_BLOCK if Q % MOBA_Q_BLOCK == 0 else Q
    out = lax.map(attend, (to_chunks(q, qblk), q_pos.reshape(Q // qblk, qblk)))
    return from_chunks(out)

def retention(q, k, v, s0, chunk):
    log_g = jnp.log1p(-jnp.exp2(-5.0 - jnp.arange(H_B, dtype=F32)))
    i = jnp.arange(chunk, dtype=F32)
    d_in = jnp.exp((i[:, None] + 1.0) * log_g)[None, :, :, None]
    d_out = jnp.exp((chunk - 1.0 - i)[:, None] * log_g)[None, :, :, None]
    diff = i[:, None] - i[None, :]
    d_mask = jnp.where(diff >= 0, jnp.exp(jnp.maximum(diff, 0.0)[None] * log_g[:, None, None]), 0.0)
    g_chunk = jnp.exp(chunk * log_g)[None, :, None, None]

    def step(S, inp):
        qj, kj, vj = (t.astype(F32) for t in inp)
        att = jnp.einsum('bihd,bjhd->bhij', qj, kj) * d_mask
        o = jnp.einsum('bhij,bjhe->bihe', att, vj) + jnp.einsum('bihd,bhde->bihe', qj * d_in, S)
        S = S * g_chunk + jnp.einsum('bjhd,bjhe->bhde', kj * d_out, vj)
        return S, o

    S, o = lax.scan(step, s0.astype(F32), (to_chunks(q, chunk), to_chunks(k, chunk), to_chunks(v, chunk)))
    return from_chunks(o), S

def mlstm(q, k, v, i_pre, f_pre, C0, n0, m0, chunk):
    causal = jnp.tril(jnp.ones((chunk, chunk), dtype=bool))

    def step(carry, inp):
        C, n, m = carry
        qj, kj, vj, ij, fj = (t.astype(F32) for t in inp)
        b = jnp.cumsum(jax.nn.log_sigmoid(fj), axis=1).transpose(0, 2, 1)
        ig = ij.transpose(0, 2, 1)
        log_d = jnp.where(causal, b[..., :, None] - b[..., None, :] + ig[..., None, :], -jnp.inf)
        log_inter = b + m[..., None]
        m_t = jnp.maximum(log_inter, jnp.max(log_d, axis=-1))
        w_intra = jnp.exp(log_d - m_t[..., None])
        w_inter = jnp.exp(log_inter - m_t)
        s = jnp.einsum('bthd,bshd->bhts', qj, kj) * w_intra
        num = (jnp.einsum('bhts,bshe->bthe', s, vj)
               + jnp.einsum('bthd,bhed->bthe', qj, C) * w_inter.transpose(0, 2, 1)[..., None])
        den = jnp.sum(s, axis=-1) + w_inter * jnp.einsum('bthd,bhd->bht', qj, n)
        h = num / jnp.maximum(jnp.abs(den), jnp.exp(-m_t)).transpose(0, 2, 1)[..., None]
        b_last = b[..., -1]
        log_w = b_last[..., None] - b + ig
        m_new = jnp.maximum(b_last + m, jnp.max(log_w, axis=-1))
        w_k = jnp.exp(log_w - m_new[..., None]).transpose(0, 2, 1)[..., None]
        decay = jnp.exp(b_last + m - m_new)
        C = decay[..., None, None] * C + jnp.einsum('bshe,bshd->bhed', vj * w_k, kj)
        n = decay[..., None] * n + jnp.sum(kj * w_k, axis=1)
        return (C, n, m_new), h

    xs = (to_chunks(q, chunk), to_chunks(k, chunk), to_chunks(v, chunk), to_chunks(i_pre, chunk), to_chunks(f_pre, chunk))
    (C, n, m), h = lax.scan(step, (C0.astype(F32), n0.astype(F32), m0.astype(F32)), xs)
    return from_chunks(h), C, n, m

def ab_layer(x, pos, k_prev, v_prev, s0, chunk, norm_g, w_in, ret_g, w_out):
    B, T, _ = x.shape
    z = rmsnorm(x, norm_g) @ w_in
    qa, ka, va, qb, kb, vb, gb = jnp.split(z, AB_SPLITS, axis=-1)
    posf = pos.astype(F32)
    qa = rope(qa.reshape(B, T, H_A, DH_A), posf)
    ka = rope(ka.reshape(B, T, H_A, DH_A), posf)
    va = va.reshape(B, T, H_A, DH_A)
    if k_prev is None:
        k_all, v_all = ka, va
    else:
        k_all = jnp.concatenate([k_prev.astype(ka.dtype), ka], axis=1)
        v_all = jnp.concatenate([v_prev.astype(va.dtype), va], axis=1)
    oa = moba_attend(qa, pos, k_all, v_all)
    qb = rope(qb.reshape(B, T, H_B, DK_B), posf)
    kb = rope(kb.reshape(B, T, H_B, DK_B), posf) * DK_B ** -0.5
    ob, s_new = retention(qb, kb, vb.reshape(B, T, H_B, DV_B), s0, chunk)
    ob = head_rmsnorm(ob, ret_g) * jax.nn.silu(gb.astype(F32)).reshape(B, T, H_B, DV_B)
    mix = jnp.concatenate([oa.reshape(B, T, W_A), ob.reshape(B, T, W_B).astype(x.dtype)], axis=-1)
    return mix @ w_out, ka, va, s_new

def mlstm_layer(x, C0, n0, m0, chunk, norm_g, w_in, gate_bias, out_g, w_out):
    B, T, _ = x.shape
    z = rmsnorm(x, norm_g) @ w_in
    q, k, v, o, ig, fg = jnp.split(z, C_SPLITS, axis=-1)
    q = q.reshape(B, T, H_C, DH_C)
    k = k.reshape(B, T, H_C, DH_C) * DH_C ** -0.5
    v = v.reshape(B, T, H_C, DH_C)
    ig = ig.astype(F32) + gate_bias[0].astype(F32)
    fg = fg.astype(F32) + gate_bias[1].astype(F32)
    h, C, n, m = mlstm(q, k, v, ig, fg, C0, n0, m0, chunk)
    h = head_rmsnorm(h, out_g) * jax.nn.sigmoid(o.astype(F32)).reshape(B, T, H_C, DH_C)
    return h.reshape(B, T, W_C).astype(x.dtype) @ w_out, C, n, m

def conv_ffn(x, buf, norm_g, w1, w3, conv_w, conv_b, w2):
    h = rmsnorm(x, norm_g)
    a = h @ w1
    g = h @ w3
    T = a.shape[1]
    ext = jnp.concatenate([buf.astype(a.dtype), a], axis=1)
    ac = conv_b
    for j in range(CONV_W):
        ac = ac + ext[:, j:j + T] * conv_w[j]
    y = (jax.nn.gelu(ac) * g) @ w2
    return y, ext[:, -(CONV_W - 1):]

def setup_inputs(seed: int = 0) -> dict:
    key = jax.random.key(seed)
    ks = jax.random.split(key, 32)

    def nrm(i, shape, scale):
        return jax.random.normal(ks[i], shape, F32) * scale

    n_pages = PAST_LEN // PAGE_SIZE
    n_pool = (5 * DEC_BATCH * n_pages) // 4
    page_table = jax.random.permutation(ks[4], n_pool)[: DEC_BATCH * n_pages].reshape(DEC_BATCH, n_pages).astype(jnp.int32)
    gate_base = jnp.stack([jnp.zeros((H_C,), F32), jnp.linspace(3.0, 6.0, H_C, dtype=F32)])
    out_scale = 0.5
    return {
        'x_prompt': nrm(0, (BATCH, SEQ, D_MODEL), 1.0),
        'x_sample': nrm(1, (DEC_BATCH, DEC_SEQ, D_MODEL), 1.0),
        'cache_k': nrm(2, (N_AB, n_pool, PAGE_SIZE, H_A, DH_A), 1.0),
        'cache_v': nrm(3, (N_AB, n_pool, PAGE_SIZE, H_A, DH_A), 1.0),
        'page_table': page_table,
        'state_ret': nrm(5, (N_AB, DEC_BATCH, H_B, DK_B, DV_B), 0.3),
        'state_mlstm_C': nrm(6, (N_C, DEC_BATCH, H_C, DH_C, DH_C), 0.3),
        'state_mlstm_n': nrm(7, (N_C, DEC_BATCH, H_C, DH_C), 1.0),
        'state_mlstm_m': nrm(8, (N_C, DEC_BATCH, H_C), 0.5),
        'state_ffn_conv': nrm(9, (DEPTH, DEC_BATCH, CONV_W - 1, D_FF), 1.0),
        'ab_norm_g': 1.0 + nrm(10, (N_AB, D_MODEL), 0.05),
        'ab_w_in': nrm(11, (N_AB, D_MODEL, IN_AB), D_MODEL ** -0.5),
        'ab_ret_norm_g': 1.0 + nrm(12, (N_AB, W_B), 0.05),
        'ab_w_out': nrm(13, (N_AB, W_A + W_B, D_MODEL), out_scale * (W_A + W_B) ** -0.5),
        'c_norm_g': 1.0 + nrm(14, (N_C, D_MODEL), 0.05),
        'c_w_in': nrm(15, (N_C, D_MODEL, IN_C), D_MODEL ** -0.5),
        'c_gate_bias': gate_base[None] + nrm(16, (N_C, 2, H_C), 0.1),
        'c_out_norm_g': 1.0 + nrm(17, (N_C, W_C), 0.05),
        'c_w_out': nrm(18, (N_C, W_C, D_MODEL), out_scale * W_C ** -0.5),
        'ffn_norm_g': 1.0 + nrm(19, (DEPTH, D_MODEL), 0.05),
        'ffn_w1': nrm(20, (DEPTH, D_MODEL, D_FF), D_MODEL ** -0.5),
        'ffn_w3': nrm(21, (DEPTH, D_MODEL, D_FF), D_MODEL ** -0.5),
        'ffn_conv_w': nrm(22, (DEPTH, CONV_W, D_FF), CONV_W ** -0.5),
        'ffn_conv_b': nrm(23, (DEPTH, D_FF), 0.02),
        'ffn_w2': nrm(24, (DEPTH, D_FF, D_MODEL), out_scale * D_FF ** -0.5),
        'final_norm_g': 1.0 + nrm(25, (D_MODEL,), 0.05),
    }

def reference(x_prompt, x_sample, cache_k, cache_v, page_table, state_ret, state_mlstm_C, state_mlstm_n,
              state_mlstm_m, state_ffn_conv, ab_norm_g, ab_w_in, ab_ret_norm_g, ab_w_out, c_norm_g, c_w_in,
              c_gate_bias, c_out_norm_g, c_w_out, ffn_norm_g, ffn_w1, ffn_w3, ffn_conv_w, ffn_conv_b, ffn_w2,
              final_norm_g):
    Bp, Tp, _ = x_prompt.shape
    Bs, Ts, _ = x_sample.shape
    pos_p = jnp.arange(Tp, dtype=jnp.int32)
    pos_s = PAST_LEN + jnp.arange(Ts, dtype=jnp.int32)
    ret_chunk = RET_CHUNK if Tp % RET_CHUNK == 0 else Tp
    ml_chunk = MLSTM_CHUNK if Tp % MLSTM_CHUNK == 0 else Tp
    xp, xs = x_prompt, x_sample
    kp, vp, ksm, vsm, rp, rs = [], [], [], [], [], []
    cp, cs, nps, nss, mps, mss = [], [], [], [], [], []
    fp, fs = [], []
    for l in range(DEPTH):
        j = l // 2
        if l % 2 == 0:
            y, k_new, v_new, s_new = ab_layer(xp, pos_p, None, None, jnp.zeros((Bp, H_B, DK_B, DV_B), F32), ret_chunk,
                                              ab_norm_g[j], ab_w_in[j], ab_ret_norm_g[j], ab_w_out[j])
            xp = xp + y
            kp.append(k_new)
            vp.append(v_new)
            rp.append(s_new)
            k_prev = cache_k[j][page_table].reshape(Bs, PAST_LEN, H_A, DH_A)
            v_prev = cache_v[j][page_table].reshape(Bs, PAST_LEN, H_A, DH_A)
            y, k_new, v_new, s_new = ab_layer(xs, pos_s, k_prev, v_prev, state_ret[j], Ts,
                                              ab_norm_g[j], ab_w_in[j], ab_ret_norm_g[j], ab_w_out[j])
            xs = xs + y
            ksm.append(k_new)
            vsm.append(v_new)
            rs.append(s_new)
        else:
            y, C, n, m = mlstm_layer(xp, jnp.zeros((Bp, H_C, DH_C, DH_C), F32), jnp.zeros((Bp, H_C, DH_C), F32),
                                     jnp.zeros((Bp, H_C), F32), ml_chunk,
                                     c_norm_g[j], c_w_in[j], c_gate_bias[j], c_out_norm_g[j], c_w_out[j])
            xp = xp + y
            cp.append(C)
            nps.append(n)
            mps.append(m)
            y, C, n, m = mlstm_layer(xs, state_mlstm_C[j], state_mlstm_n[j], state_mlstm_m[j], Ts,
                                     c_norm_g[j], c_w_in[j], c_gate_bias[j], c_out_norm_g[j], c_w_out[j])
            xs = xs + y
            cs.append(C)
            nss.append(n)
            mss.append(m)
        y, buf = conv_ffn(xp, jnp.zeros((Bp, CONV_W - 1, D_FF), xp.dtype), ffn_norm_g[l], ffn_w1[l], ffn_w3[l],
                          ffn_conv_w[l], ffn_conv_b[l], ffn_w2[l])
        xp = xp + y
        fp.append(buf)
        y, buf = conv_ffn(xs, state_ffn_conv[l], ffn_norm_g[l], ffn_w1[l], ffn_w3[l],
                          ffn_conv_w[l], ffn_conv_b[l], ffn_w2[l])
        xs = xs + y
        fs.append(buf)
    y_prompt = rmsnorm(xp, final_norm_g)
    y_sample = rmsnorm(xs, final_norm_g)
    return (y_prompt, y_sample, jnp.stack(kp), jnp.stack(vp), jnp.stack(ksm), jnp.stack(vsm),
            jnp.stack(rp), jnp.stack(rs), jnp.stack(cp), jnp.stack(cs), jnp.stack(nps), jnp.stack(nss),
            jnp.stack(mps), jnp.stack(mss), jnp.stack(fp), jnp.stack(fs))


_drawn_inputs = setup_inputs


def setup_inputs(seed=0):
    import zlib

    import numpy as np

    out = dict(_drawn_inputs(seed))
    spreads = {}
    factors = {'cache_k': 2.853, 'ab_ret_norm_g': 2.873, 'c_out_norm_g': 4.51, 'ffn_conv_b': 5.469}
    for name, (base, spread) in spreads.items():
        noise = np.random.default_rng([zlib.crc32(name.encode()), seed]).standard_normal(out[name].shape)
        drawn = base * np.exp(spread * noise) if base else spread * noise
        out[name] = jnp.asarray(drawn.astype(out[name].dtype))
    for name, factor in factors.items():
        out[name] = (out[name] * factor).astype(out[name].dtype)
    return out
```

```python
from contextlib import ExitStack

import concourse.bass as bass
import numpy as np
from concourse import mybir

F32 = mybir.dt.float32
F32R = mybir.dt.float32r
I32 = mybir.dt.int32
ALU = mybir.AluOpType
ACT = mybir.ActivationFunctionType
AX = mybir.AxisListType.X

P = 128
D = 1024
KT = D // P
TP = 256
NB = 8
T = TP + NB
NPAGE = 8
PAST = NPAGE * P
NPOOL = 5 * NB * NPAGE // 4
H = 8
DA = 64
DC = 128
DFF = 11 * D // 4
FT = DFF // P
IN_AB = 7 * H * DA
IN_C = 4 * D + 2 * H
EPS = 1e-6
BIG = 1e30
MOBA_BLOCK = 256
NBLK = PAST // MOBA_BLOCK
TOPK = 3
RING = 4
LOOK = 3
KGROUPS = ((0, 6), (6, 6), (12, 5), (17, 5))
LOG_G = [float(v) for v in np.log1p(-np.exp2(np.float32(-5.0) - np.arange(H, dtype=np.float32))).astype(np.float32)]

C_ID, C_PERM, C_BONES = 0, 128, 256
C_COS, C_SIN = 384, 384 + T
C_AMASK = C_SIN + T
C_RDIFF = C_AMASK + 384
C_MMASK = C_RDIFF + 384
C_RDEC = C_MMASK + 384
C_GAM = C_RDEC + 16
C_QSEL = C_GAM + 4
C_HMASK = C_QSEL + 4
NCONST = C_HMASK + 8
G_AB, G_RET, G_C, G_OUT, G_FFN, G_FIN = 0, 8, 12, 20, 28, 44

JOBS_AFTER = {5: [("t", "qa", 2)], 6: [("b", 0)], 7: [("b", 1)], 8: [("b", 2)], 9: [("b", 3)],
              10: [("t", "ka", 0), ("t", "ka", 1), ("t", "ka", 2)], 13: [("b", 4)],
              14: [("t", "va", 0), ("t", "va", 1), ("t", "va", 2)], 16: [("b", 5)], 19: [("b", 6)],
              21: [("t", "kb", 0), ("t", "kb", 1), ("t", "kb", 2)], 22: [("b", 7)],
              25: [("t", "vb", 0), ("t", "vb", 1), ("t", "vb", 2)]}
JOBS = [j for u in sorted(JOBS_AFTER) for j in JOBS_AFTER[u]]
TILE0 = {"qa": 0, "ka": 4, "va": 8, "qb": 12, "kb": 16, "vb": 20, "gb": 24}
ROPED = list(range(0, 8)) + list(range(12, 20))

JOBS1 = [(n, t, half) for n, t in (("q", 2), ("k", 2), ("v", 2), ("k", 0), ("k", 1), ("v", 0), ("v", 1)) for half in (0, 1)]
CRING = 3
EXP_MAX = 41.0


def jobs_until(u):
    return sum(len(v) for k, v in JOBS_AFTER.items() if k <= u)


def constants():
    c = np.zeros((P, NCONST), np.float32)
    p = np.arange(P)
    c[:, C_ID:C_ID + P] = np.eye(P)
    c[p ^ 32, C_PERM + p] = 1.0
    c[:, C_BONES:C_BONES + P] = (p[:, None] // 64) == (p[None, :] // 64)
    pos = np.concatenate([np.arange(TP), np.full(NB, PAST)]).astype(np.float32)
    inv = np.power(np.float32(10000.0), -(np.arange(32, dtype=np.float32) / np.float32(32))).astype(np.float32)
    ang = (pos[None, :] * inv[p % 32][:, None]).astype(np.float32).astype(np.float64)
    c[:, C_COS:C_COS + T] = np.cos(ang)
    c[:, C_SIN:C_SIN + T] = np.where((p % 64 < 32)[:, None], -np.sin(ang), np.sin(ang))
    j = np.arange(P)
    diag = np.where(j[None, :] > p[:, None], -BIG, 0.0)
    c[:, C_AMASK:C_AMASK + 128] = diag
    c[:, C_AMASK + 256:C_AMASK + 384] = diag
    i = np.concatenate([np.arange(256), np.arange(128)])
    d = (i[None, :] - p[:, None]).astype(np.float64)
    c[:, C_RDIFF:C_RDIFF + 384] = np.where(d >= 0, d, BIG)
    c[:, C_MMASK:C_MMASK + 384] = np.where(d >= 0, 0.0, BIG)
    lg = np.array(LOG_G, np.float64)
    for t in range(2):
        c[:, C_RDEC + 8 * t:C_RDEC + 8 * t + 8] = np.exp((TP - 1 - (t * P + p))[:, None] * lg[None, :])
    for t in range(4):
        c[:, C_GAM + t] = np.exp(lg[2 * t + p // 64])
    c[:, C_QSEL:C_QSEL + 4] = (p[:, None] // 32) == np.arange(4)[None, :]
    c[:, C_HMASK:C_HMASK + 8] = (p[:, None] % 32) == np.arange(8)[None, :]
    return c


def build(nc, consts, x_prompt, x_sample, cache_k, cache_v, page_table, state_ret, state_mlstm_C, state_mlstm_n,
          state_mlstm_m, state_ffn_conv, ab_norm_g, ab_w_in, ab_ret_norm_g, ab_w_out, c_norm_g, c_w_in,
          c_gate_bias, c_out_norm_g, c_w_out, ffn_norm_g, ffn_w1, ffn_w3, ffn_conv_w, ffn_conv_b, ffn_w2,
          final_norm_g, y_prompt, y_sample, k_prompt, v_prompt, k_sample, v_sample, ret_prompt, ret_sample,
          C_prompt, C_sample, n_prompt, n_sample, m_prompt, m_sample, conv_prompt, conv_sample):
    with ExitStack() as ctx:
        sems = {}

        def sem(name):
            if name not in sems:
                sems[name] = ctx.enter_context(nc.semaphore(name))
            return sems[name]

        def sbuf(stack, name, shape, dt=F32):
            return stack.enter_context(nc.sbuf_tensor(name, shape, dt))

        raw = [sbuf(ctx, f"w_raw{i}", [P, 8, 256]) for i in range(RING)]
        whi = [sbuf(ctx, f"w_hi{i}", [P, 8, P], F32R) for i in range(RING)]
        wlo = [sbuf(ctx, f"w_lo{i}", [P, 8, P], F32R) for i in range(RING)]
        x = sbuf(ctx, "x", [P, KT, T])
        sq = sbuf(ctx, "sq", [P, KT, T])
        actA = [sbuf(ctx, "actA_hi", [P, KT, T], F32R), sbuf(ctx, "actA_lo", [P, KT, T], F32R)]
        cst = sbuf(ctx, "cst", [P, NCONST])
        ones = sbuf(ctx, "ones", [P, P])
        gains = sbuf(ctx, "gains", [P, 52])
        convp = [sbuf(ctx, f"convp{l}", [P, 4, FT]) for l in range(2)]
        convb = [sbuf(ctx, f"convb{l}", [P, NB, 2, FT]) for l in range(2)]
        rstd = sbuf(ctx, "rstd", [P, T])
        var = sbuf(ctx, "var", [P, T])
        nwt = sbuf(ctx, "nwt", [P, T])
        bank = [ctx.enter_context(nc.psum_tensor(f"bank{i}", [P, 512], F32)) for i in range(8)]

        with ExitStack() as st:
            z0 = sbuf(st, "z0", [P, 28, T])
            tok = {n: sbuf(st, f"tok_{n}", [P, 2, 512]) for n in ("ka", "va", "kb", "vb")}
            tks = {n: sbuf(st, f"tks_{n}", [NB, 512]) for n in ("qa", "ka", "va", "kb", "vb")}
            kv = [sbuf(st, f"kv{i}", [P, 2, 512]) for i in range(4)]
            smx = [sbuf(st, f"smx{i}", [P, 384]) for i in range(2)]
            ptt = [sbuf(st, f"ptt{i}", [P, 384]) for i in range(2)]
            rmk = [sbuf(st, f"rmk{i}", [P, 384]) for i in range(2)]
            sc_all = sbuf(st, "sc_all", [P, NPAGE, NB, H])
            s0 = sbuf(st, "s0", [P, 4, NB, DA])
            sm = sbuf(st, "sm", [P, 80])
            pts = sbuf(st, "pts", [P, NPAGE, 64])
            rst = sbuf(st, "rst", [64, 512])
            dgs = sbuf(st, "dgs", [NB, NB, H])
            dgp = sbuf(st, "dgp", [NB, NB, H])
            pg = sbuf(st, "pg", [1, NB * NPAGE], I32)
        zf = z0[:, :, :].rearrange("p a b -> p (a b)")
        kdec = zf[:, 4 * T:4 * T + 1024].rearrange("p (t n) -> p t n", t=2)
        ovv = tok["kb"]
        prd = zf[0:NB, 20 * T:20 * T + 512]
        sqf = sq[:, :, :].rearrange("p a b -> p (a b)")
        qb = [sqf[:, 512 * i:512 * i + 512] for i in range(4)]
        prow = sqf[0:64, 0:PAST]
        vdg = [sqf[0:NB, 1024 + 512 * i:1536 + 512 * i].rearrange("p (b e) -> p b e", b=NB) for i in range(2)]

        with ExitStack() as st:
            actB = [sbuf(st, "actB_hi", [P, KT, T], F32R), sbuf(st, "actB_lo", [P, KT, T], F32R)]
            hff = [sbuf(st, "hff_hi", [P, FT, T], F32R), sbuf(st, "hff_lo", [P, FT, T], F32R)]
            ffa = [sbuf(st, f"ffa{i}", [P, 2 + T]) for i in range(4)]
            fft = [sbuf(st, f"fft{i}", [P, T]) for i in range(4)]
            ffg = [sbuf(st, f"ffg{i}", [P, T]) for i in range(4)]
            ffp = sbuf(st, "ffp", [P, NB, FT])
            ffq = sbuf(st, "ffq", [P, NB, FT])
            fat = sbuf(st, "fat", [P, 10, FT])
            fco = sbuf(st, "fco", [110, 2, P])

        with ExitStack() as st:
            z1 = sbuf(st, "z1", [P, 32, T])
            tk1 = {n: sbuf(st, f"tok1_{n}", [P, 2, D]) for n in ("k", "v")}
            ts1 = {n: sbuf(st, f"tks1_{n}", [NB, D]) for n in ("q", "k", "v", "n")}
            cs = [sbuf(st, f"cs{i}", [P, H, DC]) for i in range(CRING)]
            vm = [sbuf(st, f"vm{i}", [NB, D]) for i in range(2)]
            prod = sbuf(st, "prod", [P, D])
            ew = [sbuf(st, f"ew{i}", [P, 384]) for i in range(2)]
            s8 = sbuf(st, "s8", [NB, 13, NB])
            dd = sbuf(st, "dd", [NB, NB, H])
            g8 = sbuf(st, "g8", [H, 4])
            acol = sbuf(st, "acol", [P, 2, H])
            decb = sbuf(st, "decb", [P, NB, H])
            ncol = sbuf(st, "ncol", [P, H])
            sel = sbuf(st, "sel", [P, 2 * H - 1])
            qkv_scale = sbuf(st, "qkv_scale", [P, 3])
        ww = [cst[:, C_AMASK:C_AMASK + 384], cst[:, C_RDIFF:C_RDIFF + 384]]
        R_I, R_F, R_D, R_T, R_B, R_A, R_M, R_E = (sq[0:H, n, :] for n in range(8))


        y_rows = [raw[i][:, 0:4, :].rearrange("p a b -> p (a b)") for i in range(3)]
        x_tok = zf[:, 0:2048].rearrange("p (t n) -> p t n", t=2)
        xs_tok = zf[0:NB, 2112:3136]
        vec_rows = zf[0:52, 3200:3328]
        cw_rows = [zf[0:88, 3328 + 128 * l:3456 + 128 * l] for l in range(2)]
        cb_rows = [zf[0:88, 3584 + 512 * l:4096 + 512 * l].rearrange("p (q n) -> p q n", q=4) for l in range(2)]
        ident = cst[:, C_ID:C_ID + P]
        perm = cst[:, C_PERM:C_PERM + P]
        bones = cst[:, C_BONES:C_BONES + P]
        cos = cst[:, C_COS:C_COS + T]
        sin = cst[:, C_SIN:C_SIN + T]
        eye8 = cst[0:NB, C_ID:C_ID + NB]

        def zt(n, c, a=0, b=T):
            return z0[:, TILE0[n] + c, a:b]

        U_IN0, U_OUT0, U_UP0, U_DN0, U_IN1, U_OUT1, U_UP1, U_DN1, U_END = np.cumsum(
            [0, 28, 8, 44, 32, 34, 8, 44, 32]).tolist()
        E_IN0, E_OUT0, E_UP0, E_DN0, E_IN1, E_OUT1, E_UP1, E_DN1, E_END = np.cumsum(
            [0, 28, 8, 44, 8, 34, 8, 44, 8]).tolist()

        def row_tiles(u):
            for u0 in (U_DN0, U_DN1):
                if u0 <= u < u0 + 32:
                    return KGROUPS[(u - u0) // 2 % 4]
            return 0, 8

        w_in0 = ab_w_in[0].rearrange("(k p) n -> p k n", p=P)
        w_out0 = ab_w_out[0].rearrange("(k p) n -> p k n", p=P)
        w_in1 = c_w_in[0].rearrange("(k p) n -> p k n", p=P)
        w_out1 = c_w_out[0].rearrange("(k p) n -> p k n", p=P)
        w_a = [ffn_w1[l].rearrange("(k p) n -> p k n", p=P) for l in range(2)]
        w_g = [ffn_w3[l].rearrange("(k p) n -> p k n", p=P) for l in range(2)]
        w_d = [ffn_w2[l].rearrange("(k p) n -> p k n", p=P) for l in range(2)]

        block = ctx.enter_context(nc.Block())

        @block.sync
        def _(sp):
            def load_raw(r, src, i8=0):
                if r >= RING:
                    sp.wait_ge(sem("lo_ready"), 2 * (r - RING) + 2 + i8)
                sp.dma_start(raw[r % RING][:, 0:src.shape[1], :], src).then_inc(sem(f"w_landed{r % RING}"), 16)

            def page_pair(j, cache, freed):
                if freed is not None:
                    sp.wait_ge(*freed)
                for t in range(2):
                    i = 8 * (j // 4) + 2 * (j % 4) + t
                    row = sp.value_load(pg[0:1, i:i + 1], min_val=0, max_val=NPOOL - 1)
                    sp.dma_start(kv[j % 4][:, t, :], cache[0, bass.ds(row, 1)].rearrange("o p h d -> p (o h d)")
                                 ).then_inc(sem(f"kv_landed{j % 4}"), 16)

            def k_pages(j):
                page_pair(j, cache_k, (sem("k_reduced"), j - 3) if j >= 4 else None)

            for n in range(14):
                load_raw(n, w_in0[:, :, 256 * n:256 * n + 256])
                if n == 0:
                    for at, v in ((G_FFN, ffn_norm_g[0]), (G_FFN + 8, ffn_norm_g[1]), (G_FIN, final_norm_g)):
                        sp.dma_start(vec_rows[at:at + 8, :], v.rearrange("(k p) -> k p", p=P)).then_inc(sem("x_landed"), 16)
                    sp.wait_ge(sem("x_landed"), 16 * 9)
                if n == 4:
                    sp.wait_ge(sem("pages_landed"), 16)
                    for j in range(4):
                        k_pages(j)
                if n >= 10:
                    k_pages(2 * n - 16)
                    k_pages(2 * n - 15)
            for n in range(4):
                load_raw(U_OUT0 // 2 + n, w_out0[:, :, 256 * n:256 * n + 256])
                k_pages(12 + 2 * n)
                k_pages(13 + 2 * n)
            for j in range(20, 32):
                k_pages(j)
            for j in range(32):
                page_pair(j, cache_v, (sem("k_reduced"), 29 + j) if j < 4 else (sem("v_used"), j - 3))

            def ffn_loads(l, u_up, u_dn):
                def pair(n, c, i8):
                    load_raw(u_up // 2 + 2 * n, w_a[l][:, :, bass.ds(c, 256)], i8)
                    load_raw(u_up // 2 + 2 * n + 1, w_g[l][:, :, bass.ds(c, 256)], i8)
                with sp.Fori(0, 5) as i:
                    pair(0, i * 512, i * 8)
                    pair(1, i * 512 + 256, i * 8)
                pair(10, 2560, 0)

                def chunk(n, c, i16):
                    for g, (k0, nk) in enumerate(KGROUPS):
                        load_raw(u_dn // 2 + 4 * n + g, w_d[l][:, k0:k0 + nk, bass.ds(c, 256)], i16)
                with sp.Fori(0, 2) as i:
                    chunk(0, i * 512, i * 16)
                    chunk(1, i * 512 + 256, i * 16)

            ffn_loads(0, U_UP0, U_DN0)
            sp.wait_ge(sem("lo_ready"), U_IN1 - 2 * RING + 2)
            with nc.allow_non_contiguous_dma(reason="16 columns of gates"):
                for t, name in ((0, f"w_landed{U_IN1 // 2 % RING}"), (1, "f_gate_landed")):
                    sp.dma_start(raw[U_IN1 // 2 % RING][:, :, P * t:P * t + H],
                                 w_in1[:, :, 4 * D + H * t:4 * D + H * t + H]).then_inc(sem(name), 16)
            with sp.Fori(0, 4) as i:
                for n in range(4):
                    load_raw(U_IN1 // 2 + 1 + n, w_in1[:, :, bass.ds(i * 1024 + 256 * n, 256)], i * 8)
            sp.wait_ge(sem("c_small"), 64)

            def c_load(b):
                sp.dma_start(cs[b % CRING][:], state_mlstm_C[0, b].rearrange("h e d -> e h d")
                             ).then_inc(sem(f"c_landed{b % CRING}"), 16)
            for b in range(CRING):
                c_load(b)
            for n in range(4):
                load_raw(U_OUT1 // 2 + n, w_out1[:, :, 256 * n:256 * n + 256])
            for b in range(NB):
                sp.wait_ge(sem("c_added"), 2 * b + 2)
                sp.dma_start(C_sample[0, b].rearrange("h e d -> e h d"), cs[b % CRING][:]
                             ).then_inc(sem(f"c_stored{b % CRING}"), 16)
                n = b + CRING - 1
                if CRING <= n < NB:
                    sp.wait_ge(sem(f"c_stored{n % CRING}"), 16 * (n // CRING))
                    sp.wait_ge(sem("q_mult"), 2 * (n - CRING) + 2)
                    c_load(n)
            ffn_loads(1, U_UP1, U_DN1)

        @block.gpsimd
        def _(pool):
            G = nc.gpsimd
            G.memset(ones[:], 1.0).then_inc(sem("ones_ready"), 1)
            pool.dma_start(pg[:], page_table.rearrange("(o b) n -> o (b n)", o=1)).then_inc(sem("pages_landed"), 16)
            for l in range(2):
                pool.dma_start(cw_rows[l][0:66, :], ffn_conv_w[l].rearrange("j (f p) -> (j f) p", p=P)
                               ).then_inc(sem("param_landed"), 16)
                pool.dma_start(cw_rows[l][66:88, :], ffn_conv_b[l].rearrange("(f p) -> f p", p=P)
                               ).then_inc(sem("param_landed"), 16)
                for q in range(4):
                    pool.dma_start(cb_rows[l][:, q, :],
                                   state_ffn_conv[l, 2 * q:2 * q + 2].rearrange("b j (f p) -> (b j f) p", p=P)
                                   ).then_inc(sem("param_landed"), 16)
            for b in range(NB):
                pool.dma_start(s0[:, :, b, :], state_ret[0, b].rearrange("(c q) d e -> (q d) c e", q=2)
                               ).then_inc(sem("s0_landed"), 16)
            for l in range(2):
                pool.dma_start(conv_sample[l, :, 0, :], state_ffn_conv[l, :, 1, :]).then_inc(sem("row_stored"), 16)
            pool.wait_ge(sem("const_landed"), 32)
            pool.wait_ge(sem("const_landed"), 16)

            def k_mult(j):
                b = j // 4
                if j % 4 == 0:
                    pool.wait_ge(sem("jobs_out"), JOBS.index(("b", b)) + 1)
                pool.wait_ge(sem(f"kv_landed{j % 4}"), 32 * (j // 4 + 1))
                G.tensor_tensor(kv[j % 4][:], kv[j % 4][:], qb[b % 4].unsqueeze(1).to_broadcast([P, 2, 512]),
                                ALU.mult).then_inc(sem("k_mult"), 1)

            for u in range(28):
                if u in ROPED:
                    r = ROPED.index(u)
                    pool.wait_ge(sem("evac_done"), u + 1)
                    if r >= 2:
                        pool.wait_ge(sem("roped"), r - 1)
                    G.tensor_tensor(rmk[r % 2][:, 0:T], z0[:, u, :], cos, ALU.mult).then_inc(sem("cos_prod"), 1)
                if u >= 8:
                    k_mult(u - 8)
            for j in range(20, 32):
                k_mult(j)
            pool.wait_ge(sem("k_mult"), 32)
            pool.wait_ge(sem("jobs_out"), len(JOBS))
            for h in range(H):
                if h >= 2:
                    pool.wait_ge(sem("kv_outer"), h - 1)
                G.tensor_tensor(vdg[h % 2], eye8.unsqueeze(2).to_broadcast([NB, NB, DA]),
                                tks["vb"][:, DA * h:DA * h + DA].unsqueeze(1).to_broadcast([NB, NB, DA]),
                                ALU.mult).then_inc(sem("v_diag"), 1)
            pool.wait_ge(sem("gate_act"), 1)
            pool.wait_ge(sem("ob_prompt"), 4)
            pool.wait_ge(sem("ob_sample"), 2)
            G.tensor_tensor(z0[:, 24:28, :], z0[:, 24:28, :], z0[:, 8:12, :], ALU.mult).then_inc(sem("ob_gated"), 1)

            def ffn_pool(l, stage):
                pool.wait_ge(sem("x_ready"), 8 * (stage + 1))
                for s in range(4):
                    G.memset(ffa[s][:, 0:2], 0.0).then_inc(sem("pad_zero"), 1)

                def group(f, i4, fd):
                    for t in range(2):
                        pool.wait_ge(sem("a_ready"), f + t + 1 + i4 + FT * l)
                        G.tensor_copy(fat[:, :, bass.ds(fd + t, 1)],
                                      ffa[(f + t) % 4][:, 256:266].unsqueeze(2)).then_inc(sem("a_kept"), 1)
                    for t in range(2):
                        s = (f + t) % 4
                        pool.wait_ge(sem("gelu"), f + t + 1 + i4 + FT * l)
                        pool.wait_ge(sem("g_ready"), f + t + 1 + i4 + FT * l)
                        G.tensor_tensor(ffg[s][:], ffg[s][:], fft[s][:], ALU.mult).then_inc(sem("gated"), 1)
                with pool.Fori(0, 5) as i:
                    group(0, i * 4, i * 4)
                    group(2, i * 4, i * 4 + 2)
                group(20, 0, 20)

            ffn_pool(0, 1)
            pool.wait_ge(sem("c_small"), 64)
            G.memset(sel[:], 0.0).then_inc(sem("sel_ready"), 1)
            pool.wait_ge(sem("sel_ready"), 1)
            G.memset(sel[:, H - 1:H], 1.0).then_inc(sem("sel_ready"), 1)
            pool.wait_ge(sem("small_out"), 2)
            pool.wait_ge(sem("jobs_out"), len(JOBS) + len(JOBS1))


            def rows(name):
                return ts1[name][:].rearrange("p (h d) -> p h d", h=H)


            def weight(n):
                return s8[:, n, :].unsqueeze(2).to_broadcast([NB, H, DC])


            G.tensor_tensor(rows("v"), rows("v"), weight(9), ALU.mult).then_inc(sem("v_weighted"), 1)


            def c_decay(b):
                pool.wait_ge(sem(f"c_landed{b % CRING}"), 16 * (b // CRING + 1))
                G.tensor_tensor(cs[b % CRING][:], cs[b % CRING][:], decb[:, b, :].unsqueeze(2).to_broadcast([P, H, DC]),
                                ALU.mult).then_inc(sem("c_decayed"), 1)


            pool.wait_ge(sem("small_out"), 3)
            c_decay(0)
            c_decay(1)
            pn = prod[0:NB, :].rearrange("p (h d) -> p h d", h=H)
            G.tensor_tensor(rows("n"), rows("n"), weight(8), ALU.mult).then_inc(sem("n_step"), 1)
            G.tensor_tensor(pn, rows("k"), weight(9), ALU.mult).then_inc(sem("n_step"), 1)
            pool.wait_ge(sem("n_step"), 2)
            G.tensor_tensor(rows("n"), rows("n"), pn, ALU.add).then_inc(sem("n_step"), 1)
            pool.wait_ge(sem("n_step"), 3)
            G.tensor_tensor(pn, rows("n"), rows("q"), ALU.mult).then_inc(sem("n_step"), 1)
            for b in range(2, NB):
                c_decay(b)
            pool.wait_ge(sem("gate_act"), 2)
            pool.wait_ge(sem("head_out"), 3 * H)
            pool.wait_ge(sem("num_sample"), NB)
            for t in range(2):
                a = 24 + 4 * t
                G.tensor_tensor(z1[:, a:a + 4, :], z1[:, a:a + 4, :], z1[:, a - 8:a - 4, :], ALU.mult).then_inc(sem("o1_gated"), 1)
            ffn_pool(1, 3)

        @block.scalar
        def _(act):
            A = nc.scalar.activation
            act.dma_start(cst[:, 0:C_COS], consts[:, 0:C_COS]).then_inc(sem("const_landed"), 16)
            act.dma_start(x_tok, x_prompt[0].rearrange("(t p) n -> p t n", p=P)).then_inc(sem("x_landed"), 16)
            act.dma_start(xs_tok, x_sample.rearrange("b o n -> (b o) n")).then_inc(sem("x_landed"), 16)
            for at, v, n in ((G_AB, ab_norm_g[0], 8), (G_RET, ab_ret_norm_g[0], 4), (G_C, c_norm_g[0], 8),
                             (G_OUT, c_out_norm_g[0], 8)):
                act.dma_start(vec_rows[at:at + n, :], v.rearrange("(k p) -> k p", p=P)).then_inc(sem("x_landed"), 16)
            act.dma_start(cst[:, C_COS:NCONST], consts[:, C_COS:NCONST]).then_inc(sem("const_landed"), 16)
            n_stored = 0

            def split_hi(u, i8=0):
                if u >= U_END:
                    return
                act.wait_ge(sem(f"w_landed{u // 2 % RING}"), 16 * (u // 8 + 1) + i8 * 2)
                if u == U_IN1 + 1:
                    act.wait_ge(sem("f_gate_landed"), 16)
                if u >= RING:
                    act.wait_ge(sem("mm_done"), u - RING + 1 + i8)
                nk = row_tiles(u)[1]
                A(whi[u % RING][:, 0:nk, :], raw[u // 2 % RING][:, 0:nk, P * (u % 2):P * (u % 2) + P], ACT.Copy
                  ).then_inc(sem("hi_ready"), 1)

            def norm_in(stage, k, g, dst, i=0):
                act.wait_ge(sem("x_ready"), 8 * stage + k + 1 + i)
                if g is not None:
                    A(dst[0][:, bass.ds(i + k, 1), :], x[:, bass.ds(i + k, 1), :], ACT.Copy,
                      scale=gains[:, bass.ds(g + k + i, 1)]).then_inc(sem("norm_hi"), 1)
                A(sq[:, bass.ds(i + k, 1), :], x[:, bass.ds(i + k, 1), :], ACT.Square).then_inc(sem("sq_ready"), 1)

            def rsqrt_seed(name, n, src, tmp, dst):
                act.preload_act_table_set("natural_log_exp_and_others")
                act.wait_ge(sem(f"{name}_var"), n)
                A(tmp, src, ACT.Ln).then_inc(sem("ln_done"), 1)
                lns[0] += 1
                act.wait_ge(sem("ln_done"), lns[0])
                A(dst, tmp, ACT.Exp, scale=-0.5).then_inc(sem(f"{name}_seed"), 1)

            lns = [0]
            act.wait_ge(sem("param_t"), 1)
            A(gains[:], bank[4][:, 0:52], ACT.Copy).then_inc(sem("param_out"), 1)
            act.wait_ge(sem("param_out"), 1)
            split_hi(0)
            for k in range(KT):
                norm_in(0, k, G_AB, actA)
                if k % 3 == 2:
                    split_hi(k // 3 + 1)
            split_hi(3)
            rsqrt_seed("rms", 1, var[:], nwt[:], rstd[:])

            def evict_jobs(a, b):
                for n in range(a, b):
                    act.wait_ge(sem("jobs_in"), n + 1)
                    if JOBS[n][0] == "b":
                        s = JOBS[n][1]
                        if s >= 4:
                            act.wait_ge(sem("k_mult"), 4 * (s - 4) + 4)
                        dst = qb[s % 4]
                    else:
                        dst = tks[JOBS[n][1]][:] if JOBS[n][2] == 2 else tok[JOBS[n][1]][:, JOBS[n][2], :]
                    A(dst, bank[6 + n % 2][0:dst.shape[0], :], ACT.Copy).then_inc(sem("jobs_out"), 1)

            for u in range(28):
                split_hi(u + LOOK + 1)
                evict_jobs(jobs_until(u - 1), jobs_until(u))
                if u == 0:
                    act.wait_ge(sem("param_t"), 2)
                    for l in range(2):
                        A(convp[l][:].rearrange("p a b -> p (a b)"), bank[4][:, 64 + 96 * l:152 + 96 * l], ACT.Copy
                          ).then_inc(sem("param_out"), 1)
                    for l in range(2):
                        act.wait_ge(sem("param_t"), 3 + l)
                        A(convb[l][:].rearrange("p b j f -> p (b j f)"), bank[5 + l][:, 0:352], ACT.Copy).then_inc(sem("param_out"), 1)
            act.wait_ge(sem("evac_done"), 28)
            A(z0[:, 24:28, :], z0[:, 24:28, :], ACT.Silu).then_inc(sem("gate_act"), 1)
            act.wait_ge(sem("jobs_out"), len(JOBS))
            for n, op, os_ in (("ka", k_prompt, k_sample), ("va", v_prompt, v_sample)):
                act.dma_start(op[0, 0].rearrange("(t p) h d -> p t (h d)", p=P), tok[n][:]).then_inc(sem("stored"), 16)
                act.dma_start(os_[0].rearrange("b o h d -> (b o) (h d)"), tks[n][:]).then_inc(sem("stored"), 16)
            n_stored += 4

            def attn_exp(h):
                act.wait_ge(sem("attn_nmax"), h + 1)
                for t, (a, b) in enumerate(((0, 128), (128, 384))):
                    c = 4 + 2 * (h % 2) + t
                    A(smx[h % 2][:, a:b], smx[h % 2][:, a:b], ACT.Exp, bias=sm[:, c:c + 1], scale=DA ** -0.5,
                      accum_out=sm[:, c + 4:c + 5]).then_inc(sem("attn_exp"), 1)

            def attn_pt(h):
                act.wait_ge(sem("attn_pt"), h + 1)
                if h >= 2:
                    act.wait_ge(sem("attn_pv"), h - 1)
                A(ptt[h % 2][:], bank[6 + h % 2][:, 0:384], ACT.Copy).then_inc(sem("attn_pt_out"), 1)

            def attn_out(c):
                act.wait_ge(sem("attn_pv"), 2 * c + 2)
                A(actA[0][:, c, 0:TP], bank[c % 2][:, 0:TP], ACT.Copy).then_inc(sem("attn_hi"), 1)

            for h in range(H):
                attn_exp(h)
                if h >= 1:
                    attn_pt(h - 1)
                if h >= 3 and h % 2:
                    attn_out((h - 3) // 2)
            attn_pt(H - 1)
            attn_out(3)

            act.wait_ge(sem("k_mult"), 32)
            for t in range(2):
                act.wait_ge(sem("samp_st"), t + 1)
                A(prow[:, 512 * t:512 * t + 512], bank[4 + t][0:64, :], ACT.Copy).then_inc(sem("samp_rows"), 1)

            def ret_mask(h):
                if h >= 2:
                    act.wait_ge(sem("ret_masked"), h - 1)
                A(rmk[h % 2][:], cst[:, C_RDIFF:C_RDIFF + 384], ACT.Exp, scale=LOG_G[h]).then_inc(sem("ret_mask"), 1)

            def ob_out(c):
                act.wait_ge(sem("ret_pv"), 2 * c + 2)
                A(z0[:, 8 + c, 0:TP], bank[2 + c % 2][:, 0:TP], ACT.Copy).then_inc(sem("ob_prompt"), 1)

            act.wait_ge(sem("roped"), 16)
            ret_mask(0)
            ret_mask(1)
            act.wait_ge(sem("samp_bias"), 1)
            for n in range(NBLK):
                blk = prow[:, MOBA_BLOCK * n:MOBA_BLOCK * n + MOBA_BLOCK]
                A(blk, blk, ACT.Exp, bias=sm[0:64, 24 + n:25 + n], scale=DA ** -0.5,
                  accum_out=sm[0:64, 32 + n:33 + n]).then_inc(sem("samp_exp"), 1)
            A(sm[0:64, 36:37], sm[0:64, 68:69], ACT.Exp, bias=sm[0:64, 28:29], scale=DA ** -0.5).then_inc(sem("samp_exp"), 1)
            act.wait_ge(sem("samp_pt"), 1)
            A(pts[:].rearrange("p a b -> p (a b)"), bank[6][:, :], ACT.Copy).then_inc(sem("samp_pt_out"), 1)
            for h in range(2, H):
                ret_mask(h)
                if h % 2 and h >= 3:
                    ob_out((h - 3) // 2)
            ob_out(3)
            act.wait_ge(sem("ret_state"), 1)
            A(rst[:], bank[0][0:64, :], ACT.Copy).then_inc(sem("ret_state_out"), 1)
            act.wait_ge(sem("ret_state_out"), 1)
            act.dma_start(ret_prompt[0, 0].rearrange("h d e -> d h e"), rst[:].rearrange("p (h e) -> p h e", h=H)
                          ).then_inc(sem("stored"), 16)
            n_stored += 1
            act.wait_ge(sem("s_new"), 4)
            for b in range(NB):
                act.dma_start(ret_sample[0, b].rearrange("(c q) d e -> (q d) c e", q=2), s0[:, :, b, :]).then_inc(sem("stored"), 16)
            n_stored += 8
            act.wait_ge(sem("ob_sample"), 2)
            A(z0[:, 0:4, :], z0[:, 8:12, :], ACT.Square).then_inc(sem("ret_sq"), 1)
            rsqrt_seed("ret", 4, z0[:, 4:8, :], z0[:, 16:20, :], z0[:, 20:24, :])
            for c in range(4):
                act.wait_ge(sem("ret_mix"), c + 1)
                A(actA[0][:, 4 + c, :], z0[:, c, :], ACT.Copy).then_inc(sem("ret_hi"), 1)
            act.wait_ge(sem("samp_o"), 1)
            A(actA[0][:, 0:4, TP:T], bank[5][:, 0:32].rearrange("p (c b) -> p c b", c=4), ACT.Copy).then_inc(sem("samp_hi"), 1)

            act.wait_ge(sem("stored"), 16 * n_stored)
            for n in range(8):
                split_hi(U_OUT0 + n + LOOK + 1)
                norm_in(1, n, G_FFN, actB)

            def ffn_act(l, stage, u_up, u_dn, g_next, dst_next):
                rsqrt_seed("rms", stage + 1, var[:], nwt[:], rstd[:])

                def first_tap(f, i4, fd):
                    act.wait_ge(sem("a_ready"), f + 1 + i4 + FT * l)
                    A(fft[f % 4][:, 0:TP], ffa[f % 4][:, 0:TP], ACT.Identity, scale=convp[l][:, 0, bass.ds(fd, 1)],
                      bias=convp[l][:, 3, bass.ds(fd, 1)]).then_inc(sem("tap"), 1)

                def gelu(f, i4):
                    act.wait_ge(sem("conv"), f + 1 + i4 + FT * l)
                    A(fft[f % 4][:], fft[f % 4][:], ACT.Gelu_apprx_tanh).then_inc(sem("gelu"), 1)

                def h_hi(f, i4, fd):
                    act.wait_ge(sem("gated"), f + 1 + i4 + FT * l)
                    A(hff[0][:, bass.ds(fd, 1), :], ffg[f % 4][:].unsqueeze(1), ACT.Copy).then_inc(sem("h_hi"), 1)

                def group(f, u, i4, i8, fd, first=False):
                    split_hi(u + LOOK + 1, i8)
                    first_tap(f, i4, fd)
                    if not first:
                        h_hi(f - 2, i4, fd - 2)
                    split_hi(u + LOOK + 2, i8)
                    first_tap(f + 1, i4, fd + 1)
                    if not first:
                        h_hi(f - 1, i4, fd - 1)
                    split_hi(u + LOOK + 3, i8)
                    gelu(f, i4)
                    split_hi(u + LOOK + 4, i8)
                    gelu(f + 1, i4)

                def conv_rows_out():
                    for g in range(2):
                        act.wait_ge(sem("conv_t"), g + 1 + 2 * l)
                        A(fco[:, g, :], bank[4 + g][0:110, 0:P], ACT.Copy).then_inc(sem("conv_t_out"), 1)
                    act.wait_ge(sem("conv_t_out"), 2 + 2 * l)
                    for o, rows in ((conv_prompt[l, 0], fco[0:2 * FT, 0, :]),
                                    (conv_sample[l, 0:3, 1], fco[2 * FT:5 * FT, 0, :]),
                                    (conv_sample[l, 3:8, 1], fco[0:5 * FT, 1, :])):
                        act.dma_start(o.rearrange("t (f p) -> t f p", p=P), rows).then_inc(sem("stored"), 16)

                act.wait_ge(sem("pad_zero"), 4 + 4 * l)
                group(0, u_up, 0, 0, 0, True)
                with act.Fori(0, 5) as i:
                    group(2, u_up + 4, i * 4, i * 8, i * 4 + 2)
                    group(4, u_up + 8, i * 4, i * 8, i * 4 + 4)

                for c in range(4):
                    for j in range(8):
                        split_hi(u_dn + 8 * c + j + LOOK + 1)
                        if c == 0 and j == 1:
                            h_hi(FT - 2, 0, FT - 2)
                            h_hi(FT - 1, 0, FT - 1)
                    for t in range(2):
                        norm_in(stage + 1, 2 * c + t, g_next, dst_next)
                    if c == 0:
                        conv_rows_out()

            ffn_act(0, 1, U_UP0, U_DN0, G_C, actA)
            n_stored += 3
            act.wait_ge(sem("stored"), 16 * n_stored)
            act.dma_start(g8[:, 0:1], c_gate_bias[0, 0].rearrange("(h o) -> h o", o=1)).then_inc(sem("c_small"), 16)
            act.dma_start(g8[:, 1:2], c_gate_bias[0, 1].rearrange("(h o) -> h o", o=1)).then_inc(sem("c_small"), 16)
            with nc.allow_non_contiguous_dma(reason="64 values, turned"):
                act.dma_start(s8[:, 0, :], state_mlstm_m[0].rearrange("b h -> h b")).then_inc(sem("c_small"), 16)
            act.dma_start(ts1["n"][:], state_mlstm_n[0].rearrange("b h d -> b (h d)")).then_inc(sem("c_small"), 16)
            rsqrt_seed("rms", 3, var[:], nwt[:], rstd[:])
            split_hi(U_IN1 + 4)
            split_hi(U_IN1 + 5)
            act.wait_ge(sem("gates_in"), 4)
            A(R_T, R_F, ACT.Abs).then_inc(sem("ls"), 1)
            act.wait_ge(sem("ls"), 1)
            A(R_T, R_T, ACT.Exp, scale=-1.0).then_inc(sem("ls"), 1)
            act.wait_ge(sem("ls"), 2)
            A(R_T, R_T, ACT.Ln, bias=1.0).then_inc(sem("ls"), 1)
            with act.Fori(0, 3) as i:
                for j in range(8):
                    split_hi(U_IN1 + 6 + j, i * 8)
            split_hi(U_IN1 + 30)
            act.wait_ge(sem("m_ready"), 1)
            A(R_E[:, 0:TP], R_E[:, 0:TP], ACT.Exp, scale=-1.0).then_inc(sem("gate_exp"), 1)
            act.wait_ge(sem("s_gates"), 1)
            A(R_E[:, TP:T], s8[:, 3, :], ACT.Exp).then_inc(sem("gate_exp"), 1)
            A(s8[:, 4:7, :], s8[:, 1:4, :], ACT.Exp).then_inc(sem("gate_exp"), 1)
            act.dma_start(m_prompt[0, 0].rearrange("(h o) -> h o", o=1), g8[:, 2:3]).then_inc(sem("stored"), 16)
            n_stored += 1


            def job_out(n):
                act.wait_ge(sem("jobs_in"), len(JOBS) + n + 1)
                name, t, half = JOBS1[n]
                cols = slice(512 * half, 512 * half + 512)
                dst = ts1[name][:, cols] if t == 2 else tk1[name][:, t, cols]
                A(dst, bank[4 + n % 4][0:dst.shape[0], :], ACT.Copy).then_inc(sem("jobs_out"), 1)


            for j in range(8):
                if j >= 1:
                    split_hi(U_IN1 + 30 + j)
                    job_out(2 * j - 2)
                    job_out(2 * j - 1)
            act.wait_ge(sem("evac1_done"), 36)
            A(z1[:, 24:32, :], z1[:, 24:32, :], ACT.Sigmoid).then_inc(sem("gate_act"), 1)
            act.wait_ge(sem("small_in"), 1)
            A(acol[:].rearrange("p a b -> p (a b)"), bank[7][:, 0:16], ACT.Copy).then_inc(sem("small_out"), 1)
            act.wait_ge(sem("small_out"), 2)
            act.dma_start(m_sample[0], s8[:, 11, :]).then_inc(sem("stored"), 16)
            n_stored += 1


            def v_mask(b):
                if b == 0:
                    act.wait_ge(sem("v_weighted"), 1)
                if b >= 2:
                    act.wait_ge(sem("outer"), 2 * (b - 2) + 2)
                A(vm[b % 2][:], ts1["v"][:], ACT.Copy, scale=eye8[:, b:b + 1]).then_inc(sem("v_masked"), 1)


            def head_out(h):
                b = bank[h % 2]
                act.wait_ge(sem("num_in"), h + 1)
                A(z1[:, 16 + h, 0:TP], b[:, 0:TP], ACT.Copy).then_inc(sem("head_out"), 1)
                A(z1[:, h, 0:TP], b[:, 0:TP], ACT.Square).then_inc(sem("head_sq"), 1)
                A(tk1["k"][:, 0, DC * h:DC * h + DC], b[:, 256:384], ACT.Copy).then_inc(sem("head_out"), 1)
                A(ncol[:, h:h + 1], b[:, 384:385], ACT.Copy).then_inc(sem("head_out"), 1)


            for h in range(H + 1):
                if h < H:
                    act.wait_ge(sem("e_arg"), 2 * h + 2)
                    A(ew[h % 2][:], ew[h % 2][:], ACT.Exp, scale=-1.0).then_inc(sem("e_done"), 1)
                    v_mask(h)
                    act.wait_ge(sem("e_done"), h + 1)
                    for t, c in ((0, 255), (1, 383)):
                        keys = tk1["k"][:, t, DC * h:DC * h + DC]
                        A(keys, keys, ACT.Copy, scale=ew[h % 2][:, c:c + 1]).then_inc(sem("k_weighted"), 1)
                if h >= 1:
                    head_out(h - 1)
            act.wait_ge(sem("head_out"), 3 * H)
            act.dma_start(C_prompt[0, 0].rearrange("h e d -> e h d"), tk1["k"][:, 0, :].rearrange("p (h d) -> p h d", h=H)
                          ).then_inc(sem("stored"), 16)
            act.wait_ge(sem("n_step"), 3)
            act.dma_start(n_sample[0].rearrange("b h d -> b (h d)"), ts1["n"][:]).then_inc(sem("stored"), 16)
            act.wait_ge(sem("turned"), 1)
            A(R_A[:, 0:DC], bank[3][0:H, 0:DC], ACT.Copy).then_inc(sem("n_row"), 1)
            act.wait_ge(sem("n_row"), 1)
            act.dma_start(n_prompt[0, 0], R_A[:, 0:DC]).then_inc(sem("stored"), 16)
            n_stored += 3
            act.wait_ge(sem("num_in"), H)
            A(R_D[:, 0:TP], bank[7][0:H, 0:TP], ACT.Abs).then_inc(sem("den_in"), 1)
            act.wait_ge(sem("turned"), 2)
            A(R_D[:, TP:T], bank[2][0:H, 0:NB], ACT.Abs).then_inc(sem("den_in"), 1)
            act.wait_ge(sem("num_sample"), NB)
            A(z1[:, 0:8, TP:T], z1[:, 16:24, TP:T], ACT.Square).then_inc(sem("head_sq"), 1)
            rsqrt_seed("h1", 1, R_I, R_T, R_B)
            for h in range(H):
                act.wait_ge(sem("mix1"), h + 1)
                A(actA[0][:, h, :], z1[:, 8 + h, :], ACT.Copy).then_inc(sem("mix1_hi"), 1)
            act.wait_ge(sem("stored"), 16 * n_stored)
            for c in range(CRING):
                act.wait_ge(sem(f"c_stored{c}"), 16 * ((NB - 1 - c) // CRING + 1))
            for n in range(8):
                split_hi(U_OUT1 + n + LOOK + 1)
                norm_in(3, n, G_FFN + 8, actB)
            ffn_act(1, 3, U_UP1, U_DN1, None, None)
            n_stored += 3
            rsqrt_seed("rms", 5, var[:], nwt[:], rstd[:])
            for t in range(3):
                rows_t = NB if t == 2 else P
                dst = y_sample.rearrange("b o n -> (b o) n") if t == 2 else y_prompt[0, P * t:P * t + P]
                for half in range(2):
                    act.wait_ge(sem("x_t"), KT + 2 * t + half + 1)
                    A(y_rows[t][0:rows_t, 512 * half:512 * half + 512], bank[2 * t + half][0:rows_t, :], ACT.Copy).then_inc(sem("y_out"), 1)
                act.wait_ge(sem("y_out"), 2 * t + 2)
                act.dma_start(dst, y_rows[t][0:rows_t, :]).then_inc(sem("stored"), 16)
            n_stored += 3
            act.wait_ge(sem("stored"), 16 * n_stored)
            act.wait_ge(sem("row_stored"), 32)

        @block.vector
        def _(dve):
            V = nc.vector
            own = [0]

            def step(ins):
                ins.then_inc(sem("dve_step"), 1)
                own[0] += 1
                dve.wait_ge(sem("dve_step"), own[0])

            def split_lo(u, i8=0):
                if u >= U_END:
                    return
                dve.wait_ge(sem("hi_ready"), u + 1 + i8)
                nk = row_tiles(u)[1]
                V.tensor_tensor(wlo[u % RING][:, 0:nk, :], raw[u // 2 % RING][:, 0:nk, P * (u % 2):P * (u % 2) + P],
                                whi[u % RING][:, 0:nk, :].bitcast(F32), ALU.subtract).then_inc(sem("lo_ready"), 1)

            def norm_lo(stage, k, g, dst, i=0):
                dve.wait_ge(sem("norm_hi"), 8 * stage + k + 1 + i)
                V.scalar_tensor_tensor(dst[1][:, bass.ds(i + k, 1), :], x[:, bass.ds(i + k, 1), :],
                                       gains[:, bass.ds(g + k + i, 1)], dst[0][:, bass.ds(i + k, 1), :].bitcast(F32),
                                       ALU.mult, ALU.subtract).then_inc(sem("norm_lo"), 1)

            def newton(name, n, v, t, y):
                dve.wait_ge(sem(f"{name}_seed"), n)
                step(V.scalar_tensor_tensor(t, y, -0.5, y, ALU.mult, ALU.mult))
                step(V.tensor_tensor(t, t, v, ALU.mult))
                step(V.scalar_tensor_tensor(y, t, 1.5, y, ALU.add, ALU.mult))

            def rms(stage):
                dve.wait_ge(sem("ss_done"), stage + 1)
                V.tensor_scalar(var[:], bank[7][:, 0:T], 1.0 / D, EPS, ALU.mult, ALU.add).then_inc(sem("rms_var"), 1)
                dve.wait_ge(sem("rms_var"), stage + 1)
                newton("rms", stage + 1, var[:], nwt[:], rstd[:])

            for k in range(KT):
                dve.wait_ge(sem("x_t"), k + 1)
                V.tensor_copy(x[:, k, :], bank[k % 4][:, 0:T]).then_inc(sem("x_ready"), 1)
                if k >= 1:
                    norm_lo(0, k - 1, G_AB, actA)
            norm_lo(0, 7, G_AB, actA)
            split_lo(0)
            split_lo(1)
            split_lo(2)
            rms(0)

            dve.wait_ge(sem("const_landed"), 32)

            def rope(u):
                r = ROPED.index(u)
                dve.wait_ge(sem("swapped"), r + 1)
                V.scalar_tensor_tensor(smx[r % 2][:, 0:T], bank[4 + r % 2][:, 0:T], 1.0, sin, ALU.mult, ALU.mult
                                       ).then_inc(sem("sin_prod"), 1)
                dve.wait_ge(sem("sin_prod"), r + 1)
                dve.wait_ge(sem("cos_prod"), r + 1)
                V.tensor_tensor(z0[:, u, :], smx[r % 2][:, 0:T], rmk[r % 2][:, 0:T], ALU.add).then_inc(sem("roped"), 1)

            def k_sum(j):
                dve.wait_ge(sem("k_mult"), j + 1)
                V.tensor_reduce(sc_all[:, 2 * (j % 4):2 * (j % 4) + 2, j // 4, :],
                                kv[j % 4][:].rearrange("p t (h d) -> p t h d", h=H), AX, ALU.add).then_inc(sem("k_reduced"), 1)

            for u in range(28):
                split_lo(u + LOOK)
                dve.wait_ge(sem("mm_done"), u + 1)
                V.scalar_tensor_tensor(z0[:, u, :], bank[u % RING][:, 0:T], DA ** -0.5 if 16 <= u < 20 else 1.0, rstd[:],
                                       ALU.mult, ALU.mult).then_inc(sem("evac_done"), 1)
                if u - 1 in ROPED:
                    rope(u - 1)
                if u >= 10:
                    k_sum(u - 10)

            def attn_max(h):
                s = h % 2
                dve.wait_ge(sem("attn_s"), h + 1)
                if h >= 2:
                    dve.wait_ge(sem("attn_pt"), h - 1)
                V.tensor_tensor(smx[s][:], bank[4 + s][:, 0:384], cst[:, C_AMASK:C_AMASK + 384], ALU.add
                                ).then_inc(sem("attn_masked"), 1)
                dve.wait_ge(sem("attn_masked"), h + 1)
                V.tensor_reduce(sm[:, 0:1], smx[s][:, 0:128], AX, ALU.max)
                step(V.tensor_reduce(sm[:, 1:2], smx[s][:, 128:384], AX, ALU.max))
                V.tensor_scalar(sm[:, 4 + 2 * s:6 + 2 * s], sm[:, 0:2], -DA ** -0.5, None, ALU.mult).then_inc(sem("attn_nmax"), 1)

            def attn_norm(h):
                s = h % 2
                dve.wait_ge(sem("attn_exp"), 2 * h + 2)
                step(V.reciprocal(sm[:, 2:4], sm[:, 8 + 2 * s:10 + 2 * s]))
                for t, (a, b) in enumerate(((0, 128), (128, 384))):
                    V.tensor_scalar(smx[s][:, a:b], smx[s][:, a:b], sm[:, 2 + t:3 + t], None, ALU.mult).then_inc(sem("attn_p"), 1)

            def attn_lo(c):
                dve.wait_ge(sem("attn_hi"), c + 1)
                V.tensor_tensor(actA[1][:, c, 0:TP], bank[c % 2][:, 0:TP], actA[0][:, c, 0:TP].bitcast(F32),
                                ALU.subtract).then_inc(sem("attn_lo"), 1)

            for h in range(H):
                attn_max(h)
                if h >= 1:
                    attn_norm(h - 1)
                if h >= 3 and h % 2:
                    attn_lo((h - 3) // 2)
                k_sum(18 + h)
            attn_norm(H - 1)
            attn_lo(3)

            for j in range(26, 32):
                k_sum(j)

            def ret_weights(h):
                dve.wait_ge(sem("ret_s"), h + 1)
                dve.wait_ge(sem("ret_mask"), h + 1)
                if h >= 2:
                    dve.wait_ge(sem("ret_pv"), h - 1)
                V.tensor_tensor(ptt[h % 2][:], bank[4 + h % 2][:, 0:384], rmk[h % 2][:], ALU.mult).then_inc(sem("ret_masked"), 1)

            step(V.tensor_tensor(prd, tks["qa"][:], tks["ka"][:], ALU.mult))
            step(V.tensor_reduce(sm[0:NB, 70:78], prd.rearrange("p (h d) -> p h d", h=H), AX, ALU.add))
            V.tensor_tensor(dgs[:], eye8.unsqueeze(2).to_broadcast([NB, NB, H]),
                            sm[0:NB, 70:78].unsqueeze(1).to_broadcast([NB, NB, H]), ALU.mult).then_inc(sem("own_diag"), 1)
            dve.wait_ge(sem("samp_rows"), 2)
            blocks = prow.rearrange("p (n k) -> p n k", n=NBLK)
            gate = sm[0:64, 12:16]
            V.tensor_reduce(sm[0:64, 16:20], blocks, AX, ALU.max)
            step(V.tensor_reduce(gate, blocks, AX, ALU.add))
            dve.wait_ge(sem("own_s"), 1)
            V.tensor_copy(sm[0:64, 68:69], bank[7][0:64, 0:1]).then_inc(sem("own_in"), 1)
            for n in range(NBLK):
                if n:
                    V.tensor_scalar(sm[0:64, 40 + 4 * n:40 + 5 * n], gate[:, 0:n], gate[:, n:n + 1], None, ALU.is_ge)
                last = V.tensor_scalar(sm[0:64, 40 + 5 * n:44 + 4 * n], gate[:, n:NBLK], gate[:, n:n + 1], None, ALU.is_gt)
            step(last)
            step(V.tensor_reduce(sm[0:64, 56:60], sm[0:64, 40:56].rearrange("p (n m) -> p n m", n=NBLK), AX, ALU.add))
            step(V.tensor_scalar(sm[0:64, 60:64], sm[0:64, 56:60], TOPK - 0.5, -BIG, ALU.is_gt, ALU.mult))
            dve.wait_ge(sem("own_in"), 1)
            step(V.tensor_tensor(sm[0:64, 64:68], sm[0:64, 60:64], sm[0:64, 16:20], ALU.add))
            step(V.tensor_reduce(sm[0:64, 69:70], sm[0:64, 64:69], AX, ALU.max))
            step(V.tensor_scalar(sm[0:64, 28:29], sm[0:64, 69:70], -DA ** -0.5, None, ALU.mult))
            V.tensor_scalar(sm[0:64, 24:28], sm[0:64, 60:64], sm[0:64, 28:29], None, ALU.add).then_inc(sem("samp_bias"), 1)
            ret_weights(0)
            ret_weights(1)
            dve.wait_ge(sem("samp_exp"), 5)
            step(V.tensor_reduce(sm[0:64, 37:38], sm[0:64, 32:37], AX, ALU.add))
            step(V.reciprocal(sm[0:64, 38:39], sm[0:64, 37:38]))
            V.tensor_scalar(sm[0:64, 39:40], sm[0:64, 36:37], sm[0:64, 38:39], None, ALU.mult).then_inc(sem("samp_p"), 1)
            V.tensor_scalar(prow, prow, sm[0:64, 38:39], None, ALU.mult).then_inc(sem("samp_p"), 1)
            dve.wait_ge(sem("own_s"), 2)
            V.tensor_tensor(dgp[:], bank[7][0:NB, 0:64].rearrange("p (b h) -> p b h", b=NB),
                            eye8.unsqueeze(2).to_broadcast([NB, NB, H]), ALU.mult).then_inc(sem("own_p_diag"), 1)
            for t in range(2):
                V.tensor_tensor(kdec[:, t, :].rearrange("p (h d) -> p h d", h=H), tok["kb"][:, t, :].rearrange("p (h d) -> p h d", h=H),
                                cst[:, C_RDEC + 8 * t:C_RDEC + 8 * t + 8].unsqueeze(2).to_broadcast([P, H, DA]),
                                ALU.mult).then_inc(sem("k_decayed"), 1)
            for h in range(2, H):
                ret_weights(h)
            dve.wait_ge(sem("s0_landed"), 16 * NB)
            for c in range(4):
                dve.wait_ge(sem("kv_outer"), 2 * c + 2)
                V.scalar_tensor_tensor(s0[:, c, :, :].rearrange("p b e -> p (b e)"), s0[:, c, :, :].rearrange("p b e -> p (b e)"),
                                       cst[:, C_GAM + c:C_GAM + c + 1], bank[c][:, :], ALU.mult, ALU.add).then_inc(sem("s_new"), 1)
            dve.wait_ge(sem("ret_o"), 2)
            for q in range(2):
                V.tensor_copy(z0[64 * q:64 * q + 64, 8:12, TP:T],
                              bank[4 + q][64 * q:64 * q + 64, 0:32].rearrange("p (c b) -> p c b", c=4)).then_inc(sem("ob_sample"), 1)
            for c in range(4):
                dve.wait_ge(sem("ret_ss"), c + 1)
                V.tensor_scalar(z0[:, 4 + c, :], bank[c][:, 0:T], 1.0 / DA, EPS, ALU.mult, ALU.add).then_inc(sem("ret_var"), 1)
            dve.wait_ge(sem("ret_var"), 4)
            newton("ret", 1, z0[:, 4:8, :], z0[:, 0:4, :], z0[:, 20:24, :])
            dve.wait_ge(sem("ob_gated"), 1)
            for c in range(4):
                V.scalar_tensor_tensor(z0[:, c, :], z0[:, 24 + c, :], gains[:, G_RET + c:G_RET + c + 1], z0[:, 20 + c, :],
                                       ALU.mult, ALU.mult).then_inc(sem("ret_mix"), 1)
            for c in range(4):
                dve.wait_ge(sem("ret_hi"), c + 1)
                V.tensor_tensor(actA[1][:, 4 + c, :], z0[:, c, :], actA[0][:, 4 + c, :].bitcast(F32), ALU.subtract
                                ).then_inc(sem("mix_lo"), 1)
            dve.wait_ge(sem("v_used"), 32)
            for t in range(2):
                V.tensor_tensor(ovv[:, t, :].rearrange("p (h d) -> p h d", h=H), bank[6 + t][:, :].rearrange("p (h d) -> p h d", h=H),
                                cst[:, C_HMASK:C_HMASK + 8].unsqueeze(2).to_broadcast([P, H, DA]), ALU.mult).then_inc(sem("samp_own"), 1)
            dve.wait_ge(sem("samp_hi"), 1)
            V.tensor_tensor(actA[1][:, 0:4, TP:T], bank[5][:, 0:32].rearrange("p (c b) -> p c b", c=4),
                            actA[0][:, 0:4, TP:T].bitcast(F32), ALU.subtract).then_inc(sem("mix_lo"), 1)

            def residual(stage, e, d, g, dst, i=0):
                V.tensor_tensor(x[:, bass.ds(d + i, 1), :], x[:, bass.ds(d + i, 1), :], bank[e % RING][:, 0:T].unsqueeze(1),
                                ALU.add).then_inc(sem("x_ready"), 1)

            def out_proj(stage, u0, e0, g, dst):
                for n in range(8):
                    split_lo(u0 + n + LOOK)
                    dve.wait_ge(sem("mm_done"), u0 + n + 1)
                    residual(stage, e0 + n, n, g, dst)
                    if n >= 1:
                        norm_lo(stage, n - 1, g, dst)
                norm_lo(stage, 7, g, dst)

            out_proj(1, U_OUT0, E_OUT0, G_FFN, actB)

            def ffn_dve(l, stage, u_up, u_dn, e_up, e_dn, g_next, dst_next):
                rms(stage)
                w = [convp[l][:, j, :].unsqueeze(1).to_broadcast([P, NB, FT]) for j in range(4)]
                step(V.tensor_tensor(ffp[:], convb[l][:, :, 0, :], w[0], ALU.mult))
                step(V.tensor_tensor(ffq[:], convb[l][:, :, 1, :], w[1], ALU.mult))
                step(V.tensor_tensor(ffp[:], ffp[:], ffq[:], ALU.add))
                step(V.tensor_tensor(ffp[:], ffp[:], w[3], ALU.add))

                def scaled(u, dst, name, i8, f=None, i4=0):
                    dve.wait_ge(sem("mm_done"), u + 1 + i8)
                    V.tensor_tensor(dst, bank[(u - u_up + e_up) % RING][:, 0:T], rstd[:], ALU.mult).then_inc(sem(name), 1)

                def conv(f, i4, fd):
                    a, t = ffa[f % 4], fft[f % 4]
                    w1, w2 = (convp[l][:, j, bass.ds(fd, 1)] for j in (1, 2))
                    dve.wait_ge(sem("a_ready"), f + 1 + i4 + FT * l)
                    dve.wait_ge(sem("tap"), f + 1 + i4 + FT * l)
                    V.scalar_tensor_tensor(t[:, TP:T], a[:, 2 + TP:2 + T], w2, ffp[:, :, bass.ds(fd, 1)].rearrange("p b o -> p (b o)"),
                                           ALU.mult, ALU.add)
                    V.scalar_tensor_tensor(t[:, 0:TP], a[:, 1:1 + TP], w1, t[:, 0:TP], ALU.mult, ALU.add).then_inc(sem("tap1"), 1)
                    dve.wait_ge(sem("tap1"), f + 1 + i4 + FT * l)
                    V.scalar_tensor_tensor(t[:, 0:TP], a[:, 2:2 + TP], w2, t[:, 0:TP], ALU.mult, ALU.add).then_inc(sem("conv"), 1)

                def h_lo(f, i4, fd):
                    dve.wait_ge(sem("h_hi"), f + 1 + i4 + FT * l)
                    V.tensor_tensor(hff[1][:, bass.ds(fd, 1), :], ffg[f % 4][:].unsqueeze(1), hff[0][:, bass.ds(fd, 1), :].bitcast(F32),
                                    ALU.subtract).then_inc(sem("h_lo"), 1)

                def group(f, u, i4, i8, fd, first=0):
                    split_lo(u + LOOK, i8)
                    if first < 1:
                        dve.wait_ge(sem("a_kept"), f - 2 + i4 + FT * l)
                    scaled(u, ffa[f % 4][:, 2:2 + T], "a_ready", i8)
                    split_lo(u + LOOK + 1, i8)
                    scaled(u + 1, ffa[(f + 1) % 4][:, 2:2 + T], "a_ready", i8)
                    conv(f, i4, fd)
                    split_lo(u + LOOK + 2, i8)
                    scaled(u + 2, ffg[f % 4][:], "g_ready", i8)
                    conv(f + 1, i4, fd + 1)
                    if first < 2:
                        h_lo(f - 2, i4, fd - 2)
                    split_lo(u + LOOK + 3, i8)
                    scaled(u + 3, ffg[(f + 1) % 4][:], "g_ready", i8)
                    if first < 2:
                        h_lo(f - 1, i4, fd - 1)

                group(0, u_up, 0, 0, 0, 2)
                with dve.Fori(0, 5) as i:
                    group(2, u_up + 4, i * 4, i * 8, i * 4 + 2)
                    group(4, u_up + 8, i * 4, i * 8, i * 4 + 4)

                for c in range(4):
                    for j in range(8):
                        split_lo(u_dn + 8 * c + j + LOOK)
                        if c == 0 and j == 1:
                            h_lo(FT - 2, 0, FT - 2)
                            h_lo(FT - 1, 0, FT - 1)
                        if j >= 6:
                            dve.wait_ge(sem("mm_done"), u_dn + 8 * c + j + 1)
                            residual(stage + 1, e_dn + 2 * c + j - 6, 2 * c + j - 6, g_next, dst_next)
                            if g_next is not None and 2 * c + j - 6 >= 1:
                                norm_lo(stage + 1, 2 * c + j - 7, g_next, dst_next)
                if g_next is not None:
                    norm_lo(stage + 1, 7, g_next, dst_next)

            ffn_dve(0, 1, U_UP0, U_DN0, E_UP0, E_DN0, G_C, actA)
            dve.wait_ge(sem("c_small"), 64)
            V.memset(qkv_scale[:, 0:3:2], 1.0)
            V.memset(qkv_scale[:, 1:2], DC ** -0.5).then_inc(sem("evac1_done"), 2)
            rms(2)
            split_lo(U_IN1 + 3)
            split_lo(U_IN1 + 4)
            for t, r in ((0, R_I), (1, R_F)):
                dve.wait_ge(sem("mm_done"), U_IN1 + t + 1)
                V.tensor_tensor(r, bank[(E_IN1 + t) % RING][0:H, 0:T], rstd[0:H, :], ALU.mult).then_inc(sem("evac1_done"), 1)
            dve.wait_ge(sem("evac1_done"), 4)
            for t, r in ((0, R_I), (1, R_F)):
                V.tensor_scalar(r, r, g8[:, t:t + 1], None, ALU.add).then_inc(sem("gates_in"), 2)


            def in1(e, c, scale, i8=0):
                dve.wait_ge(sem("mm_done"), U_IN1 + e + 1 + i8)
                V.scalar_tensor_tensor(z1[:, bass.ds(c, 1), :], bank[(E_IN1 + e) % RING][:, 0:T].unsqueeze(1), scale,
                                       rstd[:].unsqueeze(1), ALU.mult, ALU.mult).then_inc(sem("evac1_done"), 1)


            with dve.Fori(0, 3) as i:
                for j in range(8):
                    split_lo(U_IN1 + 5 + j, i * 8)
                    in1(2 + j, i * 8 + j, qkv_scale[:, bass.ds(i, 1)], i * 8)
            dve.wait_ge(sem("gates_in"), 4)
            dve.wait_ge(sem("ls"), 3)
            step(V.scalar_tensor_tensor(R_T, R_F, 0.0, R_T, ALU.min, ALU.subtract))
            step(V.tensor_tensor(s8[:, 1, :], R_T[:, TP:T], s8[:, 0, :], ALU.add))
            step(V.tensor_tensor(s8[:, 7, :], s8[:, 1, :], R_I[:, TP:T], ALU.max))
            V.tensor_tensor(s8[:, 2, :], R_I[:, TP:T], s8[:, 7, :], ALU.subtract)
            V.tensor_scalar(s8[:, 3, :], s8[:, 7, :], -1.0, EXP_MAX, ALU.mult, ALU.min)
            V.tensor_tensor(s8[:, 1, :], s8[:, 1, :], s8[:, 7, :], ALU.subtract).then_inc(sem("s_gates"), 1)
            split_lo(U_IN1 + 29)
            one_row = ones[0:H, 0:1].to_broadcast([H, TP])
            step(V.tensor_tensor_scan(R_B[:, 0:TP], one_row, R_T[:, 0:TP], 0.0, ALU.mult, ALU.add))
            step(V.tensor_tensor(R_A[:, 0:TP], R_I[:, 0:TP], R_B[:, 0:TP], ALU.subtract))
            step(V.tensor_tensor_scan(R_M[:, 0:TP], one_row, R_A[:, 0:TP], 0.0, ALU.mult, ALU.max))
            step(V.tensor_tensor(R_B[:, 0:TP], R_B[:, 0:TP], R_M[:, 0:TP], ALU.add))
            V.tensor_copy(g8[:, 2:3], R_B[:, TP - 1:TP])
            V.tensor_scalar(R_E[:, 0:TP], R_B[:, 0:TP], -EXP_MAX, None, ALU.max).then_inc(sem("m_ready"), 1)
            for j in range(8):
                if j:
                    split_lo(U_IN1 + 29 + j)
                in1(26 + j, 24 + j, 1.0)
            dve.wait_ge(sem("small_in"), 2)
            V.tensor_copy(s8[:, 8:12, :].rearrange("p a b -> p (a b)"), bank[7][0:NB, 0:32]).then_inc(sem("small_out"), 1)
            dve.wait_ge(sem("small_out"), 2)
            V.tensor_tensor(dd[:], eye8.unsqueeze(2).to_broadcast([NB, NB, H]), s8[:, 8, :].unsqueeze(1).to_broadcast([NB, NB, H]),
                            ALU.mult).then_inc(sem("dec_diag"), 1)
            dve.wait_ge(sem("small_in"), 3)
            V.tensor_copy(decb[:].rearrange("p b h -> p (b h)"), bank[7][:, 0:64]).then_inc(sem("small_out"), 1)
            dve.wait_ge(sem("small_out"), 1)


            def head_exponent(h):
                dve.wait_ge(sem("m_b"), h + 1)
                if h >= 2:
                    dve.wait_ge(sem("k_weighted"), 2 * (h - 2) + 2)
                e, mb = ew[h % 2], bank[3]
                V.scalar_tensor_tensor(e[:, 0:256], mb[:, 0:256], acol[:, 0, h:h + 1], cst[:, C_MMASK:C_MMASK + 256],
                                       ALU.subtract, ALU.max).then_inc(sem("e_arg"), 1)
                V.scalar_tensor_tensor(e[:, 256:384], mb[:, 128:256], acol[:, 1, h:h + 1], cst[:, C_MMASK + 256:C_MMASK + 384],
                                       ALU.subtract, ALU.max).then_inc(sem("e_arg"), 1)


            def head_weights(h):
                dve.wait_ge(sem("m_s"), h + 1)
                dve.wait_ge(sem("e_done"), h + 1)
                if h >= 2:
                    dve.wait_ge(sem("num_in"), h - 1)
                V.tensor_tensor(ww[h % 2], bank[2][:, 0:384], ew[h % 2][:], ALU.mult).then_inc(sem("w_ready"), 1)


            def c_update(b):
                c = cs[b % CRING][:].rearrange("p h d -> p (h d)")
                dve.wait_ge(sem("c_decayed"), b + 1)
                for half in range(2):
                    cols = slice(512 * half, 512 * half + 512)
                    dve.wait_ge(sem("outer"), 2 * b + half + 1)
                    V.tensor_tensor(c[:, cols], c[:, cols], bank[4 + half][:, :], ALU.add).then_inc(sem("c_added"), 1)
                for half in range(2):
                    cols = slice(512 * half, 512 * half + 512)
                    dve.wait_ge(sem("q_b"), 2 * b + half + 1)
                    dve.wait_ge(sem("c_added"), 2 * b + half + 1)
                    if b >= 1:
                        dve.wait_ge(sem("num_sample"), b)
                    V.tensor_tensor(prod[:, cols], c[:, cols], bank[6][:, :], ALU.mult).then_inc(sem("q_mult"), 1)
                dve.wait_ge(sem("q_mult"), 2 * b + 2)
                V.tensor_reduce(z1[:, 16:24, TP + b], prod[:].rearrange("p (h d) -> p h d", h=H), AX, ALU.add).then_inc(sem("num_sample"), 1)


            head_exponent(0)
            for h in range(H):
                head_weights(h)
                if h + 1 < H:
                    head_exponent(h + 1)
                if h == 0:
                    dve.wait_ge(sem("n_step"), 4)
                    V.tensor_reduce(s8[:, 12, :], prod[0:NB, :].rearrange("p (h d) -> p h d", h=H), AX, ALU.add).then_inc(sem("den_sample"), 1)
                    dve.wait_ge(sem("den_sample"), 1)
                c_update(h)
            dve.wait_ge(sem("den_in"), 2)
            step(V.tensor_tensor(R_D, R_D, R_E, ALU.max))
            step(V.scalar_tensor_tensor(R_D, R_D, EPS, R_D, ALU.mult, ALU.mult))
            dve.wait_ge(sem("head_ss"), 1)
            V.scalar_tensor_tensor(R_I, bank[4][0:H, 0:T], 1.0 / DC, R_D, ALU.mult, ALU.add).then_inc(sem("h1_var"), 1)
            newton("h1", 1, R_I, R_T, R_B)
            V.tensor_copy(R_M, R_B).then_inc(sem("h1_rstd"), 1)


            def mix_lo(h):
                dve.wait_ge(sem("mix1_hi"), h + 1)
                V.tensor_tensor(actA[1][:, h, :], z1[:, 8 + h, :], actA[0][:, h, :].bitcast(F32), ALU.subtract).then_inc(sem("mix1_lo"), 1)


            for h in range(H):
                dve.wait_ge(sem("rstd_b"), h + 1)
                dve.wait_ge(sem("o1_gated"), h // 4 + 1)
                V.scalar_tensor_tensor(z1[:, 8 + h, :], z1[:, 24 + h, :], gains[:, G_OUT + h:G_OUT + h + 1], bank[h % 4][:, 0:T],
                                       ALU.mult, ALU.mult).then_inc(sem("mix1"), 1)
                if h:
                    mix_lo(h - 1)
            mix_lo(H - 1)
            out_proj(3, U_OUT1, E_OUT1, G_FFN + 8, actB)
            ffn_dve(1, 3, U_UP1, U_DN1, E_UP1, E_DN1, None, None)
            rms(4)
            for k in range(KT):
                V.scalar_tensor_tensor(sq[:, k, :], x[:, k, :], gains[:, G_FIN + k:G_FIN + k + 1], rstd[:], ALU.mult, ALU.mult
                                       ).then_inc(sem("y_scaled"), 1)
        @block.tensor
        def _(pe):
            M = nc.tensor.matmul
            TR = nc.tensor.transpose
            last_reader = {}

            def claim(b, name, value):
                if b in last_reader:
                    pe.wait_ge(*last_reader[b])
                last_reader[b] = (sem(name), value)

            def unit(u, b, src, k0=0, nk=8, first=True, last=True, i8=0):
                pe.wait_ge(sem("lo_ready"), u + 1 + i8)
                hi, lo = whi[u % RING], wlo[u % RING]
                for k in range(nk):
                    M(bank[b][:, 0:T], hi[:, k, :], src[0][:, k0 + k, :], start=first and k == 0, stop=False)
                    M(bank[b][:, 0:T], hi[:, k, :], src[1][:, k0 + k, :], start=False, stop=False)
                    ins = M(bank[b][:, 0:T], lo[:, k, :], src[0][:, k0 + k, :], start=False, stop=last and k == nk - 1)
                ins.then_inc(sem("mm_done"), 1)

            def sum_squares(stage):
                claim(7, "rms_var", stage + 1)
                for k in range(KT):
                    pe.wait_ge(sem("sq_ready"), 8 * stage + k + 1)
                    ins = M(bank[7][:, 0:T], ones[:], sq[:, k, :], start=k == 0, stop=k == KT - 1)
                ins.then_inc(sem("ss_done"), 1)

            pe.wait_ge(sem("const_landed"), 16)
            pe.wait_ge(sem("x_landed"), 16 * 9)
            claim(4, "param_out", 1)
            TR(bank[4][:, 0:52], vec_rows, ident[0:52, 0:52]).then_inc(sem("param_t"), 1)
            for k in range(KT):
                claim(k % 4, "x_ready", k + 1)
                for t in range(2):
                    TR(bank[k % 4][:, P * t:P * t + P], x_tok[:, t, P * k:P * k + P], ident)
                TR(bank[k % 4][:, TP:T], xs_tok[:, P * k:P * k + P], ident[0:NB, 0:NB]).then_inc(sem("x_t"), 1)
            pe.wait_ge(sem("ones_ready"), 1)
            sum_squares(0)
            pe.wait_ge(sem("norm_lo"), 8)

            def job(n):
                claim(6 + n % 2, "jobs_out", n + 1)
                b, what = bank[6 + n % 2], JOBS[n]
                if what[0] == "b":
                    pe.wait_ge(sem("jobs_out"), 1)
                    M(b[:, :], eye8[:, what[1]:what[1] + 1].to_broadcast([NB, P]), tks["qa"][:], start=True, stop=True
                      ).then_inc(sem("jobs_in"), 1)
                    return
                name, t = what[1:]
                if TILE0[name] + 3 in ROPED:
                    pe.wait_ge(sem("roped"), ROPED.index(TILE0[name] + 3) + 1)
                else:
                    pe.wait_ge(sem("evac_done"), TILE0[name] + 4)
                for c in range(4):
                    if t < 2:
                        ins = TR(b[:, P * c:P * c + P], zt(name, c, P * t, P * t + P), ident)
                    else:
                        ins = TR(b[0:NB, P * c:P * c + P], zt(name, c, TP, T), ident)
                ins.then_inc(sem("jobs_in"), 1)

            for u in range(28):
                claim(u % RING, "evac_done", u + 1)
                unit(u, u % RING, actA)
                if u == 0:
                    pe.wait_ge(sem("param_landed"), 16 * 12)
                    claim(4, "param_out", 3)
                    for l in range(2):
                        ins = TR(bank[4][:, 64 + 96 * l:152 + 96 * l], cw_rows[l], ident[0:88, 0:88])
                    ins.then_inc(sem("param_t"), 1)
                    for l in range(2):
                        claim(5 + l, "param_out", 4 + l)
                        for q in range(4):
                            ins = TR(bank[5 + l][:, 88 * q:88 * q + 88], cb_rows[l][:, q, :], ident[0:88, 0:88])
                        ins.then_inc(sem("param_t"), 1)
                if u - 1 in ROPED:
                    r = ROPED.index(u - 1)
                    claim(4 + r % 2, "sin_prod", r + 1)
                    pe.wait_ge(sem("evac_done"), u)
                    M(bank[4 + r % 2][:, 0:T], perm, z0[:, u - 1, :], start=True, stop=True).then_inc(sem("swapped"), 1)
                for n in range(jobs_until(u - 1), jobs_until(u)):
                    job(n)

            def attn_s(h):
                c, r = h // 2, 64 * (h % 2)
                claim(4 + h % 2, "attn_masked", h + 1)
                q, k = z0[r:r + 64, c, :], z0[r:r + 64, 4 + c, :]
                M(bank[4 + h % 2][:, 0:128], q[:, 0:128], k[:, 0:128], start=True, stop=True)
                M(bank[4 + h % 2][:, 128:384], q[:, 128:256], k[:, 0:256], start=True, stop=True).then_inc(sem("attn_s"), 1)

            def attn_p(h):
                claim(6 + h % 2, "attn_pt_out", h + 1)
                pe.wait_ge(sem("attn_p"), 2 * h + 2)
                for t in range(3):
                    ins = TR(bank[6 + h % 2][:, P * t:P * t + P], smx[h % 2][:, P * t:P * t + P], ident)
                ins.then_inc(sem("attn_pt"), 1)

            def causal_pv(out, v0, v1, p):
                M(out[:, 0:128], v0, p[:, 0:128], start=True, stop=True)
                M(out[:, 128:256], v0, p[:, 128:256], start=True, stop=False)
                return M(out[:, 128:256], v1, p[:, 256:384], start=False, stop=True)

            def attn_pv(h):
                c, r = h // 2, 64 * (h % 2)
                if h % 2 == 0:
                    claim(c % 2, "attn_lo", c + 1)
                pe.wait_ge(sem("attn_pt_out"), h + 1)
                v = tok["va"]
                causal_pv(bank[c % 2][r:r + 64, :], v[:, 0, DA * h:DA * h + DA], v[:, 1, DA * h:DA * h + DA], ptt[h % 2]
                          ).then_inc(sem("attn_pv"), 1)

            pe.wait_ge(sem("jobs_out"), len(JOBS))
            attn_s(0)
            for h in range(1, H + 1):
                if h < H:
                    attn_s(h)
                if h >= 2:
                    attn_pv(h - 2)
                attn_p(h - 1)
            attn_pv(H - 1)

            def ret_s(h):
                c, r = h // 2, 64 * (h % 2)
                claim(4 + h % 2, "ret_masked", h + 1)
                q, k = zt("qb", c)[r:r + 64, :], zt("kb", c)[r:r + 64, :]
                M(bank[4 + h % 2][:, 0:256], k[:, 0:128], q[:, 0:256], start=True, stop=True)
                M(bank[4 + h % 2][:, 256:384], k[:, 128:256], q[:, 128:256], start=True, stop=True).then_inc(sem("ret_s"), 1)

            def ret_pv(h):
                c, r = h // 2, 64 * (h % 2)
                if h % 2 == 0:
                    claim(2 + c % 2, "ob_prompt", c + 1)
                pe.wait_ge(sem("ret_masked"), h + 1)
                v = tok["vb"]
                causal_pv(bank[2 + c % 2][r:r + 64, :], v[:, 0, DA * h:DA * h + DA], v[:, 1, DA * h:DA * h + DA], ptt[h % 2]
                          ).then_inc(sem("ret_pv"), 1)

            pe.wait_ge(sem("k_reduced"), 32)
            for t in range(2):
                claim(4 + t, "samp_rows", t + 1)
                for g in range(4):
                    ins = TR(bank[4 + t][0:64, P * g:P * g + P], sc_all[:, 4 * t + g, :, :].rearrange("p b h -> p (b h)"), ident)
                ins.then_inc(sem("samp_st"), 1)
            claim(7, "own_in", 1)
            pe.wait_ge(sem("own_diag"), 1)
            M(bank[7][0:64, 0:1], dgs[:].rearrange("p b h -> p (b h)"), ones[0:NB, 0:1], start=True, stop=True).then_inc(sem("own_s"), 1)
            ret_s(0)
            ret_s(1)
            claim(7, "own_p_diag", 1)
            pe.wait_ge(sem("samp_p"), 1)
            M(bank[7][0:NB, 0:64], sm[0:64, 39:40].to_broadcast([64, NB]), ident[0:64, 0:64], start=True, stop=True).then_inc(sem("own_s"), 1)
            claim(6, "samp_pt_out", 1)
            pe.wait_ge(sem("samp_p"), 2)
            for g in range(NPAGE):
                ins = TR(bank[6][:, 64 * g:64 * g + 64], prow[:, P * g:P * g + P], ident[0:64, 0:64])
            ins.then_inc(sem("samp_pt"), 1)

            def ret_state():
                claim(0, "ret_state_out", 1)
                pe.wait_ge(sem("k_decayed"), 2)
                for h in range(H):
                    for t in range(2):
                        ins = M(bank[0][0:64, DA * h:DA * h + DA], kdec[:, t, DA * h:DA * h + DA],
                                tok["vb"][:, t, DA * h:DA * h + DA], start=t == 0, stop=t == 1)
                ins.then_inc(sem("ret_state"), 1)

            def state_update(h):
                c, r = h // 2, 64 * (h % 2)
                if h % 2 == 0:
                    claim(c, "s_new", c + 1)
                pe.wait_ge(sem("v_diag"), h + 1)
                M(bank[c][r:r + 64, :], tks["kb"][:, DA * h:DA * h + DA], vdg[h % 2].rearrange("p b e -> p (b e)"),
                  start=True, stop=True).then_inc(sem("kv_outer"), 1)

            def ret_o(q):
                pe.wait_ge(sem("s_new"), 4)
                claim(4 + q, "ob_sample", q + 1)
                r = slice(64 * q, 64 * q + 64)
                for c in range(4):
                    for b in range(NB):
                        ins = M(bank[4 + q][r, 8 * c + b:8 * c + b + 1], s0[r, c, b, :], zt("qb", c)[r, TP + b:TP + b + 1],
                                start=True, stop=True)
                ins.then_inc(sem("ret_o"), 1)

            def ret_squares(c):
                pe.wait_ge(sem("ret_sq"), 1)
                claim(c, "ret_var", c + 1)
                M(bank[c][:, 0:T], bones, z0[:, c, :], start=True, stop=True).then_inc(sem("ret_ss"), 1)

            claim(6, "samp_own", 1)
            claim(7, "samp_own", 2)
            pe.wait_ge(sem("own_p_diag"), 1)
            pe.wait_ge(sem("samp_pt_out"), 1)
            for j in range(32):
                b, r = j // 4, 32 * (j // 4 % 4)
                out = bank[6 + b // 4][r:r + H, :]
                if j % 4 == 0:
                    M(out, dgp[:, b, :], tks["va"][:], start=True, stop=False)
                pe.wait_ge(sem(f"kv_landed{j % 4}"), 32 * (8 + b + 1))
                for t in range(2):
                    g = 2 * (j % 4) + t
                    ins = M(out, pts[:, g, 8 * b:8 * b + 8], kv[j % 4][:, t, :], start=False, stop=g == NPAGE - 1)
                ins.then_inc(sem("v_used"), 1)
                if j < H:
                    ret_pv(j)
                    if j + 2 < H:
                        ret_s(j + 2)
                elif j == 8:
                    ret_state()
                elif j < 17:
                    state_update(j - 9)
                elif j in (20, 21):
                    ret_o(j - 20)
                elif 26 <= j < 30:
                    ret_squares(j - 26)
            claim(5, "mix_lo", 5)
            pe.wait_ge(sem("samp_own"), 2)
            for t in range(2):
                for c in range(4):
                    ins = M(bank[5][:, 8 * c + 4 * t:8 * c + 4 * t + 4], ovv[:, t, P * c:P * c + P],
                            cst[:, C_QSEL:C_QSEL + 4], start=True, stop=True)
            ins.then_inc(sem("samp_o"), 1)

            def out_proj(stage, u0, e0):
                for n in range(8):
                    b = (e0 + n) % RING
                    claim(b, "x_ready", 8 * stage + n + 1)
                    unit(u0 + n, b, actA)
                sum_squares(stage)

            pe.wait_ge(sem("mix_lo"), 5)
            pe.wait_ge(sem("attn_lo"), 4)
            out_proj(1, U_OUT0, E_OUT0)

            def ffn_pe(l, stage, u_up, u_dn, e_up, e_dn):
                pe.wait_ge(sem("norm_lo"), 8 * (stage + 1))

                def group(f, v, i4, i8, first=False):
                    for j in range(4):
                        name = "a_ready" if j < 2 else "g_ready"
                        b = (e_up + v + j) % RING
                        if first:
                            claim(b, name, FT * l + 1)
                        else:
                            pe.wait_ge(sem(name), FT * l + f + j % 2 - 1 + i4)
                        unit(u_up + v + j, b, actB, i8=i8)
                group(0, 0, 0, 0, True)
                with pe.Fori(0, 5) as i:
                    group(2, 4, i * 4, i * 8)
                    group(4, 8, i * 4, i * 8)
                for j in range(4):
                    last_reader[(e_up + 40 + j) % RING] = (sem("a_ready" if j < 2 else "g_ready"), FT * l + 21 + j % 2)
                for c in range(4):
                    for g, (k0, nk) in enumerate(KGROUPS):
                        for t in range(2):
                            b = (e_dn + 2 * c + t) % RING
                            if g == 0:
                                claim(b, "x_ready", 8 * (stage + 1) + 2 * c + t + 1)
                            if c == 0 and t == 0:
                                pe.wait_ge(sem("h_lo"), k0 + nk + FT * l)
                            unit(u_dn + 8 * c + 2 * g + t, b, hff, k0, nk, first=g == 0, last=g == 3)
                    if c == 0:
                        for g in range(2):
                            claim(4 + g, "conv_t_out", 2 * l + g + 1)
                            pe.wait_ge(sem("a_kept"), FT + FT * l)
                            TR(bank[4 + g][0:110, 0:P], fat[:, 5 * g:5 * g + 5, :].rearrange("p t f -> p (t f)"), ident).then_inc(sem("conv_t"), 1)
                sum_squares(stage + 1)

            ffn_pe(0, 1, U_UP0, U_DN0, E_UP0, E_DN0)
            pe.wait_ge(sem("norm_lo"), 24)
            for t in range(2):
                unit(U_IN1 + t, (E_IN1 + t) % RING, actA)


            def in1_unit(e, i8=0):
                pe.wait_ge(sem("evac1_done"), e - 1 + i8)
                unit(U_IN1 + e, (E_IN1 + e) % RING, actA, i8=i8)


            with pe.Fori(0, 3) as i:
                for j in range(8):
                    in1_unit(2 + j, i * 8)


            def job1(n):
                name, t, half = JOBS1[n]
                claim(4 + n % 4, "jobs_out", len(JOBS) + n + 1)
                for c in range(4):
                    f = {"q": 0, "k": 8, "v": 16}[name] + 4 * half + c
                    if t < 2:
                        ins = TR(bank[4 + n % 4][:, P * c:P * c + P], z1[:, f, P * t:P * t + P], ident)
                    else:
                        ins = TR(bank[4 + n % 4][0:NB, P * c:P * c + P], z1[:, f, TP:T], ident)
                ins.then_inc(sem("jobs_in"), 1)


            for j in range(8):
                in1_unit(26 + j)
                if j:
                    pe.wait_ge(sem("evac1_done"), 28)
                    job1(2 * j - 2)
                    job1(2 * j - 1)
            for r in range(RING):
                last_reader[r] = (sem("evac1_done"), 36)
            id8 = ident[0:8, 0:8]
            claim(7, "small_out", 1)
            pe.wait_ge(sem("m_ready"), 1)
            TR(bank[7][:, 0:8], R_A[:, 0:P], id8)
            TR(bank[7][:, 8:16], R_A[:, P:TP], id8).then_inc(sem("small_in"), 1)
            claim(7, "small_out", 2)
            pe.wait_ge(sem("gate_exp"), 3)
            for n in range(4):
                ins = TR(bank[7][0:NB, 8 * n:8 * n + 8], s8[:, 4 + n, :], id8)
            ins.then_inc(sem("small_in"), 1)
            claim(7, "small_out", 3)
            pe.wait_ge(sem("dec_diag"), 1)
            M(bank[7][:, 0:64], ones[0:NB, :], dd[:].rearrange("p b h -> p (b h)"), start=True, stop=True).then_inc(sem("small_in"), 1)


            def row_bcast(out, row, rhs):
                return M(out, ident[0:8, row:row + 1].to_broadcast([8, P]), rhs, start=True, stop=True)


            def head_s(h):
                claim(3, "e_arg", 2 * h + 2)
                row_bcast(bank[3][:, 0:TP], h, R_M[:, 0:TP]).then_inc(sem("m_b"), 1)
                claim(2, "w_ready", h + 1)
                q, k = z1[:, h, :], z1[:, 8 + h, :]
                M(bank[2][:, 0:256], k[:, 0:128], q[:, 0:256], start=True, stop=True)
                M(bank[2][:, 256:384], k[:, 128:256], q[:, 128:256], start=True, stop=True).then_inc(sem("m_s"), 1)


            def head_num(h):
                cols = slice(DC * h, DC * h + DC)
                w, v, kw, out = ww[h % 2], tk1["v"], tk1["k"], bank[h % 2]
                claim(h % 2, "head_out", 3 * h + 3)
                pe.wait_ge(sem("k_weighted"), 2 * h + 2)
                for t in range(2):
                    M(out[:, 256:384], v[:, t, cols], kw[:, t, cols], start=t == 0, stop=t == 1)
                for t in range(2):
                    M(out[:, 384:385], kw[:, t, cols], ones[:, 0:1], start=t == 0, stop=t == 1)
                pe.wait_ge(sem("w_ready"), h + 1)
                causal_pv(out[:, :], v[:, 0, cols], v[:, 1, cols], w)
                pick = sel[:, H - 1 - h:2 * H - 1 - h]
                M(bank[7][0:H, 0:256], pick, w[:, 0:256], start=h == 0, stop=False, skip_group_check=True)
                M(bank[7][0:H, 128:256], pick, w[:, 256:384], start=False, stop=h == H - 1, skip_group_check=True).then_inc(sem("num_in"), 1)


            def c_outer(b):
                for half in range(2):
                    claim(4 + half, "c_added", 2 * b + half + 1)
                    pe.wait_ge(sem("v_masked"), b + 1)
                    for n in range(4):
                        cols = slice(512 * half + DC * n, 512 * half + DC * n + DC)
                        ins = M(bank[4 + half][:, DC * n:DC * n + DC], vm[b % 2][:, cols], ts1["k"][:, cols], start=True, stop=True)
                    ins.then_inc(sem("outer"), 1)


            def q_bcast(b, half):
                claim(6, "q_mult", 2 * b + half + 1)
                row_bcast(bank[6][:, :], b, ts1["q"][:, 512 * half:512 * half + 512]).then_inc(sem("q_b"), 1)


            pe.wait_ge(sem("jobs_out"), len(JOBS) + len(JOBS1))
            pe.wait_ge(sem("sel_ready"), 2)
            claim(7, "den_in", 1)
            head_s(0)
            for h in range(H):
                c_outer(h)
                q_bcast(h, 0)
                head_num(h)
                if h + 1 < H:
                    head_s(h + 1)
                q_bcast(h, 1)
            claim(3, "n_row", 1)
            pe.wait_ge(sem("head_out"), 3 * H)
            TR(bank[3][0:H, 0:DC], ncol[:], ident).then_inc(sem("turned"), 1)
            claim(2, "den_in", 2)
            pe.wait_ge(sem("den_sample"), 1)
            TR(bank[2][0:H, 0:NB], s8[:, 12, :], id8).then_inc(sem("turned"), 1)
            claim(4, "h1_var", 1)
            pe.wait_ge(sem("head_sq"), H + 1)
            for h in range(H):
                ins = M(bank[4][0:H, 0:T], sel[:, H - 1 - h:2 * H - 1 - h], z1[:, h, :], start=h == 0, stop=h == H - 1)
            ins.then_inc(sem("head_ss"), 1)
            pe.wait_ge(sem("h1_rstd"), 1)
            for h in range(H):
                claim(h % 4, "mix1", h + 1)
                row_bcast(bank[h % 4][:, 0:T], h, R_M).then_inc(sem("rstd_b"), 1)
            pe.wait_ge(sem("mix1_lo"), 8)
            out_proj(3, U_OUT1, E_OUT1)
            ffn_pe(1, 3, U_UP1, U_DN1, E_UP1, E_DN1)
            for t in range(3):
                for half in range(2):
                    claim(2 * t + half, "y_out", 2 * t + half + 1)
                    for c in range(4):
                        k = 4 * half + c
                        pe.wait_ge(sem("y_scaled"), k + 1)
                        if t < 2:
                            ins = TR(bank[2 * t + half][:, P * c:P * c + P], sq[:, k, P * t:P * t + P], ident)
                        else:
                            ins = TR(bank[2 * t + half][0:NB, P * c:P * c + P], sq[:, k, TP:T], ident)
                    ins.then_inc(sem("x_t"), 1)


_INS = ["x_prompt", "x_sample", "cache_k", "cache_v", "page_table", "state_ret", "state_mlstm_C", "state_mlstm_n",
        "state_mlstm_m", "state_ffn_conv", "ab_norm_g", "ab_w_in", "ab_ret_norm_g", "ab_w_out", "c_norm_g", "c_w_in",
        "c_gate_bias", "c_out_norm_g", "c_w_out", "ffn_norm_g", "ffn_w1", "ffn_w3", "ffn_conv_w", "ffn_conv_b",
        "ffn_w2", "final_norm_g"]
_OUTS = [("y_prompt", (1, TP, D)), ("y_sample", (NB, 1, D)), ("k_prompt", (1, 1, TP, H, DA)), ("v_prompt", (1, 1, TP, H, DA)),
         ("k_sample", (1, NB, 1, H, DA)), ("v_sample", (1, NB, 1, H, DA)), ("ret_prompt", (1, 1, H, DA, DA)),
         ("ret_sample", (1, NB, H, DA, DA)), ("C_prompt", (1, 1, H, DC, DC)), ("C_sample", (1, NB, H, DC, DC)),
         ("n_prompt", (1, 1, H, DC)), ("n_sample", (1, NB, H, DC)), ("m_prompt", (1, 1, H)), ("m_sample", (1, NB, H)),
         ("conv_prompt", (2, 1, 2, DFF)), ("conv_sample", (2, NB, 2, DFF))]


def kernel(**inputs):
    from concourse import bacc
    from concourse.bass_utils import run_bass_kernel_spmd

    nc = bacc.Bacc("TRN2", target_bir_lowering=False, num_devices=1)
    arrays, args = {"in_consts": constants()}, {}
    args["consts"] = nc.dram_tensor("in_consts", [P, NCONST], F32, kind="ExternalInput").ap()
    for name in _INS:
        a = np.ascontiguousarray(inputs[name])
        arrays[f"in_{name}"] = a
        args[name] = nc.dram_tensor(f"in_{name}", a.shape, mybir.dt.from_np(a.dtype), kind="ExternalInput").ap()
    for name, shape in _OUTS:
        args[name] = nc.dram_tensor(f"out_{name}", shape, F32, kind="ExternalOutput").ap()
    build(nc, **args)
    r = run_bass_kernel_spmd(nc, [arrays], core_ids=[0])
    return tuple(r.results[0][f"out_{name}"] for name, _ in _OUTS)
```

```python
from contextlib import ExitStack

import concourse.bass as bass
import numpy as np
from concourse import mybir

F32 = mybir.dt.float32
F32R = mybir.dt.float32r
I32 = mybir.dt.int32
ALU = mybir.AluOpType
ACT = mybir.ActivationFunctionType
AX = mybir.AxisListType.X

P = 128
D = 1024
KT = D // P
TP = 256
NB = 8
T = TP + NB
NPAGE = 8
PAST = NPAGE * P
NPOOL = 5 * NB * NPAGE // 4
H = 8
DA = 64
DC = 128
DFF = 11 * D // 4
FT = DFF // P
IN_AB = 7 * H * DA
IN_C = 4 * D + 2 * H
EPS = 1e-6
BIG = 1e30
MOBA_BLOCK = 256
NBLK = PAST // MOBA_BLOCK
TOPK = 3
RING = 4
LOOK = 3
KGROUPS = ((0, 6), (6, 6), (12, 5), (17, 5))
LOG_G = [float(v) for v in np.log1p(-np.exp2(np.float32(-5.0) - np.arange(H, dtype=np.float32))).astype(np.float32)]

C_ID, C_PERM, C_BONES = 0, 128, 256
C_COS, C_SIN = 384, 384 + T
C_AMASK = C_SIN + T
C_RDIFF = C_AMASK + 384
C_MMASK = C_RDIFF + 384
C_RDEC = C_MMASK + 384
C_GAM = C_RDEC + 16
C_QSEL = C_GAM + 4
C_HMASK = C_QSEL + 4
NCONST = C_HMASK + 8
G_AB, G_RET, G_C, G_OUT, G_FFN, G_FIN = 0, 8, 12, 20, 28, 44

JOBS_AFTER = {5: [("t", "qa", 2)], 6: [("b", 0)], 7: [("b", 1)], 8: [("b", 2)], 9: [("b", 3)],
              10: [("t", "ka", 0), ("t", "ka", 1), ("t", "ka", 2)], 13: [("b", 4)],
              14: [("t", "va", 0), ("t", "va", 1), ("t", "va", 2)], 16: [("b", 5)], 19: [("b", 6)],
              21: [("t", "kb", 0), ("t", "kb", 1), ("t", "kb", 2)], 22: [("b", 7)],
              25: [("t", "vb", 0), ("t", "vb", 1), ("t", "vb", 2)]}
JOBS = [j for u in sorted(JOBS_AFTER) for j in JOBS_AFTER[u]]
TILE0 = {"qa": 0, "ka": 4, "va": 8, "qb": 12, "kb": 16, "vb": 20, "gb": 24}
ROPED = list(range(0, 8)) + list(range(12, 20))

JOBS1 = [(n, t, half) for n, t in (("q", 2), ("k", 2), ("v", 2), ("k", 0), ("k", 1), ("v", 0), ("v", 1)) for half in (0, 1)]
CRING = 3
EXP_MAX = 41.0


def jobs_until(u):
    return sum(len(v) for k, v in JOBS_AFTER.items() if k <= u)


def constants():
    c = np.zeros((P, NCONST), np.float32)
    p = np.arange(P)
    c[:, C_ID:C_ID + P] = np.eye(P)
    c[p ^ 32, C_PERM + p] = 1.0
    c[:, C_BONES:C_BONES + P] = (p[:, None] // 64) == (p[None, :] // 64)
    pos = np.concatenate([np.arange(TP), np.full(NB, PAST)]).astype(np.float32)
    inv = np.power(np.float32(10000.0), -(np.arange(32, dtype=np.float32) / np.float32(32))).astype(np.float32)
    ang = (pos[None, :] * inv[p % 32][:, None]).astype(np.float32).astype(np.float64)
    c[:, C_COS:C_COS + T] = np.cos(ang)
    c[:, C_SIN:C_SIN + T] = np.where((p % 64 < 32)[:, None], -np.sin(ang), np.sin(ang))
    j = np.arange(P)
    diag = np.where(j[None, :] > p[:, None], -BIG, 0.0)
    c[:, C_AMASK:C_AMASK + 128] = diag
    c[:, C_AMASK + 256:C_AMASK + 384] = diag
    i = np.concatenate([np.arange(256), np.arange(128)])
    d = (i[None, :] - p[:, None]).astype(np.float64)
    c[:, C_RDIFF:C_RDIFF + 384] = np.where(d >= 0, d, BIG)
    c[:, C_MMASK:C_MMASK + 384] = np.where(d >= 0, 0.0, BIG)
    lg = np.array(LOG_G, np.float64)
    for t in range(2):
        c[:, C_RDEC + 8 * t:C_RDEC + 8 * t + 8] = np.exp((TP - 1 - (t * P + p))[:, None] * lg[None, :])
    for t in range(4):
        c[:, C_GAM + t] = np.exp(lg[2 * t + p // 64])
    c[:, C_QSEL:C_QSEL + 4] = (p[:, None] // 32) == np.arange(4)[None, :]
    c[:, C_HMASK:C_HMASK + 8] = (p[:, None] % 32) == np.arange(8)[None, :]
    return c


def build(nc, consts, x_prompt, x_sample, cache_k, cache_v, page_table, state_ret, state_mlstm_C, state_mlstm_n,
          state_mlstm_m, state_ffn_conv, ab_norm_g, ab_w_in, ab_ret_norm_g, ab_w_out, c_norm_g, c_w_in,
          c_gate_bias, c_out_norm_g, c_w_out, ffn_norm_g, ffn_w1, ffn_w3, ffn_conv_w, ffn_conv_b, ffn_w2,
          final_norm_g, y_prompt, y_sample, k_prompt, v_prompt, k_sample, v_sample, ret_prompt, ret_sample,
          C_prompt, C_sample, n_prompt, n_sample, m_prompt, m_sample, conv_prompt, conv_sample):
    with ExitStack() as ctx:
        sems = {}

        def sem(name):
            if name not in sems:
                sems[name] = ctx.enter_context(nc.semaphore(name))
            return sems[name]

        def sbuf(stack, name, shape, dt=F32):
            return stack.enter_context(nc.sbuf_tensor(name, shape, dt))

        raw = [sbuf(ctx, f"w_raw{i}", [P, 8, 256]) for i in range(RING)]
        whi = [sbuf(ctx, f"w_hi{i}", [P, 8, P], F32R) for i in range(RING)]
        wlo = [sbuf(ctx, f"w_lo{i}", [P, 8, P], F32R) for i in range(RING)]
        x = sbuf(ctx, "x", [P, KT, T])
        sq = sbuf(ctx, "sq", [P, KT, T])
        actA = [sbuf(ctx, "actA_hi", [P, KT, T], F32R), sbuf(ctx, "actA_lo", [P, KT, T], F32R)]
        cst = sbuf(ctx, "cst", [P, NCONST])
        ones = sbuf(ctx, "ones", [P, P])
        gains = sbuf(ctx, "gains", [P, 52])
        convp = [sbuf(ctx, f"convp{l}", [P, 4, FT]) for l in range(2)]
        convb = [sbuf(ctx, f"convb{l}", [P, NB, 2, FT]) for l in range(2)]
        rstd = sbuf(ctx, "rstd", [P, T])
        var = sbuf(ctx, "var", [P, T])
        nwt = sbuf(ctx, "nwt", [P, T])
        bank = [ctx.enter_context(nc.psum_tensor(f"bank{i}", [P, 512], F32)) for i in range(8)]

        with ExitStack() as st:
            z0 = sbuf(st, "z0", [P, 28, T])
            tok = {n: sbuf(st, f"tok_{n}", [P, 2, 512]) for n in ("ka", "va", "kb", "vb")}
            tks = {n: sbuf(st, f"tks_{n}", [NB, 512]) for n in ("qa", "ka", "va", "kb", "vb")}
            kv = [sbuf(st, f"kv{i}", [P, 2, 512]) for i in range(4)]
            smx = [sbuf(st, f"smx{i}", [P, 384]) for i in range(2)]
            ptt = [sbuf(st, f"ptt{i}", [P, 384]) for i in range(2)]
            rmk = [sbuf(st, f"rmk{i}", [P, 384]) for i in range(2)]
            sc_all = sbuf(st, "sc_all", [P, NPAGE, NB, H])
            s0 = sbuf(st, "s0", [P, 4, NB, DA])
            sm = sbuf(st, "sm", [P, 80])
            pts = sbuf(st, "pts", [P, NPAGE, 64])
            rst = sbuf(st, "rst", [64, 512])
            dgs = sbuf(st, "dgs", [NB, NB, H])
            dgp = sbuf(st, "dgp", [NB, NB, H])
            pg = sbuf(st, "pg", [1, NB * NPAGE], I32)
        zf = z0[:, :, :].rearrange("p a b -> p (a b)")
        kdec = zf[:, 4 * T:4 * T + 1024].rearrange("p (t n) -> p t n", t=2)
        ovv = tok["kb"]
        prd = zf[0:NB, 20 * T:20 * T + 512]
        sqf = sq[:, :, :].rearrange("p a b -> p (a b)")
        qb = [sqf[:, 512 * i:512 * i + 512] for i in range(4)]
        prow = sqf[0:64, 0:PAST]
        vdg = [sqf[0:NB, 1024 + 512 * i:1536 + 512 * i].rearrange("p (b e) -> p b e", b=NB) for i in range(2)]

        with ExitStack() as st:
            actB = [sbuf(st, "actB_hi", [P, KT, T], F32R), sbuf(st, "actB_lo", [P, KT, T], F32R)]
            hff = [sbuf(st, "hff_hi", [P, FT, T], F32R), sbuf(st, "hff_lo", [P, FT, T], F32R)]
            ffa = [sbuf(st, f"ffa{i}", [P, 2 + T]) for i in range(4)]
            fft = [sbuf(st, f"fft{i}", [P, T]) for i in range(4)]
            ffg = [sbuf(st, f"ffg{i}", [P, T]) for i in range(4)]
            ffp = sbuf(st, "ffp", [P, NB, FT])
            ffq = sbuf(st, "ffq", [P, NB, FT])
            fat = sbuf(st, "fat", [P, 10, FT])
            fco = sbuf(st, "fco", [110, 2, P])

        with ExitStack() as st:
            z1 = sbuf(st, "z1", [P, 32, T])
            tk1 = {n: sbuf(st, f"tok1_{n}", [P, 2, D]) for n in ("k", "v")}
            ts1 = {n: sbuf(st, f"tks1_{n}", [NB, D]) for n in ("q", "k", "v", "n")}
            cs = [sbuf(st, f"cs{i}", [P, H, DC]) for i in range(CRING)]
            vm = [sbuf(st, f"vm{i}", [96, D], F32R) for i in range(2)]
            pick3 = sbuf(st, "pick3", [64, 8], F32R)
            m3 = sbuf(st, "m3", [64, T], F32R)
            prod = sbuf(st, "prod", [P, D])
            ew = [sbuf(st, f"ew{i}", [P, 384]) for i in range(2)]
            s8 = sbuf(st, "s8", [NB, 13, NB])
            dd = sbuf(st, "dd", [NB, NB, H])
            g8 = sbuf(st, "g8", [H, 4])
            acol = sbuf(st, "acol", [P, 2, H])
            decb = sbuf(st, "decb", [P, NB, H])
            ncol = sbuf(st, "ncol", [P, H])
            sel = sbuf(st, "sel", [P, 2 * H - 1])
            qkv_scale = sbuf(st, "qkv_scale", [P, 3])
        ww = [cst[:, C_AMASK:C_AMASK + 384], cst[:, C_RDIFF:C_RDIFF + 384]]
        R_I, R_F, R_D, R_T, R_B, R_A, R_M, R_E = (sq[0:H, n, :] for n in range(8))


        q3 = actA[0][:, :, :].rearrange("p a b -> p (a b)")[0:64, 0:D]
        k3 = actA[1][:, :, :].rearrange("p a b -> p (a b)")[0:96, 0:D]
        v3 = actA[1][:, :, :].rearrange("p a b -> p (a b)")[0:96, D:2 * D]
        def seq_bank(b, n):
            return 4 + (4 * b + n) % 3


        y_rows = [raw[i][:, 0:4, :].rearrange("p a b -> p (a b)") for i in range(3)]
        x_tok = zf[:, 0:2048].rearrange("p (t n) -> p t n", t=2)
        xs_tok = zf[0:NB, 2112:3136]
        vec_rows = zf[0:52, 3200:3328]
        cw_rows = [zf[0:88, 3328 + 128 * l:3456 + 128 * l] for l in range(2)]
        cb_rows = [zf[0:88, 3584 + 512 * l:4096 + 512 * l].rearrange("p (q n) -> p q n", q=4) for l in range(2)]
        ident = cst[:, C_ID:C_ID + P]
        perm = cst[:, C_PERM:C_PERM + P]
        bones = cst[:, C_BONES:C_BONES + P]
        cos = cst[:, C_COS:C_COS + T]
        sin = cst[:, C_SIN:C_SIN + T]
        eye8 = cst[0:NB, C_ID:C_ID + NB]

        def zt(n, c, a=0, b=T):
            return z0[:, TILE0[n] + c, a:b]

        U_IN0, U_OUT0, U_UP0, U_DN0, U_IN1, U_OUT1, U_UP1, U_DN1, U_END = np.cumsum(
            [0, 28, 8, 44, 32, 34, 8, 44, 32]).tolist()
        E_IN0, E_OUT0, E_UP0, E_DN0, E_IN1, E_OUT1, E_UP1, E_DN1, E_END = np.cumsum(
            [0, 28, 8, 44, 8, 34, 8, 44, 8]).tolist()

        def row_tiles(u):
            for u0 in (U_DN0, U_DN1):
                if u0 <= u < u0 + 32:
                    return KGROUPS[(u - u0) // 2 % 4]
            return 0, 8

        w_in0 = ab_w_in[0].rearrange("(k p) n -> p k n", p=P)
        w_out0 = ab_w_out[0].rearrange("(k p) n -> p k n", p=P)
        w_in1 = c_w_in[0].rearrange("(k p) n -> p k n", p=P)
        w_out1 = c_w_out[0].rearrange("(k p) n -> p k n", p=P)
        w_a = [ffn_w1[l].rearrange("(k p) n -> p k n", p=P) for l in range(2)]
        w_g = [ffn_w3[l].rearrange("(k p) n -> p k n", p=P) for l in range(2)]
        w_d = [ffn_w2[l].rearrange("(k p) n -> p k n", p=P) for l in range(2)]

        block = ctx.enter_context(nc.Block())

        @block.sync
        def _(sp):
            def load_raw(r, src, i8=0):
                if r >= RING:
                    sp.wait_ge(sem("lo_ready"), 2 * (r - RING) + 2 + i8)
                sp.dma_start(raw[r % RING][:, 0:src.shape[1], :], src).then_inc(sem(f"w_landed{r % RING}"), 16)

            pages = [None]

            def page_pair(j, cache, freed):
                if j % 4 == 0:
                    i = 8 * (j // 4)
                    pages[0] = nc.values_load_multi_w_load_instructions(
                        pg[0:1, i:i + 8], engines=[mybir.EngineType.SP], min_val=0, max_val=NPOOL - 1)[1]
                if freed is not None:
                    sp.wait_ge(*freed)
                for t in range(2):
                    row = pages[0][2 * (j % 4) + t]
                    sp.dma_start(kv[j % 4][:, t, :], cache[0, bass.ds(row, 1)].rearrange("o p h d -> p (o h d)")
                                 ).then_inc(sem(f"kv_landed{j % 4}"), 16)

            def k_pages(j):
                page_pair(j, cache_k, (sem("k_reduced"), j - 3) if j >= 4 else None)

            for n in range(14):
                load_raw(n, w_in0[:, :, 256 * n:256 * n + 256])
                if n == 0:
                    for at, v in ((G_FFN, ffn_norm_g[0]), (G_FFN + 8, ffn_norm_g[1]), (G_FIN, final_norm_g)):
                        sp.dma_start(vec_rows[at:at + 8, :], v.rearrange("(k p) -> k p", p=P)).then_inc(sem("x_landed"), 16)
                    sp.wait_ge(sem("x_landed"), 16 * 9)
                if n == 4:
                    sp.wait_ge(sem("pages_landed"), 16)
                    for j in range(4):
                        k_pages(j)
                if n >= 10:
                    k_pages(2 * n - 16)
                    k_pages(2 * n - 15)
            for n in range(4):
                load_raw(U_OUT0 // 2 + n, w_out0[:, :, 256 * n:256 * n + 256])
                k_pages(12 + 2 * n)
                k_pages(13 + 2 * n)
            for j in range(20, 32):
                k_pages(j)
            for j in range(32):
                page_pair(j, cache_v, (sem("k_reduced"), 29 + j) if j < 4 else (sem("v_used"), j - 3))

            def ffn_loads(l, u_up, u_dn):
                def pair(n, c, i8):
                    load_raw(u_up // 2 + 2 * n, w_a[l][:, :, bass.ds(c, 256)], i8)
                    load_raw(u_up // 2 + 2 * n + 1, w_g[l][:, :, bass.ds(c, 256)], i8)
                with sp.Fori(0, 5) as i:
                    pair(0, i * 512, i * 8)
                    pair(1, i * 512 + 256, i * 8)
                pair(10, 2560, 0)

                def chunk(n, c, i16):
                    for g, (k0, nk) in enumerate(KGROUPS):
                        load_raw(u_dn // 2 + 4 * n + g, w_d[l][:, k0:k0 + nk, bass.ds(c, 256)], i16)
                with sp.Fori(0, 2) as i:
                    chunk(0, i * 512, i * 16)
                    chunk(1, i * 512 + 256, i * 16)

            ffn_loads(0, U_UP0, U_DN0)
            sp.wait_ge(sem("lo_ready"), U_IN1 - 2 * RING + 2)
            with nc.allow_non_contiguous_dma(reason="16 columns of gates"):
                for t, name in ((0, f"w_landed{U_IN1 // 2 % RING}"), (1, "f_gate_landed")):
                    sp.dma_start(raw[U_IN1 // 2 % RING][:, :, P * t:P * t + H],
                                 w_in1[:, :, 4 * D + H * t:4 * D + H * t + H]).then_inc(sem(name), 16)
            with sp.Fori(0, 4) as i:
                for n in range(4):
                    load_raw(U_IN1 // 2 + 1 + n, w_in1[:, :, bass.ds(i * 1024 + 256 * n, 256)], i * 8)
            sp.wait_ge(sem("c_small"), 64)

            def c_load(b):
                sp.dma_start(cs[b % CRING][:], state_mlstm_C[0, b].rearrange("h e d -> e h d")
                             ).then_inc(sem(f"c_landed{b % CRING}"), 16)
            for b in range(CRING):
                c_load(b)
            for n in range(4):
                load_raw(U_OUT1 // 2 + n, w_out1[:, :, 256 * n:256 * n + 256])
            for b in range(NB):
                sp.wait_ge(sem("c_added"), 2 * b + 2)
                sp.dma_start(C_sample[0, b].rearrange("h e d -> e h d"), cs[b % CRING][:]
                             ).then_inc(sem(f"c_stored{b % CRING}"), 16)
                n = b + CRING - 1
                if CRING <= n < NB:
                    sp.wait_ge(sem(f"c_stored{n % CRING}"), 16 * (n // CRING))
                    sp.wait_ge(sem("q_mult"), 2 * (n - CRING) + 2)
                    c_load(n)
            ffn_loads(1, U_UP1, U_DN1)

        @block.gpsimd
        def _(pool):
            G = nc.gpsimd
            G.memset(ones[:], 1.0).then_inc(sem("ones_ready"), 1)
            pool.dma_start(pg[:], page_table.rearrange("(o b) n -> o (b n)", o=1)).then_inc(sem("pages_landed"), 16)
            for l in range(2):
                pool.dma_start(cw_rows[l][0:66, :], ffn_conv_w[l].rearrange("j (f p) -> (j f) p", p=P)
                               ).then_inc(sem("param_landed"), 16)
                pool.dma_start(cw_rows[l][66:88, :], ffn_conv_b[l].rearrange("(f p) -> f p", p=P)
                               ).then_inc(sem("param_landed"), 16)
                for q in range(4):
                    pool.dma_start(cb_rows[l][:, q, :],
                                   state_ffn_conv[l, 2 * q:2 * q + 2].rearrange("b j (f p) -> (b j f) p", p=P)
                                   ).then_inc(sem("param_landed"), 16)
            for b in range(NB):
                pool.dma_start(s0[:, :, b, :], state_ret[0, b].rearrange("(c q) d e -> (q d) c e", q=2)
                               ).then_inc(sem("s0_landed"), 16)
            for l in range(2):
                pool.dma_start(conv_sample[l, :, 0, :], state_ffn_conv[l, :, 1, :]).then_inc(sem("row_stored"), 16)
            pool.wait_ge(sem("const_landed"), 32)
            pool.wait_ge(sem("const_landed"), 16)

            def add_squares(stage):
                for k in range(1, KT):
                    pool.wait_ge(sem("sq_ready"), 8 * stage + k + 1)
                    if k > 1:
                        pool.wait_ge(sem("sq_added"), 7 * stage + k - 8)
                    G.tensor_tensor(sq[:, 0, :], sq[:, 0, :], sq[:, k, :], ALU.add).then_inc(sem("sq_added"), 1)

            def k_mult(j):
                b = j // 4
                if j % 4 == 0:
                    pool.wait_ge(sem("jobs_out"), JOBS.index(("b", b)) + 1)
                pool.wait_ge(sem(f"kv_landed{j % 4}"), 32 * (j // 4 + 1))
                G.tensor_tensor(kv[j % 4][:], kv[j % 4][:], qb[b % 4].unsqueeze(1).to_broadcast([P, 2, 512]),
                                ALU.mult).then_inc(sem("k_mult"), 1)

            for u in range(28):
                if u in ROPED:
                    r = ROPED.index(u)
                    pool.wait_ge(sem("evac_done"), u + 1)
                    if r >= 2:
                        pool.wait_ge(sem("roped"), r - 1)
                    G.tensor_tensor(rmk[r % 2][:, 0:T], z0[:, u, :], cos, ALU.mult).then_inc(sem("cos_prod"), 1)
                if u >= 8:
                    k_mult(u - 8)
            for j in range(20, 32):
                k_mult(j)
            pool.wait_ge(sem("k_mult"), 32)
            pool.wait_ge(sem("jobs_out"), len(JOBS))
            for h in range(H):
                if h >= 2:
                    pool.wait_ge(sem("kv_outer"), h - 1)
                G.tensor_tensor(vdg[h % 2], eye8.unsqueeze(2).to_broadcast([NB, NB, DA]),
                                tks["vb"][:, DA * h:DA * h + DA].unsqueeze(1).to_broadcast([NB, NB, DA]),
                                ALU.mult).then_inc(sem("v_diag"), 1)
            pool.wait_ge(sem("gate_act"), 1)
            pool.wait_ge(sem("ob_prompt"), 4)
            pool.wait_ge(sem("ob_sample"), 2)
            G.tensor_tensor(z0[:, 24:28, :], z0[:, 24:28, :], z0[:, 8:12, :], ALU.mult).then_inc(sem("ob_gated"), 1)

            def ffn_pool(l, stage):
                add_squares(stage)
                pool.wait_ge(sem("x_ready"), 8 * (stage + 1))
                for s in range(4):
                    G.memset(ffa[s][:, 0:2], 0.0).then_inc(sem("pad_zero"), 1)

                def group(f, i4, fd):
                    for t in range(2):
                        pool.wait_ge(sem("a_ready"), f + t + 1 + i4 + FT * l)
                        G.tensor_copy(fat[:, :, bass.ds(fd + t, 1)],
                                      ffa[(f + t) % 4][:, 256:266].unsqueeze(2)).then_inc(sem("a_kept"), 1)
                    for t in range(2):
                        s = (f + t) % 4
                        pool.wait_ge(sem("gelu"), f + t + 1 + i4 + FT * l)
                        pool.wait_ge(sem("g_ready"), f + t + 1 + i4 + FT * l)
                        G.tensor_tensor(ffg[s][:], ffg[s][:], fft[s][:], ALU.mult).then_inc(sem("gated"), 1)
                with pool.Fori(0, 5) as i:
                    group(0, i * 4, i * 4)
                    group(2, i * 4, i * 4 + 2)
                group(20, 0, 20)
                add_squares(stage + 1)

            ffn_pool(0, 1)
            pool.wait_ge(sem("c_small"), 64)
            G.memset(sel[:], 0.0).then_inc(sem("sel_ready"), 1)
            pool.wait_ge(sem("sel_ready"), 1)
            G.memset(sel[:, H - 1:H], 1.0).then_inc(sem("sel_ready"), 1)
            pool.wait_ge(sem("small_out"), 2)
            pool.wait_ge(sem("jobs_out"), len(JOBS) + 6)


            def rows(name):
                return ts1[name][:].rearrange("p (h d) -> p h d", h=H)


            def weight(n):
                return s8[:, n, :].unsqueeze(2).to_broadcast([NB, H, DC])


            G.tensor_tensor(rows("v"), rows("v"), weight(9), ALU.mult).then_inc(sem("v_weighted"), 1)


            def c_decay(b):
                pool.wait_ge(sem(f"c_landed{b % CRING}"), 16 * (b // CRING + 1))
                G.tensor_tensor(cs[b % CRING][:], cs[b % CRING][:], decb[:, b, :].unsqueeze(2).to_broadcast([P, H, DC]),
                                ALU.mult).then_inc(sem("c_decayed"), 1)


            pool.wait_ge(sem("small_out"), 3)
            c_decay(0)
            c_decay(1)
            pn = prod[0:NB, :].rearrange("p (h d) -> p h d", h=H)
            G.tensor_tensor(rows("n"), rows("n"), weight(8), ALU.mult).then_inc(sem("n_step"), 1)
            G.tensor_tensor(pn, rows("k"), weight(9), ALU.mult).then_inc(sem("n_step"), 1)
            pool.wait_ge(sem("n_step"), 2)
            G.tensor_tensor(rows("n"), rows("n"), pn, ALU.add).then_inc(sem("n_step"), 1)
            pool.wait_ge(sem("n_step"), 3)
            G.tensor_tensor(pn, rows("n"), rows("q"), ALU.mult).then_inc(sem("n_step"), 1)
            for b in range(2, NB):
                c_decay(b)
            pool.wait_ge(sem("gate_act"), 2)
            pool.wait_ge(sem("head_out"), 3 * H)
            pool.wait_ge(sem("num_sample"), NB)
            for t in range(2):
                a = 24 + 4 * t
                G.tensor_tensor(z1[:, a:a + 4, :], z1[:, a:a + 4, :], z1[:, a - 8:a - 4, :], ALU.mult).then_inc(sem("o1_gated"), 1)
            ffn_pool(1, 3)

        @block.scalar
        def _(act):
            A = nc.scalar.activation
            act.dma_start(cst[:, 0:C_COS], consts[:, 0:C_COS]).then_inc(sem("const_landed"), 16)
            act.dma_start(x_tok, x_prompt[0].rearrange("(t p) n -> p t n", p=P)).then_inc(sem("x_landed"), 16)
            act.dma_start(xs_tok, x_sample.rearrange("b o n -> (b o) n")).then_inc(sem("x_landed"), 16)
            for at, v, n in ((G_AB, ab_norm_g[0], 8), (G_RET, ab_ret_norm_g[0], 4), (G_C, c_norm_g[0], 8),
                             (G_OUT, c_out_norm_g[0], 8)):
                act.dma_start(vec_rows[at:at + n, :], v.rearrange("(k p) -> k p", p=P)).then_inc(sem("x_landed"), 16)
            act.dma_start(cst[:, C_COS:NCONST], consts[:, C_COS:NCONST]).then_inc(sem("const_landed"), 16)
            n_stored = 0

            def split_hi(u, i8=0):
                if u >= U_END:
                    return
                act.wait_ge(sem(f"w_landed{u // 2 % RING}"), 16 * (u // 8 + 1) + i8 * 2)
                if u == U_IN1 + 1:
                    act.wait_ge(sem("f_gate_landed"), 16)
                if u >= RING:
                    act.wait_ge(sem("mm_done"), u - RING + 1 + i8)
                nk = row_tiles(u)[1]
                A(whi[u % RING][:, 0:nk, :], raw[u // 2 % RING][:, 0:nk, P * (u % 2):P * (u % 2) + P], ACT.Copy
                  ).then_inc(sem("hi_ready"), 1)

            def norm_in(stage, k, g, dst, i=0):
                act.wait_ge(sem("x_ready"), 8 * stage + k + 1 + i)
                if g is not None:
                    A(dst[0][:, bass.ds(i + k, 1), :], x[:, bass.ds(i + k, 1), :], ACT.Copy,
                      scale=gains[:, bass.ds(g + k + i, 1)]).then_inc(sem("norm_hi"), 1)
                A(sq[:, bass.ds(i + k, 1), :], x[:, bass.ds(i + k, 1), :], ACT.Square).then_inc(sem("sq_ready"), 1)

            def rsqrt_seed(name, n, src, tmp, dst):
                act.preload_act_table_set("natural_log_exp_and_others")
                act.wait_ge(sem(f"{name}_var"), n)
                A(tmp, src, ACT.Ln).then_inc(sem("ln_done"), 1)
                lns[0] += 1
                act.wait_ge(sem("ln_done"), lns[0])
                A(dst, tmp, ACT.Exp, scale=-0.5).then_inc(sem(f"{name}_seed"), 1)

            lns = [0]
            act.wait_ge(sem("param_t"), 1)
            A(gains[:], bank[4][:, 0:52], ACT.Copy).then_inc(sem("param_out"), 1)
            act.wait_ge(sem("param_out"), 1)
            split_hi(0)
            for k in range(KT):
                norm_in(0, k, G_AB, actA)
            for u in (1, 2, 3):
                split_hi(u)
            rsqrt_seed("rms", 1, var[:], nwt[:], rstd[:])

            def evict_jobs(a, b):
                for n in range(a, b):
                    act.wait_ge(sem("jobs_in"), n + 1)
                    if JOBS[n][0] == "b":
                        s = JOBS[n][1]
                        if s >= 4:
                            act.wait_ge(sem("k_mult"), 4 * (s - 4) + 4)
                        dst = qb[s % 4]
                    else:
                        dst = tks[JOBS[n][1]][:] if JOBS[n][2] == 2 else tok[JOBS[n][1]][:, JOBS[n][2], :]
                    A(dst, bank[6 + n % 2][0:dst.shape[0], :], ACT.Copy).then_inc(sem("jobs_out"), 1)

            for u in range(28):
                split_hi(u + LOOK + 1)
                evict_jobs(jobs_until(u - 1), jobs_until(u))
                if u == 0:
                    act.wait_ge(sem("param_t"), 2)
                    for l in range(2):
                        A(convp[l][:].rearrange("p a b -> p (a b)"), bank[4][:, 64 + 96 * l:152 + 96 * l], ACT.Copy
                          ).then_inc(sem("param_out"), 1)
                    for l in range(2):
                        act.wait_ge(sem("param_t"), 3 + l)
                        A(convb[l][:].rearrange("p b j f -> p (b j f)"), bank[5 + l][:, 0:352], ACT.Copy).then_inc(sem("param_out"), 1)
            act.wait_ge(sem("jobs_out"), len(JOBS))
            for n, op, os_ in (("ka", k_prompt, k_sample), ("va", v_prompt, v_sample)):
                act.dma_start(op[0, 0].rearrange("(t p) h d -> p t (h d)", p=P), tok[n][:]).then_inc(sem("stored"), 16)
                act.dma_start(os_[0].rearrange("b o h d -> (b o) (h d)"), tks[n][:]).then_inc(sem("stored"), 16)
            n_stored += 4

            def attn_exp(h):
                act.wait_ge(sem("attn_nmax"), h + 1)
                for t, (a, b) in enumerate(((0, 128), (128, 384))):
                    c = 4 + 2 * (h % 2) + t
                    A(smx[h % 2][:, a:b], smx[h % 2][:, a:b], ACT.Exp, bias=sm[:, c:c + 1], scale=DA ** -0.5,
                      accum_out=sm[:, c + 4:c + 5]).then_inc(sem("attn_exp"), 1)

            def attn_scale(h):
                act.wait_ge(sem("attn_rcp"), h + 1)
                for t, (a, b) in enumerate(((0, 128), (128, 384))):
                    c = 20 + 2 * (h % 2) + t
                    A(smx[h % 2][:, a:b], smx[h % 2][:, a:b], ACT.Copy, scale=sm[:, c:c + 1]).then_inc(sem("attn_p"), 1)

            def attn_pt(h):
                act.wait_ge(sem("attn_pt"), h + 1)
                if h >= 2:
                    act.wait_ge(sem("attn_pv"), h - 1)
                A(ptt[h % 2][:], bank[6][:, 0:384], ACT.Copy).then_inc(sem("attn_pt_out"), 1)

            def attn_out(c):
                act.wait_ge(sem("attn_pv"), 2 * c + 2)
                A(actA[0][:, c, 0:TP], bank[c % 2][:, 0:TP], ACT.Copy).then_inc(sem("attn_hi"), 1)

            def ret_mask(h):
                if h >= 2:
                    act.wait_ge(sem("ret_pv"), h - 1)
                A(rmk[h % 2][:], cst[:, C_RDIFF:C_RDIFF + 384], ACT.Exp, scale=LOG_G[h]).then_inc(sem("ret_mask"), 1)

            def ob_out(c):
                act.wait_ge(sem("ret_pv"), 2 * c + 2)
                A(z0[:, 8 + c, 0:TP], bank[7][:, 0:TP], ACT.Copy).then_inc(sem("ob_prompt"), 1)

            act.wait_ge(sem("roped"), 16)
            for h in range(H):
                attn_exp(h)
                if h >= 1:
                    attn_scale(h - 1)
                if h >= 2:
                    attn_pt(h - 2)
                if h >= 4 and h % 2 == 0:
                    attn_out((h - 4) // 2)
                    ob_out((h - 4) // 2)
                if h >= 1:
                    ret_mask(h - 1)
            attn_scale(H - 1)
            attn_pt(H - 2)
            ret_mask(H - 1)
            attn_out(2)
            ob_out(2)
            attn_pt(H - 1)
            attn_out(3)
            ob_out(3)

            act.wait_ge(sem("k_mult"), 32)
            for t in range(2):
                act.wait_ge(sem("samp_st"), t + 1)
                A(prow[:, 512 * t:512 * t + 512], bank[4 + t][0:64, :], ACT.Copy).then_inc(sem("samp_rows"), 1)

            act.wait_ge(sem("ret_state"), 1)
            A(rst[:], bank[3][0:64, :], ACT.Copy).then_inc(sem("ret_state_out"), 1)
            act.wait_ge(sem("ret_state_out"), 1)
            act.dma_start(ret_prompt[0, 0].rearrange("h d e -> d h e"), rst[:].rearrange("p (h e) -> p h e", h=H)
                          ).then_inc(sem("stored"), 16)
            n_stored += 1
            act.wait_ge(sem("samp_bias"), 1)
            for n in range(NBLK):
                blk = prow[:, MOBA_BLOCK * n:MOBA_BLOCK * n + MOBA_BLOCK]
                A(blk, blk, ACT.Exp, bias=sm[0:64, 24 + n:25 + n], scale=DA ** -0.5,
                  accum_out=sm[0:64, 32 + n:33 + n]).then_inc(sem("samp_exp"), 1)
            A(sm[0:64, 36:37], sm[0:64, 68:69], ACT.Exp, bias=sm[0:64, 28:29], scale=DA ** -0.5).then_inc(sem("samp_exp"), 1)
            act.wait_ge(sem("samp_pt"), 1)
            A(pts[:].rearrange("p a b -> p (a b)"), bank[6][:, :], ACT.Copy).then_inc(sem("samp_pt_out"), 1)
            act.wait_ge(sem("evac_done"), 28)
            A(z0[:, 24:28, :], z0[:, 24:28, :], ACT.Silu).then_inc(sem("gate_act"), 1)
            act.wait_ge(sem("s_new"), 4)
            for b in range(NB):
                act.dma_start(ret_sample[0, b].rearrange("(c q) d e -> (q d) c e", q=2), s0[:, :, b, :]).then_inc(sem("stored"), 16)
            n_stored += 8
            act.wait_ge(sem("ob_sample"), 2)
            A(z0[:, 0:4, :], z0[:, 8:12, :], ACT.Square).then_inc(sem("ret_sq"), 1)
            rsqrt_seed("ret", 4, z0[:, 4:8, :], z0[:, 16:20, :], z0[:, 20:24, :])
            for c in range(4):
                act.wait_ge(sem("ret_mix"), c + 1)
                A(actA[0][:, 4 + c, :], z0[:, c, :], ACT.Copy).then_inc(sem("ret_hi"), 1)
            act.wait_ge(sem("samp_o"), 1)
            A(actA[0][:, 0:4, TP:T], bank[5][:, 0:32].rearrange("p (c b) -> p c b", c=4), ACT.Copy).then_inc(sem("samp_hi"), 1)

            act.wait_ge(sem("stored"), 16 * n_stored)

            def out_inputs(stage, u0, g):
                for n in range(8):
                    if n < 7:
                        split_hi(u0 + n + LOOK + 1)
                    norm_in(stage, n, g, actB)
                split_hi(u0 + 7 + LOOK + 1)

            out_inputs(1, U_OUT0, G_FFN)

            def ffn_act(l, stage, u_up, u_dn, g_next, dst_next):
                rsqrt_seed("rms", stage + 1, var[:], nwt[:], rstd[:])

                def first_tap(f, i4, fd):
                    act.wait_ge(sem("a_ready"), f + 1 + i4 + FT * l)
                    A(fft[f % 4][:, 0:TP], ffa[f % 4][:, 0:TP], ACT.Identity, scale=convp[l][:, 0, bass.ds(fd, 1)],
                      bias=convp[l][:, 3, bass.ds(fd, 1)]).then_inc(sem("tap"), 1)

                def gelu(f, i4):
                    act.wait_ge(sem("conv"), f + 1 + i4 + FT * l)
                    A(fft[f % 4][:], fft[f % 4][:], ACT.Gelu_apprx_tanh).then_inc(sem("gelu"), 1)

                def h_hi(f, i4, fd):
                    act.wait_ge(sem("gated"), f + 1 + i4 + FT * l)
                    A(hff[0][:, bass.ds(fd, 1), :], ffg[f % 4][:].unsqueeze(1), ACT.Copy).then_inc(sem("h_hi"), 1)

                def group(f, u, i4, i8, fd, first=False):
                    split_hi(u + LOOK + 1, i8)
                    first_tap(f, i4, fd)
                    if not first:
                        h_hi(f - 2, i4, fd - 2)
                    split_hi(u + LOOK + 2, i8)
                    first_tap(f + 1, i4, fd + 1)
                    if not first:
                        h_hi(f - 1, i4, fd - 1)
                    split_hi(u + LOOK + 3, i8)
                    gelu(f, i4)
                    split_hi(u + LOOK + 4, i8)
                    gelu(f + 1, i4)

                def conv_rows_out():
                    for g in range(2):
                        act.wait_ge(sem("conv_t"), g + 1 + 2 * l)
                        A(fco[:, g, :], bank[4 + g][0:110, 0:P], ACT.Copy).then_inc(sem("conv_t_out"), 1)
                    act.wait_ge(sem("conv_t_out"), 2 + 2 * l)
                    for o, rows in ((conv_prompt[l, 0], fco[0:2 * FT, 0, :]),
                                    (conv_sample[l, 0:3, 1], fco[2 * FT:5 * FT, 0, :]),
                                    (conv_sample[l, 3:8, 1], fco[0:5 * FT, 1, :])):
                        act.dma_start(o.rearrange("t (f p) -> t f p", p=P), rows).then_inc(sem("stored"), 16)

                act.wait_ge(sem("pad_zero"), 4 + 4 * l)
                group(0, u_up, 0, 0, 0, True)
                with act.Fori(0, 5) as i:
                    group(2, u_up + 4, i * 4, i * 8, i * 4 + 2)
                    group(4, u_up + 8, i * 4, i * 8, i * 4 + 4)

                for c in range(4):
                    for j in range(8):
                        split_hi(u_dn + 8 * c + j + LOOK + 1)
                        if c == 0 and j == 1:
                            h_hi(FT - 2, 0, FT - 2)
                            h_hi(FT - 1, 0, FT - 1)
                    for t in range(2):
                        norm_in(stage + 1, 2 * c + t, g_next, dst_next)
                    if c == 0:
                        conv_rows_out()

            ffn_act(0, 1, U_UP0, U_DN0, G_C, actA)
            n_stored += 3
            act.wait_ge(sem("stored"), 16 * n_stored)
            act.dma_start(g8[:, 0:1], c_gate_bias[0, 0].rearrange("(h o) -> h o", o=1)).then_inc(sem("c_small"), 16)
            act.dma_start(g8[:, 1:2], c_gate_bias[0, 1].rearrange("(h o) -> h o", o=1)).then_inc(sem("c_small"), 16)
            with nc.allow_non_contiguous_dma(reason="64 values, turned"):
                act.dma_start(s8[:, 0, :], state_mlstm_m[0].rearrange("b h -> h b")).then_inc(sem("c_small"), 16)
            act.dma_start(ts1["n"][:], state_mlstm_n[0].rearrange("b h d -> b (h d)")).then_inc(sem("c_small"), 16)
            rsqrt_seed("rms", 3, var[:], nwt[:], rstd[:])
            split_hi(U_IN1 + 4)
            split_hi(U_IN1 + 5)
            act.wait_ge(sem("gates_in"), 4)
            A(R_T, R_F, ACT.Abs).then_inc(sem("ls"), 1)
            act.wait_ge(sem("ls"), 1)
            A(R_T, R_T, ACT.Exp, scale=-1.0).then_inc(sem("ls"), 1)
            act.wait_ge(sem("ls"), 2)
            A(R_T, R_T, ACT.Ln, bias=1.0).then_inc(sem("ls"), 1)
            with act.Fori(0, 3) as i:
                for j in range(8):
                    split_hi(U_IN1 + 6 + j, i * 8)
            split_hi(U_IN1 + 30)
            act.wait_ge(sem("m_ready"), 1)
            A(R_E[:, 0:TP], R_E[:, 0:TP], ACT.Exp, scale=-1.0).then_inc(sem("gate_exp"), 1)
            A(m3[:], cst[0:64, 0:T], ACT.Copy, scale=0.0).then_inc(sem("m_hi"), 1)
            act.wait_ge(sem("m_hi"), 1)
            A(m3[0:H, 0:TP], R_M[:, 0:TP], ACT.Copy).then_inc(sem("m_hi"), 1)
            A(pick3[:], cst[0:64, C_HMASK:C_HMASK + 8], ACT.Copy).then_inc(sem("m_hi"), 1)
            act.wait_ge(sem("s_gates"), 1)
            A(R_E[:, TP:T], s8[:, 3, :], ACT.Exp).then_inc(sem("gate_exp"), 1)
            A(s8[:, 4:7, :], s8[:, 1:4, :], ACT.Exp).then_inc(sem("gate_exp"), 1)
            act.dma_start(m_prompt[0, 0].rearrange("(h o) -> h o", o=1), g8[:, 2:3]).then_inc(sem("stored"), 16)
            n_stored += 1


            def job_out(n):
                act.wait_ge(sem("jobs_in"), len(JOBS) + n + 1)
                name, t, half = JOBS1[n]
                cols = slice(512 * half, 512 * half + 512)
                dst = ts1[name][:, cols] if t == 2 else tk1[name][:, t, cols]
                A(dst, bank[4 + n % 4][0:dst.shape[0], :], ACT.Copy).then_inc(sem("jobs_out"), 1)


            for j in range(8):
                if j >= 1:
                    split_hi(U_IN1 + 30 + j)
                    job_out(2 * j - 2)
                    job_out(2 * j - 1)
                if j == 3:
                    act.wait_ge(sem("small_in"), 1)
                    A(acol[:].rearrange("p a b -> p (a b)"), bank[7][:, 0:16], ACT.Copy).then_inc(sem("small_out"), 1)
            act.wait_ge(sem("small_out"), 2)
            act.dma_start(m_sample[0], s8[:, 11, :]).then_inc(sem("stored"), 16)
            n_stored += 1


            def v_mask(b):
                if b == 0:
                    act.wait_ge(sem("rows_hi"), 5)
                    act.wait_ge(sem("rows_lo"), 3)
                if b >= 2:
                    act.wait_ge(sem("outer"), 2 * (b - 2) + 2)
                A(vm[b % 2][:], v3.bitcast(F32), ACT.Copy, scale=cst[0:96, C_HMASK + b:C_HMASK + b + 1]).then_inc(sem("v_masked"), 1)


            def head_out(h):
                b = bank[h % 2]
                act.wait_ge(sem("num_in"), h + 1)
                A(z1[:, 16 + h, 0:TP], b[:, 0:TP], ACT.Copy).then_inc(sem("head_out"), 1)
                A(z1[:, h, 0:TP], b[:, 0:TP], ACT.Square).then_inc(sem("head_sq"), 1)
                A(tk1["k"][:, 0, DC * h:DC * h + DC], b[:, 256:384], ACT.Copy).then_inc(sem("head_out"), 1)
                A(ncol[:, h:h + 1], b[:, 384:385], ACT.Copy).then_inc(sem("head_out"), 1)


            for h in range(H + 1):
                if h < H:
                    act.wait_ge(sem("e_arg"), 2 * h + 2)
                    A(ew[h % 2][:], ew[h % 2][:], ACT.Exp, scale=-1.0).then_inc(sem("e_done"), 1)
                    act.wait_ge(sem("e_done"), h + 1)
                    for t, c in ((0, 255), (1, 383)):
                        keys = tk1["k"][:, t, DC * h:DC * h + DC]
                        A(keys, keys, ACT.Copy, scale=ew[h % 2][:, c:c + 1]).then_inc(sem("k_weighted"), 1)
                    if h == 0:
                        act.wait_ge(sem("mm_done"), U_OUT1)
                        A(q3[0:NB, :], ts1["q"][:], ACT.Copy).then_inc(sem("rows_hi"), 1)
                        A(k3[0:NB, :], ts1["k"][:], ACT.Copy).then_inc(sem("rows_hi"), 1)
                        act.wait_ge(sem("v_weighted"), 1)
                        A(v3[0:NB, :], ts1["v"][:], ACT.Copy).then_inc(sem("rows_hi"), 1)
                        A(v3[32:32 + NB, :], ts1["v"][:], ACT.Copy).then_inc(sem("rows_hi"), 1)
                        A(k3[64:64 + NB, :], ts1["k"][:], ACT.Copy).then_inc(sem("rows_hi"), 1)
                    v_mask(h)
                    if h == 3:
                        act.wait_ge(sem("evac1_done"), 36)
                        A(z1[:, 24:32, :], z1[:, 24:32, :], ACT.Sigmoid).then_inc(sem("gate_act"), 1)
                if h >= 1:
                    head_out(h - 1)
            act.wait_ge(sem("head_ss"), 1)
            A(R_D[:, 0:TP], bank[7][0:H, 0:TP], ACT.Abs).then_inc(sem("den_in"), 1)
            act.wait_ge(sem("turned"), 1)
            A(R_D[:, TP:T], bank[2][0:H, 0:NB], ACT.Abs).then_inc(sem("den_in"), 1)
            act.wait_ge(sem("num_sample"), NB)
            A(z1[:, 0:8, TP:T], z1[:, 16:24, TP:T], ACT.Square).then_inc(sem("head_sq"), 1)
            rsqrt_seed("h1", 1, R_I, R_T, R_B)
            act.wait_ge(sem("head_out"), 3 * H)
            act.dma_start(C_prompt[0, 0].rearrange("h e d -> e h d"), tk1["k"][:, 0, :].rearrange("p (h d) -> p h d", h=H)
                          ).then_inc(sem("stored"), 16)
            act.wait_ge(sem("n_step"), 3)
            act.dma_start(n_sample[0].rearrange("b h d -> b (h d)"), ts1["n"][:]).then_inc(sem("stored"), 16)
            act.wait_ge(sem("turned"), 2)
            A(R_A[:, 0:DC], bank[3][0:H, 0:DC], ACT.Copy).then_inc(sem("n_row"), 1)
            act.wait_ge(sem("n_row"), 1)
            act.dma_start(n_prompt[0, 0], R_A[:, 0:DC]).then_inc(sem("stored"), 16)
            n_stored += 3
            for h in range(H):
                act.wait_ge(sem("mix1"), h + 1)
                A(actA[0][:, h, :], z1[:, 8 + h, :], ACT.Copy).then_inc(sem("mix1_hi"), 1)
            act.wait_ge(sem("stored"), 16 * n_stored)
            for c in range(CRING):
                act.wait_ge(sem(f"c_stored{c}"), 16 * ((NB - 1 - c) // CRING + 1))
            out_inputs(3, U_OUT1, G_FFN + 8)
            ffn_act(1, 3, U_UP1, U_DN1, None, None)
            n_stored += 3
            rsqrt_seed("rms", 5, var[:], nwt[:], rstd[:])
            for t in range(3):
                rows_t = NB if t == 2 else P
                dst = y_sample.rearrange("b o n -> (b o) n") if t == 2 else y_prompt[0, P * t:P * t + P]
                for half in range(2):
                    act.wait_ge(sem("x_t"), KT + 2 * t + half + 1)
                    A(y_rows[t][0:rows_t, 512 * half:512 * half + 512], bank[2 * t + half][0:rows_t, :], ACT.Copy).then_inc(sem("y_out"), 1)
                act.wait_ge(sem("y_out"), 2 * t + 2)
                act.dma_start(dst, y_rows[t][0:rows_t, :]).then_inc(sem("stored"), 16)
            n_stored += 3
            act.wait_ge(sem("stored"), 16 * n_stored)
            act.wait_ge(sem("row_stored"), 32)

        @block.vector
        def _(dve):
            V = nc.vector
            own = [0]

            def step(ins):
                ins.then_inc(sem("dve_step"), 1)
                own[0] += 1
                dve.wait_ge(sem("dve_step"), own[0])

            def split_lo(u, i8=0):
                if u >= U_END:
                    return
                dve.wait_ge(sem("hi_ready"), u + 1 + i8)
                nk = row_tiles(u)[1]
                V.tensor_tensor(wlo[u % RING][:, 0:nk, :], raw[u // 2 % RING][:, 0:nk, P * (u % 2):P * (u % 2) + P],
                                whi[u % RING][:, 0:nk, :].bitcast(F32), ALU.subtract).then_inc(sem("lo_ready"), 1)

            def norm_lo(stage, k, g, dst, i=0):
                dve.wait_ge(sem("norm_hi"), 8 * stage + k + 1 + i)
                V.scalar_tensor_tensor(dst[1][:, bass.ds(i + k, 1), :], x[:, bass.ds(i + k, 1), :],
                                       gains[:, bass.ds(g + k + i, 1)], dst[0][:, bass.ds(i + k, 1), :].bitcast(F32),
                                       ALU.mult, ALU.subtract).then_inc(sem("norm_lo"), 1)

            def newton(name, n, v, t, y):
                dve.wait_ge(sem(f"{name}_seed"), n)
                step(V.scalar_tensor_tensor(t, y, -0.5, y, ALU.mult, ALU.mult))
                step(V.tensor_tensor(t, t, v, ALU.mult))
                step(V.scalar_tensor_tensor(y, t, 1.5, y, ALU.add, ALU.mult))

            def rms(stage):
                dve.wait_ge(sem("ss_done"), stage + 1)
                V.tensor_scalar(var[:], bank[7][:, 0:T], 1.0 / D, EPS, ALU.mult, ALU.add).then_inc(sem("rms_var"), 1)
                dve.wait_ge(sem("rms_var"), stage + 1)
                newton("rms", stage + 1, var[:], nwt[:], rstd[:])

            for k in range(KT):
                dve.wait_ge(sem("x_t"), k + 1)
                V.tensor_copy(x[:, k, :], bank[k % 4][:, 0:T]).then_inc(sem("x_ready"), 1)
                if k >= 1:
                    norm_lo(0, k - 1, G_AB, actA)
            norm_lo(0, 7, G_AB, actA)
            split_lo(0)
            split_lo(1)
            split_lo(2)
            rms(0)

            dve.wait_ge(sem("const_landed"), 32)

            def rope(u):
                r = ROPED.index(u)
                dve.wait_ge(sem("swapped"), r + 1)
                V.scalar_tensor_tensor(smx[r % 2][:, 0:T], bank[4 + r % 2][:, 0:T], 1.0, sin, ALU.mult, ALU.mult
                                       ).then_inc(sem("sin_prod"), 1)
                dve.wait_ge(sem("sin_prod"), r + 1)
                dve.wait_ge(sem("cos_prod"), r + 1)
                V.tensor_tensor(z0[:, u, :], smx[r % 2][:, 0:T], rmk[r % 2][:, 0:T], ALU.add).then_inc(sem("roped"), 1)

            def k_sum(j):
                dve.wait_ge(sem("k_mult"), j + 1)
                V.tensor_reduce(sc_all[:, 2 * (j % 4):2 * (j % 4) + 2, j // 4, :],
                                kv[j % 4][:].rearrange("p t (h d) -> p t h d", h=H), AX, ALU.add).then_inc(sem("k_reduced"), 1)

            for u in range(28):
                split_lo(u + LOOK)
                dve.wait_ge(sem("mm_done"), u + 1)
                V.scalar_tensor_tensor(z0[:, u, :], bank[u % RING][:, 0:T], DA ** -0.5 if 16 <= u < 20 else 1.0, rstd[:],
                                       ALU.mult, ALU.mult).then_inc(sem("evac_done"), 1)
                if u - 1 in ROPED:
                    rope(u - 1)
                if u >= 10:
                    k_sum(u - 10)

            def own_scores():
                dve.wait_ge(sem("jobs_out"), len(JOBS))
                step(V.tensor_tensor(prd, tks["qa"][:], tks["ka"][:], ALU.mult))
                step(V.tensor_reduce(sm[0:NB, 70:78], prd.rearrange("p (h d) -> p h d", h=H), AX, ALU.add))
                V.tensor_tensor(dgs[:], eye8.unsqueeze(2).to_broadcast([NB, NB, H]),
                                sm[0:NB, 70:78].unsqueeze(1).to_broadcast([NB, NB, H]), ALU.mult).then_inc(sem("own_diag"), 1)

            def attn_max(h):
                s = h % 2
                dve.wait_ge(sem("attn_s"), h + 1)
                if h >= 2:
                    dve.wait_ge(sem("attn_pt"), h - 1)
                V.tensor_tensor(smx[s][:], bank[2 + h % 3][:, 0:384], cst[:, C_AMASK:C_AMASK + 384], ALU.add
                                ).then_inc(sem("attn_masked"), 1)
                dve.wait_ge(sem("attn_masked"), h + 1)
                V.tensor_reduce(sm[:, 0:1], smx[s][:, 0:128], AX, ALU.max)
                step(V.tensor_reduce(sm[:, 1:2], smx[s][:, 128:384], AX, ALU.max))
                V.tensor_scalar(sm[:, 4 + 2 * s:6 + 2 * s], sm[:, 0:2], -DA ** -0.5, None, ALU.mult).then_inc(sem("attn_nmax"), 1)

            def attn_norm(h):
                s = h % 2
                dve.wait_ge(sem("attn_exp"), 2 * h + 2)
                if h >= 2:
                    dve.wait_ge(sem("attn_p"), 2 * (h - 2) + 2)
                V.reciprocal(sm[:, 20 + 2 * s:22 + 2 * s], sm[:, 8 + 2 * s:10 + 2 * s]).then_inc(sem("attn_rcp"), 1)

            def attn_lo(c):
                dve.wait_ge(sem("attn_hi"), c + 1)
                V.tensor_tensor(actA[1][:, c, 0:TP], bank[c % 2][:, 0:TP], actA[0][:, c, 0:TP].bitcast(F32),
                                ALU.subtract).then_inc(sem("attn_lo"), 1)

            def ret_weights(h):
                dve.wait_ge(sem("ret_s"), h + 1)
                dve.wait_ge(sem("ret_mask"), h + 1)
                V.tensor_tensor(rmk[h % 2][:], bank[5][:, 0:384], rmk[h % 2][:], ALU.mult).then_inc(sem("ret_masked"), 1)

            for h in range(H):
                attn_max(h)
                if h >= 1:
                    attn_norm(h - 1)
                if h >= 4 and h % 2 == 0:
                    attn_lo((h - 4) // 2)
                if h == 0:
                    own_scores()
                else:
                    k_sum(16 + 2 * h)
                if h >= 2:
                    ret_weights(h - 2)
                if h >= 1:
                    k_sum(17 + 2 * h)
            attn_norm(H - 1)
            ret_weights(H - 2)
            ret_weights(H - 1)
            attn_lo(2)
            attn_lo(3)

            for t in range(2):
                V.tensor_tensor(kdec[:, t, :].rearrange("p (h d) -> p h d", h=H), tok["kb"][:, t, :].rearrange("p (h d) -> p h d", h=H),
                                cst[:, C_RDEC + 8 * t:C_RDEC + 8 * t + 8].unsqueeze(2).to_broadcast([P, H, DA]),
                                ALU.mult).then_inc(sem("k_decayed"), 1)
            dve.wait_ge(sem("samp_rows"), 2)
            blocks = prow.rearrange("p (n k) -> p n k", n=NBLK)
            gate = sm[0:64, 12:16]
            V.tensor_reduce(sm[0:64, 16:20], blocks, AX, ALU.max)
            step(V.tensor_reduce(gate, blocks, AX, ALU.add))
            dve.wait_ge(sem("own_s"), 1)
            V.tensor_copy(sm[0:64, 68:69], bank[7][0:64, 0:1]).then_inc(sem("own_in"), 1)
            for n in range(NBLK):
                if n:
                    V.tensor_scalar(sm[0:64, 40 + 4 * n:40 + 5 * n], gate[:, 0:n], gate[:, n:n + 1], None, ALU.is_ge)
                last = V.tensor_scalar(sm[0:64, 40 + 5 * n:44 + 4 * n], gate[:, n:NBLK], gate[:, n:n + 1], None, ALU.is_gt)
            step(last)
            step(V.tensor_reduce(sm[0:64, 56:60], sm[0:64, 40:56].rearrange("p (n m) -> p n m", n=NBLK), AX, ALU.add))
            step(V.tensor_scalar(sm[0:64, 60:64], sm[0:64, 56:60], TOPK - 0.5, -BIG, ALU.is_gt, ALU.mult))
            dve.wait_ge(sem("own_in"), 1)
            step(V.tensor_tensor(sm[0:64, 64:68], sm[0:64, 60:64], sm[0:64, 16:20], ALU.add))
            step(V.tensor_reduce(sm[0:64, 69:70], sm[0:64, 64:69], AX, ALU.max))
            step(V.tensor_scalar(sm[0:64, 28:29], sm[0:64, 69:70], -DA ** -0.5, None, ALU.mult))
            V.tensor_scalar(sm[0:64, 24:28], sm[0:64, 60:64], sm[0:64, 28:29], None, ALU.add).then_inc(sem("samp_bias"), 1)

            def state_new(c):
                dve.wait_ge(sem("kv_outer"), 2 * c + 2)
                s0c = s0[:, c, :, :].rearrange("p b e -> p (b e)")
                V.scalar_tensor_tensor(s0c, s0c, cst[:, C_GAM + c:C_GAM + c + 1], bank[c][:, :], ALU.mult, ALU.add
                                       ).then_inc(sem("s_new"), 1)

            dve.wait_ge(sem("samp_exp"), 5)
            step(V.tensor_reduce(sm[0:64, 37:38], sm[0:64, 32:37], AX, ALU.add))
            step(V.reciprocal(sm[0:64, 38:39], sm[0:64, 37:38]))
            V.tensor_scalar(sm[0:64, 39:40], sm[0:64, 36:37], sm[0:64, 38:39], None, ALU.mult).then_inc(sem("samp_p"), 1)
            V.tensor_scalar(prow, prow, sm[0:64, 38:39], None, ALU.mult).then_inc(sem("samp_p"), 1)
            dve.wait_ge(sem("own_s"), 2)
            V.tensor_tensor(dgp[:], bank[7][0:NB, 0:64].rearrange("p (b h) -> p b h", b=NB),
                            eye8.unsqueeze(2).to_broadcast([NB, NB, H]), ALU.mult).then_inc(sem("own_p_diag"), 1)
            dve.wait_ge(sem("s0_landed"), 16 * NB)
            for c in range(4):
                state_new(c)
            dve.wait_ge(sem("ret_o"), 2)
            for q in range(2):
                V.tensor_copy(z0[64 * q:64 * q + 64, 8:12, TP:T],
                              bank[4 + q][64 * q:64 * q + 64, 0:32].rearrange("p (c b) -> p c b", c=4)).then_inc(sem("ob_sample"), 1)
            for c in range(4):
                dve.wait_ge(sem("ret_ss"), c + 1)
                V.tensor_scalar(z0[:, 4 + c, :], bank[c][:, 0:T], 1.0 / DA, EPS, ALU.mult, ALU.add).then_inc(sem("ret_var"), 1)
            dve.wait_ge(sem("ret_var"), 4)
            newton("ret", 1, z0[:, 4:8, :], z0[:, 0:4, :], z0[:, 20:24, :])
            dve.wait_ge(sem("ob_gated"), 1)
            for c in range(4):
                V.scalar_tensor_tensor(z0[:, c, :], z0[:, 24 + c, :], gains[:, G_RET + c:G_RET + c + 1], z0[:, 20 + c, :],
                                       ALU.mult, ALU.mult).then_inc(sem("ret_mix"), 1)
            for c in range(4):
                dve.wait_ge(sem("ret_hi"), c + 1)
                V.tensor_tensor(actA[1][:, 4 + c, :], z0[:, c, :], actA[0][:, 4 + c, :].bitcast(F32), ALU.subtract
                                ).then_inc(sem("mix_lo"), 1)
            dve.wait_ge(sem("v_used"), 32)
            for t in range(2):
                V.tensor_tensor(ovv[:, t, :].rearrange("p (h d) -> p h d", h=H), bank[6 + t][:, :].rearrange("p (h d) -> p h d", h=H),
                                cst[:, C_HMASK:C_HMASK + 8].unsqueeze(2).to_broadcast([P, H, DA]), ALU.mult).then_inc(sem("samp_own"), 1)
            dve.wait_ge(sem("samp_hi"), 1)
            V.tensor_tensor(actA[1][:, 0:4, TP:T], bank[5][:, 0:32].rearrange("p (c b) -> p c b", c=4),
                            actA[0][:, 0:4, TP:T].bitcast(F32), ALU.subtract).then_inc(sem("mix_lo"), 1)

            def residual(stage, e, d, g, dst, i=0):
                V.tensor_tensor(x[:, bass.ds(d + i, 1), :], x[:, bass.ds(d + i, 1), :], bank[e % RING][:, 0:T].unsqueeze(1),
                                ALU.add).then_inc(sem("x_ready"), 1)

            def out_proj(stage, u0, e0, g, dst):
                for n in range(8):
                    split_lo(u0 + n + LOOK)
                    dve.wait_ge(sem("mm_done"), u0 + n + 1)
                    residual(stage, e0 + n, n, g, dst)
                    if n >= 1:
                        norm_lo(stage, n - 1, g, dst)

                norm_lo(stage, 7, g, dst)

            out_proj(1, U_OUT0, E_OUT0, G_FFN, actB)

            def ffn_dve(l, stage, u_up, u_dn, e_up, e_dn, g_next, dst_next):
                split_lo(u_up + LOOK)
                rms(stage)
                w = [convp[l][:, j, :].unsqueeze(1).to_broadcast([P, NB, FT]) for j in range(4)]
                step(V.tensor_tensor(ffp[:], convb[l][:, :, 0, :], w[0], ALU.mult))
                step(V.tensor_tensor(ffq[:], convb[l][:, :, 1, :], w[1], ALU.mult))
                step(V.tensor_tensor(ffp[:], ffp[:], ffq[:], ALU.add))
                step(V.tensor_tensor(ffp[:], ffp[:], w[3], ALU.add))

                def scaled(u, dst, name, i8, f=None, i4=0):
                    dve.wait_ge(sem("mm_done"), u + 1 + i8)
                    V.tensor_tensor(dst, bank[(u - u_up + e_up) % RING][:, 0:T], rstd[:], ALU.mult).then_inc(sem(name), 1)

                def conv(f, i4, fd):
                    a, t = ffa[f % 4], fft[f % 4]
                    w1, w2 = (convp[l][:, j, bass.ds(fd, 1)] for j in (1, 2))
                    dve.wait_ge(sem("a_ready"), f + 1 + i4 + FT * l)
                    dve.wait_ge(sem("tap"), f + 1 + i4 + FT * l)
                    V.scalar_tensor_tensor(t[:, TP:T], a[:, 2 + TP:2 + T], w2, ffp[:, :, bass.ds(fd, 1)].rearrange("p b o -> p (b o)"),
                                           ALU.mult, ALU.add)
                    V.scalar_tensor_tensor(t[:, 0:TP], a[:, 1:1 + TP], w1, t[:, 0:TP], ALU.mult, ALU.add).then_inc(sem("tap1"), 1)
                    dve.wait_ge(sem("tap1"), f + 1 + i4 + FT * l)
                    V.scalar_tensor_tensor(t[:, 0:TP], a[:, 2:2 + TP], w2, t[:, 0:TP], ALU.mult, ALU.add).then_inc(sem("conv"), 1)

                def h_lo(f, i4, fd):
                    dve.wait_ge(sem("h_hi"), f + 1 + i4 + FT * l)
                    V.tensor_tensor(hff[1][:, bass.ds(fd, 1), :], ffg[f % 4][:].unsqueeze(1), hff[0][:, bass.ds(fd, 1), :].bitcast(F32),
                                    ALU.subtract).then_inc(sem("h_lo"), 1)

                def group(f, u, i4, i8, fd, first=0):
                    if first < 2:
                        split_lo(u + LOOK, i8)
                    if first < 1:
                        dve.wait_ge(sem("a_kept"), f - 2 + i4 + FT * l)
                    scaled(u, ffa[f % 4][:, 2:2 + T], "a_ready", i8)
                    split_lo(u + LOOK + 1, i8)
                    scaled(u + 1, ffa[(f + 1) % 4][:, 2:2 + T], "a_ready", i8)
                    conv(f, i4, fd)
                    split_lo(u + LOOK + 2, i8)
                    scaled(u + 2, ffg[f % 4][:], "g_ready", i8)
                    conv(f + 1, i4, fd + 1)
                    if first < 2:
                        h_lo(f - 2, i4, fd - 2)
                    split_lo(u + LOOK + 3, i8)
                    scaled(u + 3, ffg[(f + 1) % 4][:], "g_ready", i8)
                    if first < 2:
                        h_lo(f - 1, i4, fd - 1)

                group(0, u_up, 0, 0, 0, 2)
                with dve.Fori(0, 5) as i:
                    group(2, u_up + 4, i * 4, i * 8, i * 4 + 2)
                    group(4, u_up + 8, i * 4, i * 8, i * 4 + 4)

                for c in range(4):
                    for j in range(8):
                        split_lo(u_dn + 8 * c + j + LOOK)
                        if c == 0 and j == 1:
                            h_lo(FT - 2, 0, FT - 2)
                            h_lo(FT - 1, 0, FT - 1)
                        if j >= 6:
                            dve.wait_ge(sem("mm_done"), u_dn + 8 * c + j + 1)
                            residual(stage + 1, e_dn + 2 * c + j - 6, 2 * c + j - 6, g_next, dst_next)
                            if g_next is not None and 2 * c + j - 6 >= 1:
                                norm_lo(stage + 1, 2 * c + j - 7, g_next, dst_next)
                if g_next is not None:
                    norm_lo(stage + 1, 7, g_next, dst_next)

            ffn_dve(0, 1, U_UP0, U_DN0, E_UP0, E_DN0, G_C, actA)
            split_lo(U_IN1 + 3)
            rms(2)
            dve.wait_ge(sem("c_small"), 64)
            V.memset(qkv_scale[:, 0:3:2], 1.0)
            V.memset(qkv_scale[:, 1:2], DC ** -0.5).then_inc(sem("evac1_done"), 2)
            for t, r in ((0, R_I), (1, R_F)):
                dve.wait_ge(sem("mm_done"), U_IN1 + t + 1)
                V.tensor_tensor(r, bank[(E_IN1 + t) % RING][0:H, 0:T], rstd[0:H, :], ALU.mult).then_inc(sem("evac1_done"), 1)
                if t == 0:
                    split_lo(U_IN1 + 4)
            dve.wait_ge(sem("evac1_done"), 4)
            for t, r in ((0, R_I), (1, R_F)):
                V.tensor_scalar(r, r, g8[:, t:t + 1], None, ALU.add).then_inc(sem("gates_in"), 2)


            def in1(e, c, scale, i8=0):
                dve.wait_ge(sem("mm_done"), U_IN1 + e + 1 + i8)
                V.scalar_tensor_tensor(z1[:, bass.ds(c, 1), :], bank[(E_IN1 + e) % RING][:, 0:T].unsqueeze(1), scale,
                                       rstd[:].unsqueeze(1), ALU.mult, ALU.mult).then_inc(sem("evac1_done"), 1)


            with dve.Fori(0, 3) as i:
                for j in range(8):
                    split_lo(U_IN1 + 5 + j, i * 8)
                    in1(2 + j, i * 8 + j, qkv_scale[:, bass.ds(i, 1)], i * 8)
            dve.wait_ge(sem("gates_in"), 4)
            dve.wait_ge(sem("ls"), 3)
            step(V.scalar_tensor_tensor(R_T, R_F, 0.0, R_T, ALU.min, ALU.subtract))
            step(V.tensor_tensor(s8[:, 1, :], R_T[:, TP:T], s8[:, 0, :], ALU.add))
            step(V.tensor_tensor(s8[:, 7, :], s8[:, 1, :], R_I[:, TP:T], ALU.max))
            V.tensor_tensor(s8[:, 2, :], R_I[:, TP:T], s8[:, 7, :], ALU.subtract)
            V.tensor_scalar(s8[:, 3, :], s8[:, 7, :], -1.0, EXP_MAX, ALU.mult, ALU.min)
            V.tensor_tensor(s8[:, 1, :], s8[:, 1, :], s8[:, 7, :], ALU.subtract).then_inc(sem("s_gates"), 1)
            split_lo(U_IN1 + 29)
            one_row = ones[0:H, 0:1].to_broadcast([H, TP])
            step(V.tensor_tensor_scan(R_B[:, 0:TP], one_row, R_T[:, 0:TP], 0.0, ALU.mult, ALU.add))
            step(V.tensor_tensor(R_A[:, 0:TP], R_I[:, 0:TP], R_B[:, 0:TP], ALU.subtract))
            step(V.tensor_tensor_scan(R_M[:, 0:TP], one_row, R_A[:, 0:TP], 0.0, ALU.mult, ALU.max))
            step(V.tensor_tensor(R_B[:, 0:TP], R_B[:, 0:TP], R_M[:, 0:TP], ALU.add))
            V.tensor_copy(g8[:, 2:3], R_B[:, TP - 1:TP])
            V.tensor_scalar(R_E[:, 0:TP], R_B[:, 0:TP], -EXP_MAX, None, ALU.max).then_inc(sem("m_ready"), 1)
            for j in range(8):
                if j:
                    split_lo(U_IN1 + 29 + j)
                in1(26 + j, 24 + j, 1.0)
                if j == 0:
                    dve.wait_ge(sem("m_hi"), 2)
                    V.tensor_tensor(m3[32:32 + H, 0:TP], R_M[:, 0:TP], m3[0:H, 0:TP].bitcast(F32), ALU.subtract).then_inc(sem("m_lo"), 1)
                if j == 4:
                    dve.wait_ge(sem("small_in"), 2)
                    V.tensor_copy(s8[:, 8:12, :].rearrange("p a b -> p (a b)"), bank[7][0:NB, 0:32]).then_inc(sem("small_out"), 1)
                    dve.wait_ge(sem("small_out"), 2)
                    V.tensor_tensor(dd[:], eye8.unsqueeze(2).to_broadcast([NB, NB, H]), s8[:, 8, :].unsqueeze(1).to_broadcast([NB, NB, H]),
                                    ALU.mult).then_inc(sem("dec_diag"), 1)
                if j == 5:
                    dve.wait_ge(sem("small_in"), 3)
                    V.tensor_copy(decb[:].rearrange("p b h -> p (b h)"), bank[7][:, 0:64]).then_inc(sem("small_out"), 1)
            dve.wait_ge(sem("small_out"), 1)


            def head_exponent(h):
                dve.wait_ge(sem("m_b"), h + 1)
                if h >= 2:
                    dve.wait_ge(sem("k_weighted"), 2 * (h - 2) + 2)
                e, mb = ew[h % 2], bank[3]
                V.scalar_tensor_tensor(e[:, 0:256], mb[:, 0:256], acol[:, 0, h:h + 1], cst[:, C_MMASK:C_MMASK + 256],
                                       ALU.subtract, ALU.max).then_inc(sem("e_arg"), 1)
                V.scalar_tensor_tensor(e[:, 256:384], mb[:, 128:256], acol[:, 1, h:h + 1], cst[:, C_MMASK + 256:C_MMASK + 384],
                                       ALU.subtract, ALU.max).then_inc(sem("e_arg"), 1)


            def head_weights(h):
                dve.wait_ge(sem("m_s"), h + 1)
                dve.wait_ge(sem("e_done"), h + 1)
                if h >= 2:
                    dve.wait_ge(sem("num_in"), h - 1)
                V.tensor_tensor(ww[h % 2], bank[2][:, 0:384], ew[h % 2][:], ALU.mult).then_inc(sem("w_ready"), 1)


            def c_update(b):
                c = cs[b % CRING][:].rearrange("p h d -> p (h d)")
                dve.wait_ge(sem("c_decayed"), b + 1)
                for half in range(2):
                    cols = slice(512 * half, 512 * half + 512)
                    dve.wait_ge(sem("outer"), 2 * b + half + 1)
                    V.tensor_tensor(c[:, cols], c[:, cols], bank[seq_bank(b, half)][:, :], ALU.add).then_inc(sem("c_added"), 1)


            def c_products(b):
                c = cs[b % CRING][:].rearrange("p h d -> p (h d)")
                for half in range(2):
                    cols = slice(512 * half, 512 * half + 512)
                    dve.wait_ge(sem("q_b"), 2 * b + half + 1)
                    dve.wait_ge(sem("c_added"), 2 * b + half + 1)
                    if b >= 1:
                        dve.wait_ge(sem("num_sample"), b)
                    V.tensor_tensor(prod[:, cols], c[:, cols], bank[seq_bank(b, 2 + half)][:, :], ALU.mult).then_inc(sem("q_mult"), 1)


            def c_numerators(b):
                dve.wait_ge(sem("q_mult"), 2 * b + 2)
                V.tensor_reduce(z1[:, 16:24, TP + b], prod[:].rearrange("p (h d) -> p h d", h=H), AX, ALU.add).then_inc(sem("num_sample"), 1)


            def rows_lo(n, name, dst, src):
                dve.wait_ge(sem("rows_hi"), n)
                V.tensor_tensor(dst, ts1[name][:], src.bitcast(F32), ALU.subtract).then_inc(sem("rows_lo"), 1)


            head_exponent(0)
            head_weights(0)
            rows_lo(1, "q", q3[32:32 + NB, :], q3[0:NB, :])
            rows_lo(2, "k", k3[32:32 + NB, :], k3[0:NB, :])
            rows_lo(3, "v", v3[64:64 + NB, :], v3[0:NB, :])
            dve.wait_ge(sem("n_step"), 4)
            V.tensor_reduce(s8[:, 12, :], prod[0:NB, :].rearrange("p (h d) -> p h d", h=H), AX, ALU.add).then_inc(sem("den_sample"), 1)
            dve.wait_ge(sem("den_sample"), 1)
            for h in range(H):
                if h + 1 < H:
                    head_exponent(h + 1)
                c_update(h)
                if h + 1 < H:
                    head_weights(h + 1)
                c_products(h)
                c_numerators(h)
            dve.wait_ge(sem("den_in"), 2)
            step(V.tensor_tensor(R_D, R_D, R_E, ALU.max))
            step(V.scalar_tensor_tensor(R_D, R_D, EPS, R_D, ALU.mult, ALU.mult))
            dve.wait_ge(sem("head_ss"), 2)
            V.scalar_tensor_tensor(R_I[:, 0:TP], bank[7][0:H, 256:512], 1.0 / DC, R_D[:, 0:TP], ALU.mult, ALU.add)
            V.scalar_tensor_tensor(R_I[:, TP:T], bank[4][0:H, 0:NB], 1.0 / DC, R_D[:, TP:T], ALU.mult, ALU.add).then_inc(sem("h1_var"), 1)
            newton("h1", 1, R_I, R_T, R_B)
            step(V.tensor_copy(m3[0:H, :], R_B))
            V.tensor_tensor(m3[32:32 + H, :], R_B, m3[0:H, :].bitcast(F32), ALU.subtract).then_inc(sem("h1_rstd"), 1)


            def mix_lo(h):
                dve.wait_ge(sem("mix1_hi"), h + 1)
                V.tensor_tensor(actA[1][:, h, :], z1[:, 8 + h, :], actA[0][:, h, :].bitcast(F32), ALU.subtract).then_inc(sem("mix1_lo"), 1)


            for h in range(H):
                dve.wait_ge(sem("rstd_b"), h + 1)
                dve.wait_ge(sem("o1_gated"), h // 4 + 1)
                V.scalar_tensor_tensor(z1[:, 8 + h, :], z1[:, 24 + h, :], gains[:, G_OUT + h:G_OUT + h + 1], bank[h % 4][:, 0:T],
                                       ALU.mult, ALU.mult).then_inc(sem("mix1"), 1)
                if h:
                    mix_lo(h - 1)
            mix_lo(H - 1)
            out_proj(3, U_OUT1, E_OUT1, G_FFN + 8, actB)
            ffn_dve(1, 3, U_UP1, U_DN1, E_UP1, E_DN1, None, None)
            rms(4)
            for k in range(KT):
                V.scalar_tensor_tensor(sq[:, k, :], x[:, k, :], gains[:, G_FIN + k:G_FIN + k + 1], rstd[:], ALU.mult, ALU.mult
                                       ).then_inc(sem("y_scaled"), 1)
        @block.tensor
        def _(pe):
            M = nc.tensor.matmul
            TR = nc.tensor.transpose
            last_reader = {}

            def claim(b, name, value):
                if b in last_reader:
                    pe.wait_ge(*last_reader[b])
                last_reader[b] = (sem(name), value)

            def unit(u, b, src, k0=0, nk=8, first=True, last=True, i8=0, ready=None):
                pe.wait_ge(sem("lo_ready"), u + 1 + i8)
                hi, lo = whi[u % RING], wlo[u % RING]
                for k in range(nk):
                    if ready is not None:
                        pe.wait_ge(sem(ready[0]), ready[1] + k + 1)
                    M(bank[b][:, 0:T], hi[:, k, :], src[0][:, k0 + k, :], start=first and k == 0, stop=False)
                    M(bank[b][:, 0:T], hi[:, k, :], src[1][:, k0 + k, :], start=False, stop=False)
                    ins = M(bank[b][:, 0:T], lo[:, k, :], src[0][:, k0 + k, :], start=False, stop=last and k == nk - 1)
                ins.then_inc(sem("mm_done"), 1)

            def sum_squares(stage):
                claim(7, "rms_var", stage + 1)
                if stage:
                    pe.wait_ge(sem("sq_added"), 7 * stage)
                for k in range(1 if stage else KT):
                    pe.wait_ge(sem("sq_ready"), 8 * stage + k + 1)
                    ins = M(bank[7][:, 0:T], ones[:], sq[:, k, :], start=k == 0, stop=bool(stage) or k == KT - 1)
                ins.then_inc(sem("ss_done"), 1)

            pe.wait_ge(sem("const_landed"), 16)
            pe.wait_ge(sem("x_landed"), 16 * 9)
            claim(4, "param_out", 1)
            TR(bank[4][:, 0:52], vec_rows, ident[0:52, 0:52]).then_inc(sem("param_t"), 1)
            for k in range(KT):
                claim(k % 4, "x_ready", k + 1)
                for t in range(2):
                    TR(bank[k % 4][:, P * t:P * t + P], x_tok[:, t, P * k:P * k + P], ident)
                TR(bank[k % 4][:, TP:T], xs_tok[:, P * k:P * k + P], ident[0:NB, 0:NB]).then_inc(sem("x_t"), 1)
            pe.wait_ge(sem("ones_ready"), 1)

            def job(n):
                claim(6 + n % 2, "jobs_out", n + 1)
                b, what = bank[6 + n % 2], JOBS[n]
                if what[0] == "b":
                    pe.wait_ge(sem("jobs_out"), 1)
                    M(b[:, :], eye8[:, what[1]:what[1] + 1].to_broadcast([NB, P]), tks["qa"][:], start=True, stop=True
                      ).then_inc(sem("jobs_in"), 1)
                    return
                name, t = what[1:]
                if TILE0[name] + 3 in ROPED:
                    pe.wait_ge(sem("roped"), ROPED.index(TILE0[name] + 3) + 1)
                else:
                    pe.wait_ge(sem("evac_done"), TILE0[name] + 4)
                for c in range(4):
                    if t < 2:
                        ins = TR(b[:, P * c:P * c + P], zt(name, c, P * t, P * t + P), ident)
                    else:
                        ins = TR(b[0:NB, P * c:P * c + P], zt(name, c, TP, T), ident)
                ins.then_inc(sem("jobs_in"), 1)

            for u in range(28):
                claim(u % RING, "evac_done", u + 1)
                unit(u, u % RING, actA, ready=("norm_lo", 0) if u == 0 else None)
                if u == 0:
                    sum_squares(0)
                    pe.wait_ge(sem("param_landed"), 16 * 12)
                    claim(4, "param_out", 3)
                    for l in range(2):
                        ins = TR(bank[4][:, 64 + 96 * l:152 + 96 * l], cw_rows[l], ident[0:88, 0:88])
                    ins.then_inc(sem("param_t"), 1)
                    for l in range(2):
                        claim(5 + l, "param_out", 4 + l)
                        for q in range(4):
                            ins = TR(bank[5 + l][:, 88 * q:88 * q + 88], cb_rows[l][:, q, :], ident[0:88, 0:88])
                        ins.then_inc(sem("param_t"), 1)
                if u - 1 in ROPED:
                    r = ROPED.index(u - 1)
                    claim(4 + r % 2, "sin_prod", r + 1)
                    pe.wait_ge(sem("evac_done"), u)
                    M(bank[4 + r % 2][:, 0:T], perm, z0[:, u - 1, :], start=True, stop=True).then_inc(sem("swapped"), 1)
                for n in range(jobs_until(u - 1), jobs_until(u)):
                    job(n)

            def attn_s(h):
                c, r = h // 2, 64 * (h % 2)
                claim(2 + h % 3, "attn_masked", h + 1)
                q, k = z0[r:r + 64, c, :], z0[r:r + 64, 4 + c, :]
                M(bank[2 + h % 3][:, 0:128], q[:, 0:128], k[:, 0:128], start=True, stop=True)
                M(bank[2 + h % 3][:, 128:384], q[:, 128:256], k[:, 0:256], start=True, stop=True).then_inc(sem("attn_s"), 1)

            def attn_p(h):
                claim(6, "attn_pt_out", h + 1)
                pe.wait_ge(sem("attn_p"), 2 * h + 2)
                for t in range(3):
                    ins = TR(bank[6][:, P * t:P * t + P], smx[h % 2][:, P * t:P * t + P], ident)
                ins.then_inc(sem("attn_pt"), 1)

            def causal_pv(out, v0, v1, p):
                M(out[:, 0:128], v0, p[:, 0:128], start=True, stop=True)
                M(out[:, 128:256], v0, p[:, 128:256], start=True, stop=False)
                return M(out[:, 128:256], v1, p[:, 256:384], start=False, stop=True)

            def attn_pv(h):
                c, r = h // 2, 64 * (h % 2)
                if h % 2 == 0:
                    claim(c % 2, "attn_lo", c + 1)
                pe.wait_ge(sem("attn_pt_out"), h + 1)
                v = tok["va"]
                causal_pv(bank[c % 2][r:r + 64, :], v[:, 0, DA * h:DA * h + DA], v[:, 1, DA * h:DA * h + DA], ptt[h % 2]
                          ).then_inc(sem("attn_pv"), 1)

            def ret_s(h):
                c, r = h // 2, 64 * (h % 2)
                claim(5, "ret_masked", h + 1)
                q, k = zt("qb", c)[r:r + 64, :], zt("kb", c)[r:r + 64, :]
                M(bank[5][:, 0:256], k[:, 0:128], q[:, 0:256], start=True, stop=True)
                M(bank[5][:, 256:384], k[:, 128:256], q[:, 128:256], start=True, stop=True).then_inc(sem("ret_s"), 1)

            def ret_pv(h):
                c, r = h // 2, 64 * (h % 2)
                if h % 2 == 0:
                    claim(7, "ob_prompt", c + 1)
                pe.wait_ge(sem("ret_masked"), h + 1)
                v = tok["vb"]
                causal_pv(bank[7][r:r + 64, :], v[:, 0, DA * h:DA * h + DA], v[:, 1, DA * h:DA * h + DA], rmk[h % 2]
                          ).then_inc(sem("ret_pv"), 1)

            pe.wait_ge(sem("jobs_out"), len(JOBS))
            for h in range(3):
                attn_s(h)
            for h in range(1, H + 1):
                if h >= 3:
                    ret_pv(h - 3)
                attn_p(h - 1)
                if h + 2 < H:
                    attn_s(h + 2)
                if h >= 2:
                    attn_pv(h - 2)
                ret_s(h - 1)
            attn_pv(H - 1)
            ret_pv(H - 2)
            ret_pv(H - 1)

            pe.wait_ge(sem("k_reduced"), 32)
            for t in range(2):
                claim(4 + t, "samp_rows", t + 1)
                for g in range(4):
                    ins = TR(bank[4 + t][0:64, P * g:P * g + P], sc_all[:, 4 * t + g, :, :].rearrange("p b h -> p (b h)"), ident)
                ins.then_inc(sem("samp_st"), 1)
            claim(7, "own_in", 1)
            pe.wait_ge(sem("own_diag"), 1)
            M(bank[7][0:64, 0:1], dgs[:].rearrange("p b h -> p (b h)"), ones[0:NB, 0:1], start=True, stop=True).then_inc(sem("own_s"), 1)
            def ret_state():
                claim(3, "ret_state_out", 1)
                pe.wait_ge(sem("k_decayed"), 2)
                for h in range(H):
                    for t in range(2):
                        ins = M(bank[3][0:64, DA * h:DA * h + DA], kdec[:, t, DA * h:DA * h + DA],
                                tok["vb"][:, t, DA * h:DA * h + DA], start=t == 0, stop=t == 1)
                ins.then_inc(sem("ret_state"), 1)

            def state_update(h):
                c, r = h // 2, 64 * (h % 2)
                if h % 2 == 0:
                    claim(c, "s_new", c + 1)
                pe.wait_ge(sem("v_diag"), h + 1)
                M(bank[c][r:r + 64, :], tks["kb"][:, DA * h:DA * h + DA], vdg[h % 2].rearrange("p b e -> p (b e)"),
                  start=True, stop=True).then_inc(sem("kv_outer"), 1)

            def ret_o(q, c):
                if c == 0:
                    pe.wait_ge(sem("s_new"), 4)
                    claim(4 + q, "ob_sample", q + 1)
                r = slice(64 * q, 64 * q + 64)
                for b in range(NB):
                    ins = M(bank[4 + q][r, 8 * c + b:8 * c + b + 1], s0[r, c, b, :], zt("qb", c)[r, TP + b:TP + b + 1],
                            start=True, stop=True)
                if c == 3:
                    ins.then_inc(sem("ret_o"), 1)

            def ret_squares(c):
                pe.wait_ge(sem("ret_sq"), 1)
                claim(c, "ret_var", c + 1)
                M(bank[c][:, 0:T], bones, z0[:, c, :], start=True, stop=True).then_inc(sem("ret_ss"), 1)

            ret_state()
            for h in range(4):
                state_update(h)
            claim(7, "own_p_diag", 1)
            pe.wait_ge(sem("samp_p"), 1)
            M(bank[7][0:NB, 0:64], sm[0:64, 39:40].to_broadcast([64, NB]), ident[0:64, 0:64], start=True, stop=True).then_inc(sem("own_s"), 1)
            claim(6, "samp_pt_out", 1)
            pe.wait_ge(sem("samp_p"), 2)
            for g in range(NPAGE):
                ins = TR(bank[6][:, 64 * g:64 * g + 64], prow[:, P * g:P * g + P], ident[0:64, 0:64])
            ins.then_inc(sem("samp_pt"), 1)

            claim(6, "samp_own", 1)
            claim(7, "samp_own", 2)
            pe.wait_ge(sem("own_p_diag"), 1)
            pe.wait_ge(sem("samp_pt_out"), 1)
            for j in range(32):
                b, r = j // 4, 32 * (j // 4 % 4)
                out = bank[6 + b // 4][r:r + H, :]
                if j % 4 == 0:
                    M(out, dgp[:, b, :], tks["va"][:], start=True, stop=False)
                pe.wait_ge(sem(f"kv_landed{j % 4}"), 32 * (8 + b + 1))
                for t in range(2):
                    g = 2 * (j % 4) + t
                    ins = M(out, pts[:, g, 8 * b:8 * b + 8], kv[j % 4][:, t, :], start=False, stop=g == NPAGE - 1)
                ins.then_inc(sem("v_used"), 1)
                if j < 4:
                    state_update(4 + j)
                elif 5 <= j < 13:
                    ret_o((j - 5) // 4, (j - 5) % 4)
                elif 15 <= j < 19:
                    ret_squares(j - 15)
            claim(5, "mix_lo", 5)
            pe.wait_ge(sem("samp_own"), 2)
            for t in range(2):
                for c in range(4):
                    ins = M(bank[5][:, 8 * c + 4 * t:8 * c + 4 * t + 4], ovv[:, t, P * c:P * c + P],
                            cst[:, C_QSEL:C_QSEL + 4], start=True, stop=True)
            ins.then_inc(sem("samp_o"), 1)

            def out_proj(stage, u0, e0, ready=None):
                for n in range(8):
                    b = (e0 + n) % RING
                    claim(b, "x_ready", 8 * stage + n + 1)
                    unit(u0 + n, b, actA, ready=ready if n == 0 else None)

            pe.wait_ge(sem("mix_lo"), 5)
            pe.wait_ge(sem("attn_lo"), 4)
            out_proj(1, U_OUT0, E_OUT0)

            def ffn_pe(l, stage, u_up, u_dn, e_up, e_dn):
                def group(f, v, i4, i8, first=False):
                    for j in range(4):
                        name = "a_ready" if j < 2 else "g_ready"
                        b = (e_up + v + j) % RING
                        if first:
                            claim(b, name, FT * l + 1)
                        else:
                            pe.wait_ge(sem(name), FT * l + f + j % 2 - 1 + i4)
                        unit(u_up + v + j, b, actB, i8=i8, ready=("norm_lo", 8 * stage) if first and j == 0 else None)
                        if first and j == 0:
                            sum_squares(stage)
                group(0, 0, 0, 0, True)
                with pe.Fori(0, 5) as i:
                    group(2, 4, i * 4, i * 8)
                    group(4, 8, i * 4, i * 8)
                for j in range(4):
                    last_reader[(e_up + 40 + j) % RING] = (sem("a_ready" if j < 2 else "g_ready"), FT * l + 21 + j % 2)
                for c in range(4):
                    for g, (k0, nk) in enumerate(KGROUPS):
                        for t in range(2):
                            b = (e_dn + 2 * c + t) % RING
                            if g == 0:
                                claim(b, "x_ready", 8 * (stage + 1) + 2 * c + t + 1)
                            if c == 0 and t == 0:
                                pe.wait_ge(sem("h_lo"), k0 + nk + FT * l)
                            unit(u_dn + 8 * c + 2 * g + t, b, hff, k0, nk, first=g == 0, last=g == 3)
                    if c == 0:
                        for g in range(2):
                            claim(4 + g, "conv_t_out", 2 * l + g + 1)
                            pe.wait_ge(sem("a_kept"), FT + FT * l)
                            TR(bank[4 + g][0:110, 0:P], fat[:, 5 * g:5 * g + 5, :].rearrange("p t f -> p (t f)"), ident).then_inc(sem("conv_t"), 1)

            ffn_pe(0, 1, U_UP0, U_DN0, E_UP0, E_DN0)
            for t in range(2):
                unit(U_IN1 + t, (E_IN1 + t) % RING, actA, ready=("norm_lo", 16) if t == 0 else None)
                if t == 0:
                    sum_squares(2)


            def in1_unit(e, i8=0):
                pe.wait_ge(sem("evac1_done"), e - 1 + i8)
                unit(U_IN1 + e, (E_IN1 + e) % RING, actA, i8=i8)


            with pe.Fori(0, 3) as i:
                for j in range(8):
                    in1_unit(2 + j, i * 8)


            def job1(n):
                name, t, half = JOBS1[n]
                claim(4 + n % 4, "jobs_out", len(JOBS) + n + 1)
                for c in range(4):
                    f = {"q": 0, "k": 8, "v": 16}[name] + 4 * half + c
                    if t < 2:
                        ins = TR(bank[4 + n % 4][:, P * c:P * c + P], z1[:, f, P * t:P * t + P], ident)
                    else:
                        ins = TR(bank[4 + n % 4][0:NB, P * c:P * c + P], z1[:, f, TP:T], ident)
                ins.then_inc(sem("jobs_in"), 1)


            id8 = ident[0:8, 0:8]
            for j in range(8):
                in1_unit(26 + j)
                if j:
                    pe.wait_ge(sem("evac1_done"), 28)
                    job1(2 * j - 2)
                    job1(2 * j - 1)
                if j == 3:
                    claim(7, "small_out", 1)
                    pe.wait_ge(sem("m_ready"), 1)
                    TR(bank[7][:, 0:8], R_A[:, 0:P], id8)
                    TR(bank[7][:, 8:16], R_A[:, P:TP], id8).then_inc(sem("small_in"), 1)
                if j == 4:
                    claim(7, "small_out", 2)
                    pe.wait_ge(sem("gate_exp"), 3)
                    for n in range(4):
                        ins = TR(bank[7][0:NB, 8 * n:8 * n + 8], s8[:, 4 + n, :], id8)
                    ins.then_inc(sem("small_in"), 1)
                if j == 5:
                    claim(7, "small_out", 3)
                    pe.wait_ge(sem("dec_diag"), 1)
                    M(bank[7][:, 0:64], ones[0:NB, :], dd[:].rearrange("p b h -> p (b h)"), start=True, stop=True).then_inc(sem("small_in"), 1)
            for r in range(RING):
                last_reader[r] = (sem("evac1_done"), 36)


            def row_bcast(out, row, rhs):
                return M(out, pick3[:, row:row + 1].to_broadcast([64, P]), rhs, start=True, stop=True)


            def head_m(h):
                claim(3, "e_arg", 2 * h + 2)
                row_bcast(bank[3][:, 0:TP], h, m3[:, 0:TP]).then_inc(sem("m_b"), 1)


            def head_s(h):
                claim(2, "w_ready", h + 1)
                q, k = z1[:, h, :], z1[:, 8 + h, :]
                M(bank[2][:, 0:256], k[:, 0:128], q[:, 0:256], start=True, stop=True)
                M(bank[2][:, 256:384], k[:, 128:256], q[:, 128:256], start=True, stop=True).then_inc(sem("m_s"), 1)


            def head_num(h):
                cols = slice(DC * h, DC * h + DC)
                w, v, kw, out = ww[h % 2], tk1["v"], tk1["k"], bank[h % 2]
                claim(h % 2, "head_out", 3 * h + 3)
                pe.wait_ge(sem("k_weighted"), 2 * h + 2)
                for t in range(2):
                    M(out[:, 256:384], v[:, t, cols], kw[:, t, cols], start=t == 0, stop=t == 1)
                for t in range(2):
                    M(out[:, 384:385], kw[:, t, cols], ones[:, 0:1], start=t == 0, stop=t == 1)
                pe.wait_ge(sem("w_ready"), h + 1)
                causal_pv(out[:, :], v[:, 0, cols], v[:, 1, cols], w)
                pick = sel[:, H - 1 - h:2 * H - 1 - h]
                M(bank[7][0:H, 0:256], pick, w[:, 0:256], start=h == 0, stop=False, skip_group_check=True)
                M(bank[7][0:H, 128:256], pick, w[:, 256:384], start=False, stop=h == H - 1, skip_group_check=True).then_inc(sem("num_in"), 1)


            def head_squares(h):
                pe.wait_ge(sem("head_sq"), h + 1)
                return M(bank[7][0:H, 256:512], sel[:, H - 1 - h:2 * H - 1 - h], z1[:, h, 0:TP], start=False, stop=h == H - 1,
                         skip_group_check=True)


            def c_outer(b):
                for half in range(2):
                    out = bank[seq_bank(b, half)]
                    claim(seq_bank(b, half), "c_added", 2 * b + half + 1)
                    pe.wait_ge(sem("v_masked"), b + 1)
                    for n in range(4):
                        cols = slice(512 * half + DC * n, 512 * half + DC * n + DC)
                        ins = M(out[:, DC * n:DC * n + DC], vm[b % 2][:, cols], k3[:, cols], start=True, stop=True)
                    ins.then_inc(sem("outer"), 1)


            def q_bcast(b, half):
                claim(seq_bank(b, 2 + half), "q_mult", 2 * b + half + 1)
                row_bcast(bank[seq_bank(b, 2 + half)][:, :], b, q3[:, 512 * half:512 * half + 512]).then_inc(sem("q_b"), 1)


            pe.wait_ge(sem("jobs_out"), len(JOBS) + len(JOBS1))
            pe.wait_ge(sem("sel_ready"), 2)
            claim(7, "h1_var", 1)
            pe.wait_ge(sem("m_hi"), 3)
            pe.wait_ge(sem("m_lo"), 1)
            head_m(0)
            head_s(0)
            for h in range(H):
                if h + 1 < H:
                    head_m(h + 1)
                head_num(h)
                if h == 0:
                    pe.wait_ge(sem("rows_lo"), 3)
                c_outer(h)
                q_bcast(h, 0)
                if h + 1 < H:
                    head_s(h + 1)
                q_bcast(h, 1)
                if h >= 2:
                    head_squares(h - 2)
            head_squares(H - 2)
            head_squares(H - 1).then_inc(sem("head_ss"), 1)
            claim(2, "den_in", 2)
            pe.wait_ge(sem("den_sample"), 1)
            TR(bank[2][0:H, 0:NB], s8[:, 12, :], id8).then_inc(sem("turned"), 1)
            claim(4, "h1_var", 1)
            pe.wait_ge(sem("head_sq"), H + 1)
            for h in range(H):
                ins = M(bank[4][0:H, 0:NB], sel[:, H - 1 - h:2 * H - 1 - h], z1[:, h, TP:T], start=h == 0, stop=h == H - 1)
            ins.then_inc(sem("head_ss"), 1)
            claim(3, "n_row", 1)
            pe.wait_ge(sem("head_out"), 3 * H)
            TR(bank[3][0:H, 0:DC], ncol[:], ident).then_inc(sem("turned"), 1)
            pe.wait_ge(sem("h1_rstd"), 1)
            for h in range(H):
                claim(h % 4, "mix1", h + 1)
                row_bcast(bank[h % 4][:, 0:T], h, m3[:]).then_inc(sem("rstd_b"), 1)
            out_proj(3, U_OUT1, E_OUT1, ("mix1_lo", 0))
            ffn_pe(1, 3, U_UP1, U_DN1, E_UP1, E_DN1)
            sum_squares(4)
            for t in range(3):
                for half in range(2):
                    claim(2 * t + half, "y_out", 2 * t + half + 1)
                    for c in range(4):
                        k = 4 * half + c
                        pe.wait_ge(sem("y_scaled"), k + 1)
                        if t < 2:
                            ins = TR(bank[2 * t + half][:, P * c:P * c + P], sq[:, k, P * t:P * t + P], ident)
                        else:
                            ins = TR(bank[2 * t + half][0:NB, P * c:P * c + P], sq[:, k, TP:T], ident)
                    ins.then_inc(sem("x_t"), 1)


_INS = ["x_prompt", "x_sample", "cache_k", "cache_v", "page_table", "state_ret", "state_mlstm_C", "state_mlstm_n",
        "state_mlstm_m", "state_ffn_conv", "ab_norm_g", "ab_w_in", "ab_ret_norm_g", "ab_w_out", "c_norm_g", "c_w_in",
        "c_gate_bias", "c_out_norm_g", "c_w_out", "ffn_norm_g", "ffn_w1", "ffn_w3", "ffn_conv_w", "ffn_conv_b",
        "ffn_w2", "final_norm_g"]
_OUTS = [("y_prompt", (1, TP, D)), ("y_sample", (NB, 1, D)), ("k_prompt", (1, 1, TP, H, DA)), ("v_prompt", (1, 1, TP, H, DA)),
         ("k_sample", (1, NB, 1, H, DA)), ("v_sample", (1, NB, 1, H, DA)), ("ret_prompt", (1, 1, H, DA, DA)),
         ("ret_sample", (1, NB, H, DA, DA)), ("C_prompt", (1, 1, H, DC, DC)), ("C_sample", (1, NB, H, DC, DC)),
         ("n_prompt", (1, 1, H, DC)), ("n_sample", (1, NB, H, DC)), ("m_prompt", (1, 1, H)), ("m_sample", (1, NB, H)),
         ("conv_prompt", (2, 1, 2, DFF)), ("conv_sample", (2, NB, 2, DFF))]


def kernel(**inputs):
    from concourse import bacc
    from concourse.bass_utils import run_bass_kernel_spmd

    nc = bacc.Bacc("TRN2", target_bir_lowering=False, num_devices=1)
    arrays, args = {"in_consts": constants()}, {}
    args["consts"] = nc.dram_tensor("in_consts", [P, NCONST], F32, kind="ExternalInput").ap()
    for name in _INS:
        a = np.ascontiguousarray(inputs[name])
        arrays[f"in_{name}"] = a
        args[name] = nc.dram_tensor(f"in_{name}", a.shape, mybir.dt.from_np(a.dtype), kind="ExternalInput").ap()
    for name, shape in _OUTS:
        args[name] = nc.dram_tensor(f"out_{name}", shape, F32, kind="ExternalOutput").ap()
    build(nc, **args)
    r = run_bass_kernel_spmd(nc, [arrays], core_ids=[0])
    return tuple(r.results[0][f"out_{name}"] for name, _ in _OUTS)
```
